# Optimizing a Trainium2 kernel written in Bass

```python
import jax, jax.numpy as jnp
from jax import lax
import numpy as np

D_MODEL = 1024
BATCH = 1
SEQ = 256
DEPTH = 2
DEC_BATCH = 8
DEC_SEQ = 8
PAST_LEN = 256
PAGE_SIZE = 128

N_MIXERS = 2
N_ATTN_LAYERS = (DEPTH + 1) // 2
N_RET_LAYERS = DEPTH // 2
ATTN_HEADS = 16
ATTN_HEAD_DIM = 64
ATTN_WIDTH = ATTN_HEADS * ATTN_HEAD_DIM
IDX_HEADS = 8
IDX_DIM = 64
IDX_TOPK_MAX = 256
Q_BLOCK = 128
ROPE_THETA = 10000.0
ATTN_IN = 3 * ATTN_WIDTH + IDX_HEADS * IDX_DIM + IDX_DIM + IDX_HEADS
RET_HEADS = 4
RET_QK_DIM = D_MODEL // RET_HEADS
RET_V_DIM = 2 * D_MODEL // RET_HEADS
RET_CHUNK = 128
RET_IN = 2 * RET_HEADS * RET_QK_DIM + 2 * RET_HEADS * RET_V_DIM
N_EXPERTS = 16
N_GROUPS = 4
EXPERTS_PER_GROUP = N_EXPERTS // N_GROUPS
TOPK_EXPERTS = 2
EXPERT_DIM = D_MODEL // 2
DEEPNORM_ALPHA = (2 * DEPTH) ** 0.25
DEEPNORM_BETA = (8 * DEPTH) ** -0.25
LN_EPS = 1e-5

kernel_name = "hybrid_dsa_retention_moe_step"

F32 = jnp.float32

def layer_norm(x, g, b):
    xf = x.astype(F32)
    mu = jnp.mean(xf, -1, keepdims=True)
    var = jnp.mean(jnp.square(xf - mu), -1, keepdims=True)
    return ((xf - mu) * lax.rsqrt(var + LN_EPS) * g.astype(F32) + b.astype(F32)).astype(x.dtype)

def rope(x, pos):
    d = x.shape[-1]
    inv = ROPE_THETA ** (-jnp.arange(0, d, 2, dtype=F32) / d)
    ang = pos.astype(F32)[:, None] * inv[None, :]
    cos = jnp.cos(ang)[:, None, :].astype(x.dtype)
    sin = jnp.sin(ang)[:, None, :].astype(x.dtype)
    x1, x2 = x[..., : d // 2], x[..., d // 2:]
    return jnp.concatenate([x1 * cos - x2 * sin, x1 * sin + x2 * cos], -1)

def dsa_project(x, w_in, pos):
    B, T, _ = x.shape
    W = ATTN_WIDTH
    cuts = [W, 2 * W, 3 * W, 3 * W + IDX_HEADS * IDX_DIM, 3 * W + IDX_HEADS * IDX_DIM + IDX_DIM]
    q, k, v, qi, ki, wi = jnp.split(x @ w_in, cuts, axis=-1)
    q = rope(q.reshape(B, T, ATTN_HEADS, ATTN_HEAD_DIM), pos)
    k = rope(k.reshape(B, T, ATTN_HEADS, ATTN_HEAD_DIM), pos)
    v = v.reshape(B, T, ATTN_HEADS, ATTN_HEAD_DIM)
    qi = rope(qi.reshape(B, T, IDX_HEADS, IDX_DIM), pos)
    ki = rope(ki.reshape(B, T, 1, IDX_DIM), pos)[:, :, 0, :]
    wi = wi * IDX_HEADS ** -0.5
    return q, k, v, qi, ki, wi

def index_select(qi, wi, ki, qpos, kpos, topk):
    s = jnp.einsum('qhd,sd->qhs', qi.astype(F32), ki.astype(F32)) * IDX_DIM ** -0.5
    score = jnp.einsum('qhs,qh->qs', jax.nn.relu(s), wi.astype(F32))
    score = jnp.where(kpos[None, :] <= qpos[:, None], score, -jnp.inf)
    vals, idx = lax.top_k(score, topk)
    return idx, jnp.isfinite(vals)

def sparse_attend(q, k_sel, v_sel, valid):
    s = jnp.einsum('qhd,qshd->qhs', q.astype(F32), k_sel.astype(F32)) * ATTN_HEAD_DIM ** -0.5
    p = jax.nn.softmax(jnp.where(valid[:, None, :], s, -jnp.inf), axis=-1)
    return jnp.einsum('qhs,qshd->qhd', p, v_sel.astype(F32)).astype(q.dtype)

def dsa_prompt(x, w_in, w_out, pos, topk):
    B, T, _ = x.shape
    q, k, v, qi, ki, wi = dsa_project(x, w_in, pos)
    nb = T // Q_BLOCK

    def block(args):
        q_b, qi_b, wi_b, qpos_b, b = args
        idx, valid = index_select(qi_b, wi_b, ki[b], qpos_b, pos, topk)
        return sparse_attend(q_b, k[b, idx], v[b, idx], valid)

    xs = (q.reshape(B * nb, Q_BLOCK, ATTN_HEADS, ATTN_HEAD_DIM),
          qi.reshape(B * nb, Q_BLOCK, IDX_HEADS, IDX_DIM),
          wi.reshape(B * nb, Q_BLOCK, IDX_HEADS),
          jnp.tile(pos.reshape(nb, Q_BLOCK), (B, 1)),
          jnp.repeat(jnp.arange(B, dtype=jnp.int32), nb))
    o = lax.map(block, xs).reshape(B, T, ATTN_WIDTH)
    return o @ w_out, k, v, ki

def dsa_sample(x, w_in, w_out, cache_k, cache_v, cache_ik, page_table, pos, topk):
    Bs, Ts, _ = x.shape
    q, k, v, qi, ki, wi = dsa_project(x, w_in, pos)
    past = page_table.shape[1] * PAGE_SIZE
    kpos = jnp.arange(past + Ts, dtype=jnp.int32)

    def seq(args):
        q_b, qi_b, wi_b, k_b, v_b, ki_b, pt = args
        ki_all = jnp.concatenate([cache_ik[pt].reshape(past, IDX_DIM), ki_b], 0)
        idx, valid = index_select(qi_b, wi_b, ki_all, pos, kpos, topk)
        in_past = (idx < past)[:, :, None, None]
        ip = jnp.minimum(idx, past - 1)
        phys, off = pt[ip // PAGE_SIZE], ip % PAGE_SIZE
        inew = jnp.clip(idx - past, 0, Ts - 1)
        k_sel = jnp.where(in_past, cache_k[phys, off], k_b[inew])
        v_sel = jnp.where(in_past, cache_v[phys, off], v_b[inew])
        return sparse_attend(q_b, k_sel, v_sel, valid)

    o = lax.map(seq, (q, qi, wi, k, v, ki, page_table)).reshape(Bs, Ts, ATTN_WIDTH)
    return o @ w_out, k, v, ki

def retention_log_decay():
    return jnp.log(1.0 - 2.0 ** (-5.0 - jnp.arange(RET_HEADS, dtype=F32)))

def retention_project(x, w_in, pos):
    B, T, _ = x.shape
    hq, hv = RET_HEADS * RET_QK_DIM, RET_HEADS * RET_V_DIM
    q, k, v, g = jnp.split(x @ w_in, [hq, 2 * hq, 2 * hq + hv], axis=-1)
    q = rope(q.reshape(B, T, RET_HEADS, RET_QK_DIM), pos)
    k = rope(k.reshape(B, T, RET_HEADS, RET_QK_DIM), pos) * RET_QK_DIM ** -0.5
    v = v.reshape(B, T, RET_HEADS, RET_V_DIM)
    return q, k, v, g

def retention_chunk(state, q, k, v):
    C = q.shape[1]
    lg = retention_log_decay()
    i = jnp.arange(C, dtype=F32)
    diff = i[:, None] - i[None, :]
    dmask = jnp.where(diff[None] >= 0, jnp.exp(jnp.maximum(diff, 0.0)[None] * lg[:, None, None]), 0.0).astype(q.dtype)
    cross_decay = jnp.exp((i + 1.0)[:, None] * lg[None, :]).astype(q.dtype)
    k_decay = jnp.exp((C - 1.0 - i)[:, None] * lg[None, :]).astype(q.dtype)
    chunk_decay = jnp.exp(C * lg).astype(q.dtype)
    inner = jnp.einsum('bihd,bjhd->bhij', q, k) * dmask[None]
    o = jnp.einsum('bhij,bjhv->bihv', inner, v) + \
        jnp.einsum('bihd,bhdv->bihv', q, state) * cross_decay[None, :, :, None]
    new_state = chunk_decay[None, :, None, None] * state + \
        jnp.einsum('bjhd,bjhv->bhdv', k * k_decay[None, :, :, None], v)
    return new_state.astype(state.dtype), o

def retention_output(o, g, gain, w_out):
    B, T = o.shape[:2]
    of = o.astype(F32)
    mu = jnp.mean(of, -1, keepdims=True)
    var = jnp.mean(jnp.square(of - mu), -1, keepdims=True)
    on = ((of - mu) * lax.rsqrt(var + LN_EPS)).reshape(B, T, RET_HEADS * RET_V_DIM).astype(o.dtype) * gain
    return (jax.nn.silu(g) * on) @ w_out

def retention_prompt(x, w_in, gain, w_out, pos):
    B, T, _ = x.shape
    q, k, v, g = retention_project(x, w_in, pos)
    n = T // RET_CHUNK

    def to_chunks(a):
        return a.reshape(B, n, RET_CHUNK, *a.shape[2:]).swapaxes(0, 1)

    state0 = jnp.zeros((B, RET_HEADS, RET_QK_DIM, RET_V_DIM), x.dtype)
    state, o = lax.scan(lambda s, c: retention_chunk(s, *c), state0,
                        (to_chunks(q), to_chunks(k), to_chunks(v)))
    o = o.swapaxes(0, 1).reshape(B, T, RET_HEADS, RET_V_DIM)
    return retention_output(o, g, gain, w_out), state

def retention_sample(x, w_in, gain, w_out, state, pos):
    q, k, v, g = retention_project(x, w_in, pos)
    new_state, o = retention_chunk(state, q, k, v)
    return retention_output(o, g, gain, w_out), new_state

def moe_tokens(xt, w_router, b_router, w_gate, w_up, w_down):
    n = xt.shape[0]
    probs = jax.nn.softmax((xt @ w_router).astype(F32), axis=-1)
    sel = probs + b_router.astype(F32)
    gscore = lax.top_k(sel.reshape(n, N_GROUPS, EXPERTS_PER_GROUP), 2)[0].sum(-1)
    gbest = jnp.argmax(gscore, -1)
    in_group = (jnp.arange(N_EXPERTS) // EXPERTS_PER_GROUP)[None, :] == gbest[:, None]
    _, eidx = lax.top_k(jnp.where(in_group, sel, -jnp.inf), TOPK_EXPERTS)
    gw = jnp.take_along_axis(probs, eidx, -1)
    gw = gw / jnp.sum(gw, -1, keepdims=True)
    gate = jnp.sum(jax.nn.one_hot(eidx, N_EXPERTS, dtype=F32) * gw[..., None], axis=1)
    h = jax.nn.silu(jnp.einsum('nd,edf->nef', xt, w_gate)) * jnp.einsum('nd,edf->nef', xt, w_up)
    return jnp.einsum('nef,efd->nd', h * gate[:, :, None].astype(h.dtype), w_down)

def moe(x, w_router, b_router, w_gate, w_up, w_down):
    return lax.map(lambda xb: moe_tokens(xb, w_router, b_router, w_gate, w_up, w_down), x)

def setup_inputs(seed: int = 0) -> dict:
    key = jax.random.key(seed)
    ks = jax.random.split(key, 24)
    n_pages = PAST_LEN // PAGE_SIZE
    used = DEC_BATCH * n_pages
    pool = used + used // 4

    def nrm(k, shape, scale):
        return jax.random.normal(k, shape, F32) * scale

    return {
        'x_prompt': nrm(ks[0], (BATCH, SEQ, D_MODEL), 1.0),
        'x_sample': nrm(ks[1], (DEC_BATCH, DEC_SEQ, D_MODEL), 1.0),
        'cache_k': nrm(ks[2], (N_ATTN_LAYERS, pool, PAGE_SIZE, ATTN_HEADS, ATTN_HEAD_DIM), 1.0),
        'cache_v': nrm(ks[3], (N_ATTN_LAYERS, pool, PAGE_SIZE, ATTN_HEADS, ATTN_HEAD_DIM), 1.0),
        'cache_idx_k': nrm(ks[4], (N_ATTN_LAYERS, pool, PAGE_SIZE, IDX_DIM), 1.0),
        'state_ret': nrm(ks[5], (N_RET_LAYERS, DEC_BATCH, RET_HEADS, RET_QK_DIM, RET_V_DIM), 0.3),
        'page_table': jax.random.permutation(ks[6], pool)[:used].reshape(DEC_BATCH, n_pages).astype(jnp.int32),
        'w_in_attn': nrm(ks[7], (N_ATTN_LAYERS, D_MODEL, ATTN_IN), D_MODEL ** -0.5),
        'w_out_attn': nrm(ks[8], (N_ATTN_LAYERS, ATTN_WIDTH, D_MODEL), ATTN_WIDTH ** -0.5 * DEEPNORM_BETA),
        'w_in_ret': nrm(ks[9], (N_RET_LAYERS, D_MODEL, RET_IN), D_MODEL ** -0.5),
        'ret_norm_gain': 1.0 + nrm(ks[10], (N_RET_LAYERS, RET_HEADS * RET_V_DIM), 0.02),
        'w_out_ret': nrm(ks[11], (N_RET_LAYERS, RET_HEADS * RET_V_DIM, D_MODEL), (RET_HEADS * RET_V_DIM) ** -0.5 * DEEPNORM_BETA),
        'w_router': nrm(ks[12], (D_MODEL, N_EXPERTS), D_MODEL ** -0.5),
        'b_router': nrm(ks[13], (N_EXPERTS,), 0.01),
        'w_exp_gate': nrm(ks[14], (DEPTH, N_EXPERTS, D_MODEL, EXPERT_DIM), D_MODEL ** -0.5),
        'w_exp_up': nrm(ks[15], (DEPTH, N_EXPERTS, D_MODEL, EXPERT_DIM), D_MODEL ** -0.5),
        'w_exp_down': nrm(ks[16], (DEPTH, N_EXPERTS, EXPERT_DIM, D_MODEL), EXPERT_DIM ** -0.5 * DEEPNORM_BETA),
        'ln_gain': 1.0 + nrm(ks[17], (DEPTH, 2, D_MODEL), 0.02),
        'ln_bias': nrm(ks[18], (DEPTH, 2, D_MODEL), 0.02),
    }

def reference(x_prompt, x_sample, cache_k, cache_v, cache_idx_k, state_ret, page_table,
              w_in_attn, w_out_attn, w_in_ret, ret_norm_gain, w_out_ret,
              w_router, b_router, w_exp_gate, w_exp_up, w_exp_down, ln_gain, ln_bias):
    T = x_prompt.shape[1]
    Ts = x_sample.shape[1]
    past = page_table.shape[1] * PAGE_SIZE
    pos_p = jnp.arange(T, dtype=jnp.int32)
    pos_s = past + jnp.arange(Ts, dtype=jnp.int32)
    topk_p = min(IDX_TOPK_MAX, T // 4)
    topk_s = min(IDX_TOPK_MAX, (past + Ts) // 4)

    xp, xs = x_prompt, x_sample
    kp_l, vp_l, ikp_l, ks_l, vs_l, iks_l, sp_l, ss_l = [], [], [], [], [], [], [], []
    for i in range(DEPTH):
        if i % N_MIXERS == 0:
            a = i // N_MIXERS
            mp, kp, vp, ikp = dsa_prompt(xp, w_in_attn[a], w_out_attn[a], pos_p, topk_p)
            ms, k_s, v_s, ik_s = dsa_sample(xs, w_in_attn[a], w_out_attn[a], cache_k[a], cache_v[a],
                                            cache_idx_k[a], page_table, pos_s, topk_s)
            kp_l.append(kp); vp_l.append(vp); ikp_l.append(ikp)
            ks_l.append(k_s); vs_l.append(v_s); iks_l.append(ik_s)
        else:
            r = i // N_MIXERS
            mp, sp = retention_prompt(xp, w_in_ret[r], ret_norm_gain[r], w_out_ret[r], pos_p)
            ms, ss = retention_sample(xs, w_in_ret[r], ret_norm_gain[r], w_out_ret[r], state_ret[r], pos_s)
            sp_l.append(sp); ss_l.append(ss)
        xp = layer_norm(DEEPNORM_ALPHA * xp + mp, ln_gain[i, 0], ln_bias[i, 0])
        xs = layer_norm(DEEPNORM_ALPHA * xs + ms, ln_gain[i, 0], ln_bias[i, 0])
        xp = layer_norm(DEEPNORM_ALPHA * xp + moe(xp, w_router, b_router, w_exp_gate[i], w_exp_up[i], w_exp_down[i]),
                        ln_gain[i, 1], ln_bias[i, 1])
        xs = layer_norm(DEEPNORM_ALPHA * xs + moe(xs, w_router, b_router, w_exp_gate[i], w_exp_up[i], w_exp_down[i]),
                        ln_gain[i, 1], ln_bias[i, 1])

    return (xp, xs, jnp.stack(kp_l), jnp.stack(vp_l), jnp.stack(ikp_l),
            jnp.stack(ks_l), jnp.stack(vs_l), jnp.stack(iks_l),
            jnp.stack(sp_l), jnp.stack(ss_l))


_drawn_inputs = setup_inputs


def setup_inputs(seed=0):
    import zlib

    import numpy as np

    out = dict(_drawn_inputs(seed))
    spreads = {}
    factors = {'ret_norm_gain': 5.353}
    for name, (base, spread) in spreads.items():
        noise = np.random.default_rng([zlib.crc32(name.encode()), seed]).standard_normal(out[name].shape)
        drawn = base * np.exp(spread * noise) if base else spread * noise
        out[name] = __import__('jax').numpy.asarray(drawn.astype(out[name].dtype))
    for name, factor in factors.items():
        out[name] = (out[name] * factor).astype(out[name].dtype)
    return out
```

```python
from contextlib import ExitStack

import numpy as np
import concourse.bass as bass
from concourse import mybir

ALU = mybir.AluOpType
ACT = mybir.ActivationFunctionType
AX = mybir.AxisListType.X
F32 = mybir.dt.float32
I32 = mybir.dt.int32

D = 1024
KC = D // 128
PROMPT, NSEQ, DSEQ = 256, 8, 8
SAMPLE = NSEQ * DSEQ
TOK = PROMPT + SAMPLE
ROWS = [128, 128, 64]
PAST, PAGE = 256, 128
HEADS, HD = 16, 64
IH, ID = 8, 64
TOPK_P, TOPK_S = PROMPT // 4, (PAST + DSEQ) // 4
KEYS = PAST + SAMPLE
RH, RQ, RV = 4, 256, 512
NE, NGRP, EPG, ED = 16, 4, 4, 512
SLOTS = 64
ALPHA = 4.0 ** 0.25
EPS = 1e-5
BIG = 2.0 ** 120
TAKEN = -(2.0 ** 125)
W_KW = ID + IH
NRING, SLOT = 6, 4096

IN_ORDER = (6, 7, 0, 1, 2, 3, 4, 5)
STREAM = ([("in", u) for u in IN_ORDER] + [("cache", s) for s in range(NSEQ)]
          + [("out", u) for u in range(2)] + [("moe0", n) for n in range(3 * NE)]
          + [("rin", u) for u in range(8)] + [("state", s) for s in range(NSEQ)]
          + [("rin", u) for u in range(8, 12)] + [("rout", u) for u in range(4)]
          + [("moe1", n) for n in range(3 * NE)])
UNIT = {key: n for n, key in enumerate(STREAM)}
assert UNIT["moe0", 0] % NRING == 0 and UNIT["moe1", 0] % NRING == 0


def landed_counts():
    total, out = [0] * NRING, []
    for n, (kind, _) in enumerate(STREAM):
        total[n % NRING] += 64 if kind == "cache" else 16
        out.append(total[n % NRING])
    return out


LANDED = landed_counts()


def last_product(unit):
    kind, u = unit
    if kind in ("moe0", "moe1"):
        p, what = u // 6, u % 6 // 2
        return (("gate", "up", "down")[what], int(kind[3]), p) + ((1,) if what == 2 else ())
    return {"in": ("in", IN_ORDER.index(u) if kind == "in" else 0, 2), "cache": ("pv_s", u), "out": ("proj", 0, 2, u),
            "rin": ("rin", u, 2), "rout": ("proj", 1, 2, u // 2)}[kind]


def psum_uses():
    count, use = [0] * 8, {}

    def take(key, bank):
        use[key] = (bank, count[bank])
        count[bank] += 1

    def turn(name):
        for t in range(3):
            for h in range(2):
                take((name, t, h), 2 * t + h)

    def moe(L):
        take(("router", L), 6)
        take(("counts", L), 7)

        def gather(p):
            take(("gather", L, p, 0), 0)
            take(("gather", L, p, 1), 1)

        gather(0)
        for p in range(NE // 2):
            take(("gate", L, p), 2)
            take(("up", L, p), 3)
            if p < NE // 2 - 1:
                gather(p + 1)
            take(("hturn", L, p), 4)
            if p:
                for j in range(6):
                    take(("scatter", L, p - 1, j), 4 + j % 2)
            take(("gturn", L, p), 5)
            take(("down", L, p, 0), 6)
            take(("down", L, p, 1), 7)
        for j in range(6):
            take(("scatter", L, NE // 2 - 1, j), 4 + j % 2)

    turn("x0")
    for n in range(8):
        for t in range(3):
            take(("in", n, t), (3 * n + t) % 4)
            if 0 < n <= 6:
                take(("inturn", n - 1, t), 4 + (3 * n + t) % 2)
        if n == 2:
            take(("wturn",), 6)
            take(("wspread",), 7)
        if n == 3:
            for qt in range(2):
                for cc in range(2):
                    for par in range(2):
                        take(("index", qt, cc, par), 6 + par)
        if n == 5:
            for s in range(NSEQ):
                take(("ikturn", s), 6)
                take(("sindex", s), 6)
            take(("sscore",), 7)
    for s in range(NSEQ + 1):
        if s < NSEQ:
            for j in range(4):
                take(("kturn", s, j), j)
            take(("sattn", s), 4 + s % 2)
        if s:
            take(("pturn_s", s - 1), 6)
            take(("pv_s", s - 1), 7)
            take(("oturn_s", s - 1), 6)
    for n in range(16):
        qt, cc, par = n // 8, n // 2 % 4, n % 2
        take(("attn", qt, cc, par), n % 4)
        if n >= 2:
            take(("pturn", n - 2), 4 + n % 2)
            take(("pv", n - 2), 6 + n % 2)
    for n in (16, 17):
        take(("pturn", n - 2), 4 + n % 2)
        take(("pv", n - 2), 6 + n % 2)
    for u in range(2):
        for t in range(3):
            take(("proj", 0, t, u), 2 * t + u)
    turn("x1")
    moe(0)
    turn("x2")
    for n in range(8):
        for t in range(3):
            take(("rin", n, t), (3 * n + t) % 4)
            if 0 < n <= 4:
                take(("rturn", n - 1, t), 4 + (3 * n + t) % 2)
    for h in range(RH):
        take(("inner", h), 0)
        take(("rstate", h, 0), 4)
        take(("rstate", h, 1), 5)
        take(("ro", h, 0), 2 if h % 2 == 0 else 6)
        take(("ro", h, 1), 3 if h % 2 == 0 else 7)
    take(("sinner",), 1)
    take(("so", 0), 6)
    take(("so", 1), 7)
    for s in range(NSEQ):
        for j in range(8):
            take(("update", s, j), 2 + j % 4)
    for n in range(4):
        for t in range(3):
            take(("rin", 8 + n, t), (3 * n + t) % 4)
            if n:
                take(("oturn", n - 1, t), 4 + (3 * n + t) % 2)
    for t in range(3):
        take(("oturn", 3, t), 4 + t % 2)
    for u in range(2):
        for t in range(3):
            take(("proj", 1, t, u), 2 * t + u)
    turn("x3")
    moe(1)
    return use


USE = psum_uses()

COMMON = {"ident": 128, "tri": 128, "iota": TOK, "first16": NE, "first4": NGRP, "valid": 3}
ATTN_C = {"rope": 3 * 2 * 32, "causal": 512, "scausal": KEYS, "rep": 128, "ofseq": NSEQ,
          "wsel": NSEQ * 64, "hrep": 64, "hsel": 4}
RET_C = {"rrope": 3 * 2 * 128, "decay": RH * 256, "sdecay": RH * 64, "qdecay": 2 * RH * DSEQ,
         "kdecay": 2 * RH, "ksel": NSEQ * RH}


def constants():
    f = np.float32
    pos = np.concatenate([np.arange(PROMPT), PAST + np.arange(SAMPLE) % DSEQ, np.zeros(64, int)])
    pos = pos.reshape(3, 128)

    def rope(d):
        inv = f(10000.0) ** (-np.arange(0, d, 2, dtype=f) / f(d))
        ang = pos.astype(f)[:, :, None] * inv[None, None, :]
        t = np.stack([np.cos(ang), np.sin(ang)], 2)
        return t.transpose(1, 0, 2, 3).reshape(128, -1)

    i = np.arange(128)
    t64 = np.arange(64)
    c = {"ident": np.eye(128), "tri": (i[:, None] < i[None, :]), "iota": np.tile(np.arange(TOK), (128, 1)),
         "first16": np.tile(NE - np.arange(NE), (128, 1)), "first4": np.tile(NGRP - np.arange(NGRP), (128, 1)),
         "valid": np.stack([i >= 0, i >= 0, i < 64], 1), "rope": rope(HD)}
    q = i[:, None, None] + 128 * np.arange(2)[None, :, None]
    c["causal"] = np.where(np.arange(256)[None, None, :] <= q, BIG, -BIG).reshape(128, 512)
    sc = np.full((128, KEYS), BIG)
    same = (t64[:, None] // DSEQ == t64[None, :] // DSEQ) & (t64[None, :] % DSEQ <= t64[:, None] % DSEQ)
    sc[:64, PAST:] = np.where(same, BIG, -BIG)
    c["scausal"] = sc
    c["rep"] = np.zeros((128, 128))
    c["rep"][:64] = t64[:, None] % DSEQ == i[None, :] % DSEQ
    c["ofseq"] = i[:, None] // DSEQ == np.arange(NSEQ)[None, :]
    w = np.zeros((128, NSEQ, 64))
    w[:64] = (t64[:, None, None] % DSEQ == t64[None, None, :] % DSEQ) & (t64[None, None, :] // DSEQ == np.arange(NSEQ)[None, :, None])
    c["wsel"] = w.reshape(128, -1)
    c["hrep"] = np.zeros((128, 64))
    c["hrep"][:IH] = np.arange(IH)[:, None] == t64[None, :] // DSEQ
    c["hsel"] = (i[:, None] // DSEQ) % 4 == np.arange(4)[None, :]
    lg = np.log(1.0 - 2.0 ** (-5.0 - np.arange(RH)))
    ks = 1.0 / 16.0
    c["rrope"] = rope(RQ)
    diff = (np.arange(256)[None, :] - i[:, None])[:, None, :]
    c["decay"] = np.where(diff >= 0, np.exp(diff * lg[None, :, None]) * ks, 0).reshape(128, -1)
    sd = np.zeros((128, RH, 64))
    d8 = (t64[None, :] - t64[:, None])[:, None, :]
    inseq = (t64[None, :] // DSEQ == t64[:, None] // DSEQ)[:, None, :]
    sd[:64] = np.where((d8 >= 0) & inseq, np.exp(d8 * lg[None, :, None]) * ks, 0)
    c["sdecay"] = sd.reshape(128, -1)
    qd = np.exp((np.arange(DSEQ) + 1)[None, None, :] * lg[:, None, None]).repeat(2, 1)
    c["qdecay"] = np.tile(qd.reshape(1, -1), (128, 1))
    kd = 255 - i[:, None, None] - 128 * np.arange(2)[None, :, None]
    c["kdecay"] = (np.exp(kd * lg[None, None, :]) * ks).reshape(128, -1)
    k8 = np.exp((DSEQ - 1 - i % DSEQ)[:, None, None] * lg[None, None, :]) * ks
    c["ksel"] = np.where((i[:, None] // DSEQ == np.arange(NSEQ)[None, :])[:, :, None], k8, 0).reshape(128, -1)
    pack = lambda names: np.concatenate([np.asarray(c[n], f).reshape(128, names[n]) for n in names], 1)
    return pack(COMMON), pack(ATTN_C), pack(RET_C)


GAMMA8 = [float(np.exp(DSEQ * np.log(1.0 - 2.0 ** (-5.0 - h)))) for h in range(RH)]


def nth(key, p):
    if isinstance(p, int):
        return USE[key(p)]
    (b, n1), (_, n2) = USE[key(1)], USE[key(2)]
    assert all(USE[key(i)] == (b, n1 + (i - 1) * (n2 - n1)) for i in range(1, NE // 2 - 1))
    return b, p * (n2 - n1) + (2 * n1 - n2)


def columns(view, names):
    out, at = {}, 0
    for n, w in names.items():
        out[n] = view[:, at:at + w]
        at += w
    return out


class Chain:

    def __init__(self, eng, sem):
        self.eng, self.sem, self.n = eng, sem, 0

    def __call__(self, ins):
        self.n = self.n + 1
        ins.then_inc(self.sem, 1)
        self.eng.wait_ge(self.sem, self.n)


def build(nc, A, O):
    with ExitStack() as ctx:
        def sb(name, width, dt=F32, rows=128):
            return ctx.enter_context(nc.sbuf_tensor(name, [rows, width], dt))

        def sem(name):
            return ctx.enter_context(nc.semaphore(name))

        ring = sb("ring", NRING * SLOT)
        Xt = sb("Xt", 3 * D)
        XTt = sb("XTt", KC * TOK)
        com = sb("com", sum(COMMON.values()))
        ones = sb("ones", 128)
        stats = sb("stats", 3 * 12 + 3 * 2 + 3 * 4)
        epst = sb("epst", 1)
        pages = sb("pages", NSEQ * 2, I32, 1)
        most = sb("most", 4, I32, 1)
        wrt = sb("wrt", KC * NE)
        ARENA = 22050
        arena = sb("arena", ARENA)
        bank = [ctx.enter_context(nc.psum_tensor(f"bank{b}", [128, 512], F32)) for b in range(8)]

        X = Xt[:, :].rearrange("p (t d) -> p t d", t=3)
        XT = XTt[:, :].rearrange("p (c t) -> p c t", c=KC)
        C = columns(com, COMMON)
        ident = C["ident"]
        bnst = stats[:, 0:36].rearrange("p (t j) -> p t j", t=3)
        mv = stats[:, 36:42].rearrange("p (t j) -> p t j", t=3)
        sv = stats[:, 42:54].rearrange("p (t j) -> p t j", t=3)

        def slot(n):
            return ring[:, (n % NRING) * SLOT:(n % NRING + 1) * SLOT]

        at = [0]

        def part(width, start=None):
            if start is not None:
                at[0] = start
            a = arena[:, at[0]:at[0] + width]
            at[0] += width
            assert at[0] <= ARENA, at[0]
            return a

        lng, lnb = part(D, 0), part(D)
        AC = columns(part(sum(ATTN_C.values())), ATTN_C)
        qT = part(KC * TOK).rearrange("p (c t) -> p c t", c=KC)
        kT = part(KC * TOK).rearrange("p (c t) -> p c t", c=KC)
        qiT = part(4 * TOK).rearrange("p (c t) -> p c t", c=4)
        kiT = part(TOK)
        V = part(3 * D).rearrange("p (t d) -> p t d", t=3)
        wi = part(3 * IH).rearrange("p (t h) -> p t h", t=3)
        bias_p = part(512).rearrange("p (t k) -> p t k", t=2)
        bias_s = part(KEYS)
        small = part(64)
        best = part(8)
        QB = part(KC * 128).rearrange("p (c r) -> p c r", c=KC)
        here = at[0]
        E = part(1024).rearrange("p (b n) -> p b n", b=2)
        ropeA = part(512)
        R = part(1536).rearrange("p (b n) -> p b n", b=3)
        KT = part(KC * KEYS, here).rearrange("p (c t) -> p c t", c=KC)
        at[0] = here + 3072
        here = at[0]
        ikraw = part(512).rearrange("p (b g u d) -> p b g u d", b=2, g=2, u=2)
        kiS = part(KEYS)
        qib = part(512).rearrange("p (b c r) -> p b c r", b=2, c=4)
        relu = arena[:, 0:1024].rearrange("p (b n) -> p b n", b=2)
        reluS = part(KEYS)
        WP = part(512).rearrange("p (s t) -> p s t", s=NSEQ)
        wiT = part(64)
        work = part(512)
        end1 = at[0]
        P = part(1024, here).rearrange("p (b n) -> p b n", b=2)
        PT = part(1024).rearrange("p (b n) -> p b n", b=2)
        osel = part(256)
        O2 = part(64)
        rept = part(256).rearrange("p (b n) -> p b n", b=2)
        oT = XT
        Y = part(3 * D, 2 * D).rearrange("p (t d) -> p t d", t=3)
        OH = part(3 * 128).rearrange("p (t j s) -> p t j s", t=3, j=2)
        G = part(3 * 128).rearrange("p (t j s) -> p t j s", t=3, j=2)
        GT = part(TOK)
        xs = part(KC * 128).rearrange("p (c s) -> p c s", c=KC)
        sil, hid, hT = part(512), part(512), part(512).rearrange("p (m s) -> p m s", m=4)
        ys = part(D)
        gatev = part(3 * NE).rearrange("p (t e) -> p t e", t=3)
        place = part(3 * NE).rearrange("p (t e) -> p t e", t=3)
        chosen = part(3 * NE).rearrange("p (t e) -> p t e", t=3)
        bro = part(NE)
        rt = [part(3 * NE) for _ in range(8)]
        wover = [part(SLOT), part(SLOT)]
        RC = columns(part(sum(RET_C.values()), 0), RET_C)
        at[0] = max(at[0], 2 * D)
        v = part(3 * RH * RV).rearrange("p (t h n) -> p t h n", t=3, h=RH)
        kt = part(3 * D).rearrange("p (t h d) -> p t h d", t=3, h=RH)
        rqT = part(KC * TOK).rearrange("p (c t) -> p c t", c=KC)
        rkT = part(KC * TOK).rearrange("p (c t) -> p c t", c=KC)
        roT = arena[:, at[0] - 2 * KC * TOK:at[0]].rearrange("p (c t) -> p c t", c=2 * KC)
        gain = part(RH * RV // 128)
        inn = part(384)
        rst = part(3 * 20).rearrange("p (t j) -> p t j", t=3)
        innS = part(RH * 64).rearrange("p (h i) -> p h i", h=RH)
        kd = part(D).rearrange("p (h d) -> p h d", h=RH)
        st_out = part(1024).rearrange("p (b n) -> p b n", b=2)
        here = at[0]
        RE = part(1024).rearrange("p (b n) -> p b n", b=2)
        rropeA = part(512)
        RR = part(1024).rearrange("p (b n) -> p b n", b=2)
        QM = part(RH * 2 * NSEQ * 32, here).rearrange("p (x s t) -> p x s t", x=RH * 2, s=NSEQ)

        bank_full = [sem(f"bank_full{b}") for b in range(8)]
        bank_free = [sem(f"bank_free{b}") for b in range(8)]
        landed = [sem(f"landed{i}") for i in range(NRING)]
        state_stored = [sem(f"state_stored{s}") for s in range(NSEQ)]
        dve_step, act_step = sem("dve_step"), sem("act_step")
        x_in, com_in, attn_c_in, ret_c_in = sem("x_in"), sem("com_in"), sem("attn_c_in"), sem("ret_c_in")
        router_in, gain_in, pages_in = sem("router_in"), sem("gain_in"), sem("pages_in")
        ln_in = [sem(f"ln_in{j}") for j in range(4)]
        ik_in = [sem(f"ik_in{b}") for b in range(2)]
        bro_in = sem("bro_in")
        zeroed = sem("zeroed")
        e_used, re_used = sem("e_used"), sem("re_used")
        r_ready, rk_ready = sem("r_ready"), sem("rk_ready")
        tile_stored = [sem(f"tile_stored{t}") for t in range(3)]
        v_stored, y_stored = sem("v_stored"), sem("y_stored")
        relu_used, qib_ready, bias_ready = sem("relu_used"), sem("qib_ready"), sem("bias_ready")
        qb_ready, new_kt = sem("qb_ready"), sem("new_kt")
        max_s, exp_s, p_s, o2_s = sem("max_s"), sem("exp_s"), sem("p_s"), sem("o2_s")
        max_ready, exp_ready, p_ready = sem("max_ready"), sem("exp_ready"), sem("p_ready")
        var_ready, std_ready, nmr_ready, scaled, x_ready = (sem("var_ready"), sem("std_ready"), sem("nmr_ready"),
                                                            sem("scaled"), sem("x_ready"))
        logit_max, logit_exp, chosen_ready, most_ready = (sem("logit_max"), sem("logit_exp"), sem("chosen_ready"),
                                                          sem("most_ready"))
        oh_ready, g_ready = sem("oh_ready"), sem("g_ready")
        over = [{e: sem(f"over_{e}{L}") for e in ("gate", "up", "down", "pe", "act", "dve")} for L in range(2)]
        sto_stored = [sem("sto_stored0"), sem("sto_stored1")]
        rvar, rstd, rnmr, o_ready = sem("rvar"), sem("rstd"), sem("rnmr"), sem("o_ready")
        qm_ready, kd_ready, go_ready = sem("qm_ready"), sem("kd_ready"), sem("go_ready")

        block = ctx.enter_context(nc.Block())
        NPAIR = NE // 2

        def wait_full(eng, *key):
            b, n = USE[key]
            eng.wait_ge(bank_full[b], n + 1)
            return bank[b]

        def wait_emptied(eng, *key):
            b, n = USE[key]
            eng.wait_ge(bank_free[b], n + 1)

        def freed(key):
            return bank_free[USE[key][0]]

        def token_rows(prompt, sample, t):
            return prompt[t * 128:(t + 1) * 128, :] if t < 2 else sample[:, :]

        def expert_weights(L, what, e):
            w = (A["w_exp_gate"], A["w_exp_up"], A["w_exp_down"])[what]
            return w[L, e].rearrange("(k p) n -> p k n", p=128)

        def unit_source(kind, u):
            c512 = slice(u * 512, (u + 1) * 512)
            if kind == "in":
                return A["w_in_attn"][0, :, c512 if u < 7 else slice(3584, 3584 + W_KW)].rearrange("(k p) n -> p k n", p=128)
            if kind == "out":
                return A["w_out_attn"][0, :, c512].rearrange("(k p) n -> p k n", p=128)
            if kind == "rin":
                return A["w_in_ret"][0, :, c512].rearrange("(k p) n -> p k n", p=128)
            if kind == "rout":
                n, k = u // 2, u % 2
                return A["w_out_ret"][0, k * D:(k + 1) * D, n * 512:(n + 1) * 512].rearrange("(k p) n -> p k n", p=128)
            return A["state_ret"][0, u].rearrange("h (c p) n -> p (h c) n", p=128)

        def weights(n, width=512):
            return slot(n)[:, 0:KC * width].rearrange("p (k n) -> p k n", k=KC)

        def expert_slot(j):
            return slot(j).rearrange("p (k n) -> p k n", k=KC if j < 4 else 4)

        def overflow_any(eng, L):
            eng.wait_ge(most_ready, L + 1)
            return eng.value_load(most[0:1, L:L + 1], min_val=0, max_val=TOK) > SLOTS

        OV = {"gate": 16, "up": 16, "down": 16, "pe": 13, "act": 6, "dve": 9}

        OVER_BANK = (0, 1, 0, 1, 2, 3)

        def overflow_loop(eng, body):
            with eng.Fori(1, TOK // SLOTS) as b:
                with eng.Fori(0, NE) as e:
                    body((b - 1) * NE + e, b, e)

        def expert_pair_loads(sp, L, p):
            for j in range(6):
                what = j // 2
                if isinstance(p, int):
                    wait_full(sp, *last_product((f"moe{L}", 6 * (p - 1) + j)))
                    sp.dma_start(expert_slot(j), expert_weights(L, what, 2 * p + j % 2)).then_inc(landed[j], 16)
                else:
                    b, k = nth(lambda q: last_product((f"moe{L}", 6 * q + j)), p)
                    dn = USE[last_product((f"moe{L}", 12 + j))][1] - USE[last_product((f"moe{L}", 6 + j))][1]
                    w = (A["w_exp_gate"], A["w_exp_up"], A["w_exp_down"])[what]
                    src = w[L, bass.ds(p * 2 + j % 2, 1)].rearrange("o (k p) n -> p (o k) n", p=128)
                    sp.wait_ge(bank_full[b], k - dn + 1)
                    sp.dma_start(expert_slot(j), src).then_inc(landed[j], 16)

        def overflow_loads(sp, L):
            S = over[L]

            def body(n, b, e):
                for name, buf in (("gate", 0), ("up", 1), ("down", 0)):
                    src = A["w_exp_" + name][L, bass.ds(e, 1)].rearrange("o (k p) n -> p (o k) n", p=128)
                    sp.wait_ge(S["pe"], n * OV["pe"] + (2 if name == "down" else 0))
                    sp.dma_start(wover[buf].rearrange("p (k n) -> p k n", k=4 if name == "down" else KC), src).then_inc(S[name], 16)

            with sp.If(overflow_any(sp, L)):
                overflow_loop(sp, body)

        @block.sync
        def _(sp):
            def wait_slot_free(n):
                if n >= NRING:
                    kind, s = STREAM[n - NRING]
                    if kind == "state":
                        sp.wait_ge(state_stored[s], 16)
                    else:
                        wait_full(sp, *last_product((kind, s)))

            sp.dma_start(pages[0:1, :], A["page_table"].rearrange("s g -> (s g)").rearrange("(o s) -> o s", o=1)).then_inc(pages_in, 16)
            for n, (kind, u) in enumerate(STREAM):
                if kind in ("moe0", "moe1"):
                    if u == 0:
                        L = int(kind[3])
                        for j in range(6):
                            wait_slot_free(n + j)
                            sp.dma_start(expert_slot(j), expert_weights(L, j // 2, j % 2)).then_inc(landed[j], 16)
                        wait_full(sp, "gate", L, 0)
                        expert_pair_loads(sp, L, 1)
                        with sp.Fori(2, NPAIR) as p:
                            expert_pair_loads(sp, L, p)
                        if L == 0:
                            overflow_loads(sp, L)
                    continue
                wait_slot_free(n)
                if kind == "cache":
                    if u == 0:
                        sp.wait_ge(pages_in, 16)
                    for g in range(2):
                        page = sp.value_load(pages[0:1, 2 * u + g:2 * u + g + 1], min_val=0, max_val=A["cache_k"].shape[1] - 1)
                        for j, cache in enumerate((A["cache_k"], A["cache_v"])):
                            src = cache[0, bass.ds(page, 1)].rearrange("o p h d -> p (o h d)")
                            sp.dma_start(slot(n)[:, (2 * j + g) * D:(2 * j + g + 1) * D], src).then_inc(landed[n % NRING], 16)
                    continue
                sp.dma_start(weights(n, W_KW if (kind, u) == ("in", 7) else 512), unit_source(kind, u)).then_inc(landed[n % NRING], 16)
            overflow_loads(sp, 1)

        @block.gpsimd
        def _(pool):
            def ln_load(j):
                for dst, src in ((lng, A["ln_gain"]), (lnb, A["ln_bias"])):
                    pool.dma_start(dst, src[j // 2, j % 2:j % 2 + 1, :].to_broadcast([128, D])).then_inc(ln_in[j], 16)

            def ik_load(s):
                if s >= 2:
                    wait_full(pool, "ikturn", s - 2)
                for g in range(2):
                    page = pool.value_load(pages[0:1, 2 * s + g:2 * s + g + 1], min_val=0, max_val=A["cache_k"].shape[1] - 1)
                    src = A["cache_idx_k"][0, bass.ds(page, 1)].rearrange("o p d -> p (o d)")
                    for u in range(2):
                        pool.dma_start(ikraw[:, s % 2, g, u, :], src).then_inc(ik_in[s % 2], 16)

            pool.memset(ones[:, :], 1.0).then_inc(zeroed, 1)
            pool.memset(qib, 0.0).then_inc(zeroed, 1)
            pool.memset(QB, 0.0).then_inc(zeroed, 1)
            pool.memset(epst[:, :], EPS).then_inc(zeroed, 1)
            pool.wait_ge(pages_in, 16)
            ik_load(0)
            ik_load(1)
            pool.dma_start(wrt[:, :].rearrange("p (k e) -> p k e", k=KC), A["w_router"].rearrange("(k p) e -> p k e", p=128)).then_inc(router_in, 16)
            for t in range(3):
                pool.wait_ge(r_ready, 3 + t + 1)
                pool.dma_start(token_rows(O["ik_p"], O["ik_s"], t), R[0:ROWS[t], t, 0:ID]).then_inc(tile_stored[t], 16)
            for n in (4, 5):
                for t in range(3):
                    pool.wait_ge(r_ready, 3 * n + t + 1)
                    pool.dma_start(token_rows(O["k_p"], O["k_s"], t)[:, (n - 4) * 512:(n - 3) * 512],
                                   R[0:ROWS[t], t, :]).then_inc(tile_stored[t], 16)
            pool.wait_ge(relu_used, 2 * IH // 2)
            ln_load(0)
            for s in range(2, NSEQ):
                ik_load(s)
            for t in range(3):
                wait_emptied(pool, "in", 7, t)
                pool.dma_start(token_rows(O["v_p"], O["v_s"], t), V[0:ROWS[t], t, :]).then_inc(v_stored, 16)
            pool.wait_ge(x_ready, 3)
            pool.wait_ge(v_stored, 3 * 16)
            pool.dma_start(bro, A["b_router"].rearrange("(o e) -> o e", o=1).to_broadcast([128, NE])).then_inc(bro_in, 16)
            ln_load(1)
            pool.wait_ge(x_ready, 6)
            pool.dma_start(arena[:, 0:sum(RET_C.values())], A["c_ret"]).then_inc(ret_c_in, 16)
            pool.dma_start(gain, A["ret_norm_gain"][0].rearrange("(c p) -> p c", p=128), allow_slow_non_contiguous=True).then_inc(gain_in, 16)
            for n in range(2 * RH):
                wait_emptied(pool, "rstate", n // 2, n % 2)
                pool.dma_start(O["state_p"][n // 2, (n % 2) * 128:(n % 2 + 1) * 128, :], st_out[:, n % 2, :]).then_inc(sto_stored[n % 2], 16)
            for s in range(NSEQ):
                wait_emptied(pool, "update", s, 7)
                pool.dma_start(O["state_s"][s].rearrange("h (c p) n -> p (h c) n", p=128),
                               slot(UNIT["state", s]).rearrange("p (k n) -> p k n", k=KC)).then_inc(state_stored[s], 16)
            pool.wait_ge(kd_ready, NSEQ + 1)
            ln_load(2)
            pool.wait_ge(x_ready, 9)
            pool.dma_start(bro, A["b_router"].rearrange("(o e) -> o e", o=1).to_broadcast([128, NE])).then_inc(bro_in, 16)
            ln_load(3)
            for t in range(3):
                pool.wait_ge(x_ready, 9 + t + 1)
                pool.dma_start(token_rows(O["y_p"], O["y_s"], t), X[0:ROWS[t], t, :]).then_inc(y_stored, 16)
            for t in range(3):
                pool.wait_ge(tile_stored[t], 3 * 16)
            for b in range(2):
                pool.wait_ge(sto_stored[b], RH * 16)
            for s in range(NSEQ):
                pool.wait_ge(state_stored[s], 16)
            pool.wait_ge(y_stored, 3 * 16)

        def LANDED_EXP(L, j, p):
            return p * 16 + LANDED[UNIT[f"moe{L}", j]]

        def before_overflow(key, L):
            keys = list(USE)
            return keys.index(key) <= keys.index(("scatter", L, NPAIR - 1, 5))

        def experts_pe(pe, L, fill, full):
            def nfill(key, p):
                b, n = nth(key, p)
                pe.wait_ge(bank_free[b], n)
                return bank[b]

            def nemptied(key, p):
                b, n = nth(key, p)
                pe.wait_ge(bank_free[b], n + 1)

            for t in range(3):
                for h in range(2):
                    wait_emptied(pe, f"x{2 * L + 1}", t, h)
            if L == 0:
                pe.wait_ge(router_in, 16)
                pe.wait_ge(zeroed, 4)
            ps = fill(("router", L))
            for t in range(3):
                r = ROWS[t]
                for k in range(KC):
                    last = pe.matmul(ps[0:r, t * NE:(t + 1) * NE], XT[:, k, t * 128:t * 128 + r], wrt[:, k * NE:(k + 1) * NE],
                                     start=(k == 0), stop=(k == KC - 1))
            last.then_inc(full(("router", L)), 1)
            pe.wait_ge(chosen_ready, L + 1)
            ps = fill(("counts", L))
            for t in range(3):
                for u in range(t):
                    pe.matmul(ps[:, t * NE:(t + 1) * NE], ones[:, :], chosen[:, u, :], start=(u == 0), stop=False)
                pe.matmul(ps[:, t * NE:(t + 1) * NE], C["tri"], chosen[:, t, :], start=(t == 0), stop=True)
            for u in range(3):
                last = pe.matmul(ps[:, 3 * NE:4 * NE], ones[:, :], chosen[:, u, :], start=(u == 0), stop=(u == 2))
            last.then_inc(full(("counts", L)), 1)

            def gather(p, q):
                key = (lambda i: lambda x: ("gather", L, x + (0 if q is None else 1), i))
                x = p if q is None else q
                pe.wait_ge(oh_ready, p + (NPAIR * L + 1))
                for h in range(2):
                    ps = nfill(key(h), x) if not (q is None and p == 0) else fill(("gather", L, 0, h))
                    for c in range(4):
                        for t in range(3):
                            r = ROWS[t]
                            last = pe.matmul(ps[:, c * 128:(c + 1) * 128], X[0:r, t, (4 * h + c) * 128:(4 * h + c + 1) * 128],
                                             OH[0:r, t].rearrange("p j s -> p (j s)"), start=(t == 0), stop=(t == 2))
                    last.then_inc(full(("gather", L, 0, h)), 1)

            def scatter(q, key_p):
                for j in range(6):
                    b, n = nth(lambda x, j=j: ("scatter", L, key_p(x), j), q)
                    pe.wait_ge(bank_free[b], n)
                    t, h = j // 2, j % 2
                    r = ROWS[t]
                    pe.matmul(bank[b][0:r, :], GT[:, t * 128:t * 128 + r], ys[:, h * 512:(h + 1) * 512],
                              start=True, stop=True).then_inc(bank_full[b], 1)

            def pair(p, first=False, final=False):
                base = UNIT[f"moe{L}", 0] // NRING
                for h in range(2):
                    nemptied(lambda x, h=h: ("gather", L, x, h), p)
                for what in range(2):
                    ps = nfill(lambda x: (("gate", "up")[what], L, x), p)
                    for j in range(2):
                        pe.wait_ge(landed[2 * what + j], LANDED_EXP(L, 2 * what + j, p))
                    for k in range(KC):
                        for j in range(2):
                            last = pe.matmul(ps[64 * j:64 * j + 64, :], xs[:, k, 64 * j:64 * j + 64], expert_slot(2 * what + j)[:, k, :],
                                             start=(k == 0), stop=(k == KC - 1))
                    last.then_inc(full((("gate", "up")[what], L, 0)), 1)
                if not final:
                    gather(p + 1, p)
                nemptied(lambda x: ("up", L, x), p)
                ps = nfill(lambda x: ("hturn", L, x), p)
                for m in range(4):
                    last = pe.transpose(ps[:, m * 128:(m + 1) * 128], hid[:, m * 128:(m + 1) * 128], ident)
                last.then_inc(full(("hturn", L, 0)), 1)
                if not first:
                    nemptied(lambda x: ("down", L, x - 1, 0), p)
                    nemptied(lambda x: ("down", L, x - 1, 1), p)
                    scatter(p, lambda x: x - 1)
                pe.wait_ge(g_ready, p + (NPAIR * L + 1))
                ps = nfill(lambda x: ("gturn", L, x), p)
                for t in range(3):
                    r = ROWS[t]
                    last = pe.transpose(ps[:, t * 128:t * 128 + r], G[0:r, t].rearrange("p j s -> p (j s)"), ident[0:r, 0:r])
                last.then_inc(full(("gturn", L, 0)), 1)
                nemptied(lambda x: ("hturn", L, x), p)
                for j in range(2):
                    pe.wait_ge(landed[4 + j], LANDED_EXP(L, 4 + j, p))
                for h in range(2):
                    ps = nfill(lambda x, h=h: ("down", L, x, h), p)
                    for k in range(4):
                        for j in range(2):
                            last = pe.matmul(ps[64 * j:64 * j + 64, :], hT[:, k, 64 * j:64 * j + 64],
                                             expert_slot(4 + j)[:, k, h * 512:(h + 1) * 512], start=(k == 0), stop=(k == 3))
                    last.then_inc(full(("down", L, 0, h)), 1)

            gather(0, None)
            pair(0, first=True)
            with pe.Fori(1, NPAIR - 1) as p:
                pair(p)
            pair(NPAIR - 1, final=True)
            nemptied(lambda x: ("gturn", L, x), NPAIR - 1)
            for h in range(2):
                nemptied(lambda x, h=h: ("down", L, x, h), NPAIR - 1)
            scatter(NPAIR, lambda x: x - 1)

            def over_body(n, b, e):
                S = over[L]

                def wait_step(eng, k):
                    pe.wait_ge(S[eng], n * OV[eng] + k)

                wait_step("dve", 2)
                for c in range(KC):
                    for t in range(3):
                        r = ROWS[t]
                        last = pe.matmul(bank[0][:, c * 64:(c + 1) * 64], X[0:r, t, c * 128:(c + 1) * 128], OH[0:r, t, 0, :],
                                         start=(t == 0), stop=(t == 2))
                last.then_inc(S["pe"], 1)
                wait_step("act", 1)
                for what in range(2):
                    wait_step(("gate", "up")[what], 16)
                    for k in range(KC):
                        last = pe.matmul(bank[2 + what][0:64, :], xs[:, k, 0:64], wover[what].rearrange("p (k n) -> p k n", k=KC)[:, k, :],
                                         start=(k == 0), stop=(k == KC - 1))
                    last.then_inc(S["pe"], 1)
                wait_step("dve", 3)
                for m in range(4):
                    last = pe.transpose(bank[4][:, m * 128:(m + 1) * 128], hid[:, m * 128:(m + 1) * 128], ident)
                last.then_inc(S["pe"], 1)
                for t in range(3):
                    r = ROWS[t]
                    last = pe.transpose(bank[5][0:64, t * 128:t * 128 + r], G[0:r, t, 0, :], ident[0:r, 0:r])
                last.then_inc(S["pe"], 1)
                wait_step("act", 3)
                wait_step("down", 16)
                for h in range(2):
                    for k in range(4):
                        last = pe.matmul(bank[6 + h][0:64, :], hT[:, k, 0:64], wover[0].rearrange("p (k n) -> p k n", k=4)[:, k, h * 512:(h + 1) * 512],
                                         start=(k == 0), stop=(k == 3))
                    last.then_inc(S["pe"], 1)
                wait_step("act", 6)
                for j in range(6):
                    t, h = j // 2, j % 2
                    r = ROWS[t]
                    if j in (2, 3):
                        wait_step("dve", 3 + j - 1)
                    pe.matmul(bank[OVER_BANK[j]][0:r, :], GT[0:64, t * 128:t * 128 + r], ys[0:64, h * 512:(h + 1) * 512],
                              start=True, stop=True).then_inc(S["pe"], 1)

            any_over = overflow_any(pe, L)
            with pe.If(any_over):
                for b in range(8):
                    last_use = max(n for key, (bb, n) in USE.items() if bb == b and before_overflow(key, L))
                    pe.wait_ge(bank_free[b], last_use + 1)
                overflow_loop(pe, over_body)
                pe.wait_ge(over[L]["dve"], (TOK // SLOTS - 1) * NE * OV["dve"])

        @block.tensor
        def _(pe):
            def fill(key):
                b, n = USE[key]
                if n:
                    pe.wait_ge(bank_free[b], n)
                return bank[b]

            def full(key):
                return bank_full[USE[key][0]]

            def turn(name, count):
                for t in range(3):
                    if count is not None:
                        pe.wait_ge(x_ready, count + t + 1)
                    r = ROWS[t]
                    for h in range(2):
                        ps = fill((name, t, h))
                        for c in range(4):
                            last = pe.transpose(ps[:, c * 128:c * 128 + r], X[0:r, t, (4 * h + c) * 128:(4 * h + c + 1) * 128],
                                                ident[0:r, 0:r])
                        last.then_inc(full((name, t, h)), 1)

            def project(ps, t, lhs, w, width=512, start=True, stop=True):
                r = ROWS[t]
                for k in range(KC):
                    at = dict(start=(start and k == 0), stop=(stop and k == KC - 1))
                    x = lhs[:, k, t * 128:t * 128 + r]
                    if t < 2 or width < 512:
                        last = pe.matmul(ps[0:r, 0:width], x, w[:, k, 0:width], **at)
                    else:
                        for j in range(2):
                            last = pe.matmul(ps[64 * j:64 * j + 64, 0:256], x, w[:, k, 256 * j:256 * j + 256], **at)
                return last

            pe.wait_ge(com_in, 16)
            pe.wait_ge(x_in, 48)
            turn("x0", None)
            for n in range(8):
                width = W_KW if n == 1 else 512
                pe.wait_ge(landed[n % NRING], LANDED[n])
                for t in range(3):
                    if n == 0:
                        wait_emptied(pe, "x0", t, 1)
                        wait_emptied(pe, "x0", t, 0)
                    project(fill(("in", n, t)), t, XT, weights(n, width), width).then_inc(full(("in", n, t)), 1)
                    if 0 < n <= 6:
                        pe.wait_ge(r_ready, 3 * (n - 1) + t + 1)
                        ps = fill(("inturn", n - 1, t))
                        r = ROWS[t]
                        for c in range(1 if n - 1 == 1 else 4):
                            last = pe.transpose(ps[:, c * 128:c * 128 + r], R[0:r, t, c * 128:(c + 1) * 128], ident[0:r, 0:r])
                        last.then_inc(full(("inturn", n - 1, t)), 1)
                if n == 2:
                    ps = fill(("wturn",))
                    pe.transpose(ps[0:IH, 0:64], wi[0:64, 2, :], ident[0:64, 0:64]).then_inc(full(("wturn",)), 1)
                    wait_emptied(pe, "wturn")
                    pe.wait_ge(attn_c_in, 16)
                    ps = fill(("wspread",))
                    pe.matmul(ps[0:64, 0:64], AC["hrep"][0:IH, :], wiT[0:IH, :], start=True, stop=True).then_inc(full(("wspread",)), 1)
                if n == 3:
                    for t in range(2):
                        wait_emptied(pe, "inturn", 0, t)
                        wait_emptied(pe, "inturn", 1, t)
                    for qt in range(2):
                        nk = 128 * (qt + 1)
                        for cc in range(2):
                            for par in range(2):
                                key = ("index", qt, cc, par)
                                ps = fill(key)
                                o = 64 * par
                                for j in range(2):
                                    last = pe.matmul(ps[:, j * nk:(j + 1) * nk], qiT[o:o + 64, 2 * cc + j, qt * 128:(qt + 1) * 128],
                                                     kiT[o:o + 64, 0:nk], start=True, stop=True)
                                last.then_inc(full(key), 1)
                if n == 5:
                    score = fill(("sscore",))
                    wait_emptied(pe, "wspread")
                    for s in range(NSEQ):
                        ps = fill(("ikturn", s))
                        pe.wait_ge(ik_in[s % 2], 64 * (s // 2 + 1))
                        for g in range(2):
                            last = pe.transpose(ps[:, g * 128:(g + 1) * 128], ikraw[:, s % 2, g].rearrange("p u d -> p (u d)"), ident)
                        last.then_inc(full(("ikturn", s)), 1)
                        ps = fill(("sindex", s))
                        pe.wait_ge(qib_ready, s + 1)
                        for c in range(4):
                            last = pe.matmul(ps[0:64, 0:KEYS], qib[:, s % 2, c, :], kiS, start=(c == 0), stop=(c == 3))
                        last.then_inc(full(("sindex", s)), 1)
                        wait_emptied(pe, "sindex", s)
                        last = pe.matmul(score[0:64, 0:KEYS], WP[0:64, s, :], reluS[0:64, :], start=(s == 0), stop=(s == NSEQ - 1))
                    last.then_inc(full(("sscore",)), 1)

            for s in range(NSEQ + 1):
                if s < NSEQ:
                    n = UNIT["cache", s]
                    pe.wait_ge(landed[n % NRING], LANDED[n])
                    raw = slot(n)
                    for j in range(4):
                        ps = fill(("kturn", s, j))
                        for i in range(4):
                            c, g = 2 * j + i // 2, i % 2
                            last = pe.transpose(ps[:, i * 128:(i + 1) * 128], raw[:, g * D + c * 128:g * D + (c + 1) * 128], ident)
                        last.then_inc(full(("kturn", s, j)), 1)
                    ps = fill(("sattn", s))
                    if s == 0:
                        pe.wait_ge(new_kt, 1)
                    for j in range(4):
                        wait_emptied(pe, "kturn", s, j)
                    pe.wait_ge(qb_ready, s + 1)
                    for c in range(KC):
                        pe.matmul(ps[:, 0:KEYS], QB[:, c, :], KT[:, c, :], start=(c == 0), stop=False)
                    pe.matmul(ps[:, 0:KEYS], rept[0:64, s % 2, :], bias_s[0:64, :], start=False, stop=True).then_inc(full(("sattn", s)), 1)
                if s:
                    b = s - 1
                    raw = slot(UNIT["cache", b])
                    pe.wait_ge(p_s, b + 1)
                    ps = fill(("pturn_s", b))
                    for g in range(2):
                        pe.transpose(ps[:, g * 128:(g + 1) * 128], P[:, b % 2, g * 128:(g + 1) * 128], ident)
                    pe.transpose(ps[0:64, 256:384], P[:, b % 2, 256:KEYS], ident).then_inc(full(("pturn_s", b)), 1)
                    ps = fill(("pv_s", b))
                    wait_emptied(pe, "pturn_s", b)
                    if b == 0:
                        for i in (6, 7):
                            wait_emptied(pe, "in", i, 2)
                    for g in range(3):
                        for q in range(4):
                            r = 128 if g < 2 else 64
                            val = raw[:, (2 + g) * D + q * 256:(2 + g) * D + (q + 1) * 256] if g < 2 else V[0:64, 2, q * 256:(q + 1) * 256]
                            last = pe.matmul(ps[32 * q:32 * q + 32, 0:256], PT[0:r, b % 2, g * 128 + 32 * q:g * 128 + 32 * q + 32], val,
                                             start=(g == 0), stop=(g == 2))
                    last.then_inc(full(("pv_s", b)), 1)
                    pe.wait_ge(o2_s, b + 1)
                    ps = fill(("oturn_s", b))
                    pe.transpose(ps[0:64, 0:128], O2, ident).then_inc(full(("oturn_s", b)), 1)

            def attend(n):
                qt, cc, par = n // 8, n // 2 % 4, n % 2
                pe.wait_ge(p_ready, n + 1)
                ps = fill(("pturn", n))
                for i in range(2 * (qt + 1)):
                    last = pe.transpose(ps[:, i * 128:(i + 1) * 128], P[:, n % 2, i * 128:(i + 1) * 128], ident)
                last.then_inc(full(("pturn", n)), 1)
                ps = fill(("pv", n))
                wait_emptied(pe, "pturn", n)
                for j in range(2):
                    head = 2 * (2 * cc + j) + par
                    for g in range(qt + 1):
                        i = j * (qt + 1) + g
                        last = pe.matmul(ps[64 * par:64 * par + 64, j * 128:(j + 1) * 128], V[:, g, head * 64:(head + 1) * 64],
                                         PT[:, n % 2, i * 128:(i + 1) * 128], start=(g == 0), stop=(g == qt))
                last.then_inc(full(("pv", n)), 1)

            for t in range(2):
                for i in (2, 3, 4, 5):
                    wait_emptied(pe, "inturn", i, t)
                for i in (6, 7):
                    wait_emptied(pe, "in", i, t)
            for n in range(16):
                qt, cc, par = n // 8, n // 2 % 4, n % 2
                nk, o = 128 * (qt + 1), 64 * (n % 2)
                ps = fill(("attn", qt, cc, par))
                for j in range(2):
                    last = pe.matmul(ps[:, j * nk:(j + 1) * nk], qT[o:o + 64, 2 * cc + j, qt * 128:(qt + 1) * 128],
                                     kT[o:o + 64, 2 * cc + j, 0:nk], start=True, stop=True)
                last.then_inc(full(("attn", qt, cc, par)), 1)
                if n >= 2:
                    attend(n - 2)
            attend(14)
            attend(15)

            wait_emptied(pe, "oturn_s", NSEQ - 1)
            wait_emptied(pe, "pv", 14)
            wait_emptied(pe, "pv", 15)
            for u in range(2):
                n = UNIT["out", u]
                pe.wait_ge(landed[n % NRING], LANDED[n])
                for t in range(3):
                    project(fill(("proj", 0, t, u)), t, oT, weights(n)).then_inc(full(("proj", 0, t, u)), 1)
            turn("x1", 0)
            experts_pe(pe, 0, fill, full)
            turn("x2", 3)

            for n in range(8):
                m = UNIT["rin", n]
                pe.wait_ge(landed[m % NRING], LANDED[m])
                for t in range(3):
                    if n == 0:
                        wait_emptied(pe, "x2", t, 0)
                        wait_emptied(pe, "x2", t, 1)
                    project(fill(("rin", n, t)), t, XT, weights(m)).then_inc(full(("rin", n, t)), 1)
                    if 0 < n <= 4:
                        i = n - 1
                        src = RR[:, (3 * i + t) % 2, :] if i < 2 else kt[:, t, 2 * (i - 2):2 * (i - 2) + 2].rearrange("p h d -> p (h d)")
                        pe.wait_ge(rk_ready, 3 * i + t + 1)
                        ps = fill(("rturn", i, t))
                        r = ROWS[t]
                        for c in range(4):
                            last = pe.transpose(ps[:, c * 128:c * 128 + r], src[0:r, c * 128:(c + 1) * 128], ident[0:r, 0:r])
                        last.then_inc(full(("rturn", i, t)), 1)

            for t in range(3):
                for n in range(4):
                    wait_emptied(pe, "rturn", n, t)
                for n in range(4, 8):
                    wait_emptied(pe, "rin", n, t)
            for h in range(RH):
                ps = fill(("inner", h))
                for c in range(2):
                    pe.matmul(ps[:, 0:256], rkT[:, 2 * h + c, 0:128], rqT[:, 2 * h + c, 0:256], start=(c == 0), stop=(c == 1))
                for c in range(2):
                    last = pe.matmul(ps[:, 256:384], rkT[:, 2 * h + c, 128:256], rqT[:, 2 * h + c, 128:256], start=(c == 0), stop=(c == 1))
                last.then_inc(full(("inner", h)), 1)
                if h == 0:
                    pe.wait_ge(kd_ready, 1)
                for c in range(2):
                    ps = fill(("rstate", h, c))
                    for t in range(2):
                        last = pe.matmul(ps[:, :], kt[:, t, h, c * 128:(c + 1) * 128], v[:, t, h, :], start=(t == 0), stop=(t == 1))
                    last.then_inc(full(("rstate", h, c)), 1)
                wait_emptied(pe, "inner", h)
                ps = fill(("ro", h, 0))
                pe.matmul(ps[:, :], inn[:, 0:128], v[:, 0, h, :], start=True, stop=True).then_inc(full(("ro", h, 0)), 1)
                ps = fill(("ro", h, 1))
                pe.matmul(ps[:, :], inn[:, 128:256], v[:, 0, h, :], start=True, stop=False)
                pe.matmul(ps[:, :], inn[:, 256:384], v[:, 1, h, :], start=False, stop=True).then_inc(full(("ro", h, 1)), 1)
            ps = fill(("sinner",))
            for h in range(RH):
                for c in range(2):
                    last = pe.matmul(ps[0:64, h * 64:(h + 1) * 64], rkT[:, 2 * h + c, PROMPT:TOK], rqT[:, 2 * h + c, PROMPT:TOK],
                                     start=(c == 0), stop=(c == 1))
            last.then_inc(full(("sinner",)), 1)
            wait_emptied(pe, "sinner")
            pe.wait_ge(qm_ready, 1)
            so = [fill(("so", g)) for g in range(2)]
            for s in range(NSEQ):
                g = s // 4
                if s % 4 == 0:
                    for h in range(RH):
                        pe.matmul(so[g][32 * h:32 * h + 32, :], innS[0:64, h, 32 * g:32 * g + 32], v[0:64, 2, h, :], start=True, stop=False)
                n = UNIT["state", s]
                pe.wait_ge(landed[n % NRING], LANDED[n])
                st = weights(n)
                for c in range(2):
                    for h in range(RH):
                        last = pe.matmul(so[g][32 * h:32 * h + 32, :], QM[:, 2 * h + c, s, :], st[:, 2 * h + c, :],
                                         start=False, stop=(s % 4 == 3 and c == 1))
                if s % 4 == 3:
                    last.then_inc(full(("so", g)), 1)
                pe.wait_ge(kd_ready, s + 2)
                for j in range(8):
                    h, c = j // 2, j % 2
                    ps = fill(("update", s, j))
                    pe.matmul(ps[:, :], kd[0:64, h, c * 128:(c + 1) * 128], v[0:64, 2, h, :],
                              start=True, stop=True).then_inc(full(("update", s, j)), 1)

            def turn_o(n, t):
                pe.wait_ge(go_ready, 3 * n + t + 1)
                ps = fill(("oturn", n, t))
                r = ROWS[t]
                for c in range(4):
                    last = pe.transpose(ps[:, c * 128:c * 128 + r], v[0:r, t, n, c * 128:(c + 1) * 128], ident[0:r, 0:r])
                last.then_inc(full(("oturn", n, t)), 1)

            for n in range(4):
                m = UNIT["rin", 8 + n]
                pe.wait_ge(landed[m % NRING], LANDED[m])
                for t in range(3):
                    project(fill(("rin", 8 + n, t)), t, XT, weights(m)).then_inc(full(("rin", 8 + n, t)), 1)
                    if n:
                        turn_o(n - 1, t)
            for t in range(3):
                turn_o(3, t)
            for t in range(3):
                for n in range(4):
                    wait_emptied(pe, "oturn", n, t)
            for u in range(2):
                banks = [fill(("proj", 1, t, u)) for t in range(3)]
                for kh in range(2):
                    n = UNIT["rout", 2 * u + kh]
                    pe.wait_ge(landed[n % NRING], LANDED[n])
                    for t in range(3):
                        last = project(banks[t], t, roT[:, KC * kh:KC * kh + KC, :], weights(n), start=(kh == 0), stop=(kh == 1))
                        if kh:
                            last.then_inc(full(("proj", 1, t, u)), 1)
            turn("x3", 6)
            experts_pe(pe, 1, fill, full)

        def norm_act(act, j):
            for t in range(3):
                act.wait_ge(var_ready, 3 * j + t + 1)
                r = ROWS[t]
                act.activation(sv[0:r, t, 0:1], mv[0:r, t, 1:2], ACT.Sqrt, bias=epst[0:r, 0:1]).then_inc(std_ready, 1)
            for t in range(3):
                act.wait_ge(nmr_ready, 3 * j + t + 1)
                r = ROWS[t]
                act.activation(X[0:r, t, :], X[0:r, t, :], ACT.Identity, bias=sv[0:r, t, 2:3], scale=sv[0:r, t, 1:2]).then_inc(scaled, 1)

        def experts_act(act, L):
            def nth_full(key, p):
                b, n = nth(key, p)
                act.wait_ge(bank_full[b], n + 1)
                return bank[b], bank_free[b]

            act.wait_ge(logit_max, L + 1)
            act.activation(rt[0], rt[0], ACT.Exp).then_inc(logit_exp, 1)

            def columns_in(key, p):
                ps, free = nth_full(key, p)
                act.activation(xs[:, 4:8, :], ps[:, :].rearrange("p (c s) -> p c s", c=4), ACT.Copy).then_inc(free, 1)

            def pair(p, final=False):
                ps, free = nth_full(lambda x: ("gate", L, x), p)
                if not (isinstance(p, int) and p == 0):
                    b, n = nth(lambda x: ("up", L, x), p)
                    act.wait_ge(bank_free[b], n)
                act.activation(sil, ps[:, :], ACT.Silu).then_inc(free, 1)
                if not final:
                    columns_in(lambda x: ("gather", L, x + 1, 1), p)
                ps, free = nth_full(lambda x: ("hturn", L, x), p)
                act.activation(hT, ps[:, :].rearrange("p (m s) -> p m s", m=4), ACT.Copy).then_inc(free, 1)
                ps, free = nth_full(lambda x: ("gturn", L, x), p)
                act.activation(GT[:, :], ps[:, 0:TOK], ACT.Copy).then_inc(free, 1)
                ps, free = nth_full(lambda x: ("down", L, x, 1), p)
                act.activation(ys[:, 512:1024], ps[:, :], ACT.Copy).then_inc(free, 1)

            columns_in(lambda x: ("gather", L, x, 1), 0)
            pair(0)
            with act.Fori(1, NPAIR - 1) as p:
                pair(p)
            pair(NPAIR - 1, final=True)

            S = over[L]

            def over_body(n, b, e):
                moves = [(1, lambda: act.activation(xs[:, :, 0:64], bank[0][:, :].rearrange("p (c s) -> p c s", c=KC), ACT.Copy)),
                         (2, lambda: act.activation(sil[0:64, :], bank[2][0:64, :], ACT.Silu)),
                         (4, lambda: act.activation(hT[:, :, 0:64], bank[4][:, :].rearrange("p (m s) -> p m s", m=4)[:, :, 0:64], ACT.Copy)),
                         (5, lambda: act.activation(GT[0:64, :], bank[5][0:64, 0:TOK], ACT.Copy)),
                         (6, lambda: act.activation(ys[0:64, 0:512], bank[6][0:64, :], ACT.Copy)),
                         (7, lambda: act.activation(ys[0:64, 512:1024], bank[7][0:64, :], ACT.Copy))]
                for k, move in moves:
                    act.wait_ge(S["pe"], n * OV["pe"] + k)
                    move().then_inc(S["act"], 1)

            with act.If(overflow_any(act, L)):
                overflow_loop(act, over_body)

        @block.scalar
        def _(act):
            step = Chain(act, act_step)

            def copy(out, in_):
                return act.activation(out, in_, ACT.Copy)

            def turned(name):
                for t in range(3):
                    for h in range(2):
                        ps = wait_full(act, name, t, h)
                        r = ROWS[t]
                        copy(XT[:, 4 * h:4 * h + 4, t * 128:t * 128 + r], ps[:, :].rearrange("p (c t) -> p c t", c=4)[:, :, 0:r])\
                            .then_inc(freed((name, t, h)), 1)

            def staged(key, t, out, func=ACT.Copy, width=512):
                ps = wait_full(act, *key)
                if t < 2 or width < 512:
                    act.activation(out[0:ROWS[t], 0:width], ps[0:ROWS[t], 0:width], func).then_inc(freed(key), 1)
                else:
                    act.activation(out[0:64, 0:256], ps[0:64, 0:256], func)
                    act.activation(out[0:64, 256:512], ps[64:128, 0:256], func).then_inc(freed(key), 1)

            act.dma_start(com[:, :], A["c_common"]).then_inc(com_in, 16)
            for t in range(3):
                act.dma_start(X[0:ROWS[t], t, :], token_rows(A["x_p"], A["x_s"], t)).then_inc(x_in, 16)
            act.dma_start(arena[:, 2 * D:2 * D + sum(ATTN_C.values())], A["c_attn"]).then_inc(attn_c_in, 16)
            turned("x0")
            for n in range(8):
                for t in range(3):
                    k = 3 * n + t
                    if n < 6:
                        if k >= 2:
                            act.wait_ge(e_used, k - 1)
                        staged(("in", n, t), t, E[:, k % 2, :], width=W_KW if n == 1 else 512)
                    else:
                        staged(("in", n, t), t, V[:, t, (n - 6) * 512:(n - 5) * 512])
                    if 0 < n <= 6:
                        i, r = n - 1, ROWS[t]
                        ps = wait_full(act, "inturn", i, t)
                        view = ps[:, :].rearrange("p (c t) -> p c t", c=4)[:, :, 0:r]
                        dst = {0: qiT[:, 0:4], 2: qT[:, 0:4], 3: qT[:, 4:8], 4: kT[:, 0:4], 5: kT[:, 4:8]}.get(i)
                        if i == 1:
                            copy(kiT[:, t * 128:t * 128 + r], ps[:, 0:r]).then_inc(freed(("inturn", i, t)), 1)
                        else:
                            copy(dst[:, :, t * 128:t * 128 + r], view).then_inc(freed(("inturn", i, t)), 1)
                if n == 2:
                    ps = wait_full(act, "wturn")
                    copy(wiT[0:IH, :], ps[0:IH, 0:64]).then_inc(freed(("wturn",)), 1)
                if n == 3:
                    m = 0
                    for qt in range(2):
                        nk = 128 * (qt + 1)
                        for cc in range(2):
                            for par in range(2):
                                ps = wait_full(act, "index", qt, cc, par)
                                if m >= 2:
                                    act.wait_ge(relu_used, m - 1)
                                act.activation(relu[:, m % 2, 0:2 * nk], ps[:, 0:2 * nk], ACT.Relu, scale=ID ** -0.5)\
                                   .then_inc(freed(("index", qt, cc, par)), 1)
                                m += 1
                if n == 5:
                    wait_emptied(act, "inturn", 1, 2)
                    step(copy(kiS[:, PAST:KEYS], kiT[:, PROMPT:TOK]))
                    for s in range(NSEQ):
                        ps = wait_full(act, "ikturn", s)
                        copy(kiS[:, 0:PAST], ps[:, 0:PAST]).then_inc(freed(("ikturn", s)), 1)
                        ps = wait_full(act, "sindex", s)
                        if s:
                            pass
                        act.activation(reluS[0:64, :], ps[0:64, 0:KEYS], ACT.Relu, scale=ID ** -0.5).then_inc(freed(("sindex", s)), 1)

            for s in range(NSEQ + 1):
                if s < NSEQ:
                    if s == 0:
                        for t in range(3):
                            act.wait_ge(tile_stored[t], 3 * 16)
                    for j in range(2):
                        ps = wait_full(act, "kturn", s, j)
                        copy(KT[:, 2 * j:2 * j + 2, 0:PAST], ps[:, :].rearrange("p (c k) -> p c k", c=2)).then_inc(freed(("kturn", s, j)), 1)
                    ps = wait_full(act, "sattn", s)
                    act.wait_ge(max_s, s + 1)
                    c = 4 * (s % 2)
                    step(act.activation(P[:, s % 2, 0:KEYS], ps[:, 0:KEYS], ACT.Exp, bias=small[:, c + 1:c + 2], scale=HD ** -0.5,
                                        accum_out=small[:, c + 2:c + 3]))
                    copy(small[:, c:c + 1], small[:, c + 2:c + 3]).then_inc(freed(("sattn", s)), 1)
                if s:
                    b = s - 1
                    ps = wait_full(act, "pturn_s", b)
                    copy(PT[:, b % 2, 0:256], ps[:, 0:256])
                    copy(PT[0:64, b % 2, 256:384], ps[0:64, 256:384]).then_inc(freed(("pturn_s", b)), 1)
            for n in range(16 + 2):
                if n < 16:
                    qt = n // 8
                    nk = 128 * (qt + 1)
                    act.wait_ge(max_ready, n + 1)
                    c = 16 + 8 * (n % 2)
                    for j in range(2):
                        last = act.activation(P[:, n % 2, j * nk:(j + 1) * nk], P[:, n % 2, j * nk:(j + 1) * nk], ACT.Exp,
                                              bias=small[:, c + 2 + j:c + 3 + j], scale=HD ** -0.5, accum_out=small[:, c + 4 + j:c + 5 + j])
                    last.then_inc(exp_ready, 1)
                if n >= 2:
                    m = n - 2
                    qt, cc, par = m // 8, m // 2 % 4, m % 2
                    w, o = 256 * (qt + 1), 64 * (m % 2)
                    ps = wait_full(act, "pturn", m)
                    copy(PT[:, m % 2, 0:w], ps[:, 0:w]).then_inc(freed(("pturn", m)), 1)
                    ps = wait_full(act, "pv", m)
                    copy(oT[o:o + 64, 2 * cc:2 * cc + 2, qt * 128:(qt + 1) * 128],
                         ps[o:o + 64, 0:256].rearrange("p (c t) -> p c t", c=2)).then_inc(freed(("pv", m)), 1)
            norm_act(act, 0)
            turned("x1")
            experts_act(act, 0)
            norm_act(act, 1)
            turned("x2")
            for n in range(8):
                for t in range(3):
                    k = 3 * n + t
                    if n < 4:
                        if k >= 2:
                            act.wait_ge(re_used, k - 1)
                        staged(("rin", n, t), t, RE[:, k % 2, :])
                    else:
                        staged(("rin", n, t), t, v[:, t, n - 4, :])
                    if 0 < n <= 4:
                        i, r = n - 1, ROWS[t]
                        ps = wait_full(act, "rturn", i, t)
                        dst = (rqT if i < 2 else rkT)[:, 4 * (i % 2):4 * (i % 2) + 4, t * 128:t * 128 + r]
                        copy(dst, ps[:, :].rearrange("p (c t) -> p c t", c=4)[:, :, 0:r]).then_inc(freed(("rturn", i, t)), 1)
            for h in range(RH):
                for c in range(2):
                    ps = wait_full(act, "rstate", h, c)
                    if h:
                        act.wait_ge(sto_stored[c], 16 * h)
                    copy(st_out[:, c, :], ps[:, :]).then_inc(freed(("rstate", h, c)), 1)
                act.wait_ge(rvar, h + 1)
                act.activation(rst[:, 0:2, 14:15], rst[:, 0:2, 13:14], ACT.Sqrt, bias=epst[:, 0:1]).then_inc(rstd, 1)
                act.wait_ge(rnmr, h + 1)
                for t in range(2):
                    ps = wait_full(act, "ro", h, t)
                    act.activation(v[:, t, h, :], ps[:, :], ACT.Identity, bias=rst[:, t, 16:17], scale=rst[:, t, 15:16])\
                       .then_inc(freed(("ro", h, t)), 1)
            for g in range(2):
                act.wait_ge(rvar, RH + g + 1)
                act.activation(rst[:, 2, 14:15], rst[:, 2, 13:14], ACT.Sqrt, bias=epst[:, 0:1]).then_inc(rstd, 1)
                act.wait_ge(rnmr, RH + g + 1)
                for h in range(RH):
                    ps = bank[USE["so", g][0]]
                    o = 32 * h
                    last = act.activation(v[32 * g:32 * g + 32, 2, h, :], ps[o:o + 32, :], ACT.Identity,
                                          bias=rst[o:o + 32, 2, 16:17], scale=rst[o:o + 32, 2, 15:16])
                last.then_inc(freed(("so", g)), 1)
            for n in range(4):
                for t in range(3):
                    k = 3 * n + t
                    if k >= 2:
                        act.wait_ge(go_ready, k - 1)
                    staged(("rin", 8 + n, t), t, RE[:, k % 2, :], func=ACT.Silu)
            norm_act(act, 2)
            turned("x3")
            experts_act(act, 1)
            norm_act(act, 3)

        def bass_step(a, start, count, stride, width):
            part, _ = a.ap[0], a.ap[1]
            return bass.AP(a.tensor, a.offset + start, [list(part), [stride, count], [1, width]])

        def experts_dve(dve, L, step):
            def nth_full(key, p):
                b, n = nth(key, p)
                dve.wait_ge(bank_full[b], n + 1)
                return bank[b], bank_free[b]

            def flat(a):
                return a.rearrange("p (t e) -> p t e", t=3)

            def over16(a, width=NE):
                return a.unsqueeze(2).to_broadcast([128, 3, width])

            def first_max(values, weights_, width, out, tmp, top, mark):
                step(dve.tensor_reduce(top, values, AX, ALU.max))
                step(dve.tensor_tensor(tmp, values, over16(top, width), ALU.is_equal))
                step(dve.tensor_tensor(tmp, tmp, weights_.unsqueeze(1).to_broadcast([128, 3, width]), ALU.mult))
                step(dve.tensor_reduce(mark, tmp, AX, ALU.max))
                step(dve.tensor_tensor(out, tmp, over16(mark, width), ALU.is_equal))

            e3, sel3, tmp3, pick3 = flat(rt[0]), flat(rt[1]), flat(rt[2]), flat(rt[3])
            four = [rt[4][:, 12 * i:12 * i + 12].rearrange("p (t g) -> p t g", t=3) for i in range(4)]
            four += [rt[5][:, 12 * i:12 * i + 12].rearrange("p (t g) -> p t g", t=3) for i in range(4)]
            hi = rt[6][:, 0:24].rearrange("p (t g u) -> p t g u", t=3, u=2)
            lo = rt[6][:, 24:48].rearrange("p (t g u) -> p t g u", t=3, u=2)
            one = [rt[7][:, 3 * i:3 * i + 3] for i in range(8)]
            step(dve.memset(rt[0], 0.0))
            ps = wait_full(dve, "router", L)
            dve.tensor_copy(e3[:, 0:2, :], ps[:, 0:2 * NE].rearrange("p (t e) -> p t e", t=2))
            dve.tensor_copy(e3[0:64, 2, :], ps[0:64, 2 * NE:3 * NE]).then_inc(freed(("router", L)), 1)
            wait_emptied(dve, "router", L)
            step(dve.tensor_reduce(one[0], e3, AX, ALU.max))
            dve.tensor_tensor(e3, e3, over16(one[0]), ALU.subtract).then_inc(logit_max, 1)
            step(dve.memset(Y.rearrange("p t d -> p (t d)"), 0.0))
            dve.wait_ge(logit_exp, L + 1)
            step(dve.tensor_reduce(one[1], e3, AX, ALU.add))
            step(dve.reciprocal(one[2], one[1]))
            step(dve.tensor_tensor(e3, e3, over16(one[2]), ALU.mult))
            dve.wait_ge(bro_in, 16 * (L + 1))
            step(dve.tensor_tensor(sel3, e3, bro.unsqueeze(1).to_broadcast([128, 3, NE]), ALU.add))
            s5 = rt[1].rearrange("p (t g u v) -> p t g u v", t=3, g=NGRP, u=2)
            for t in range(3):
                dve.tensor_tensor(hi[:, t], s5[:, t, :, :, 0], s5[:, t, :, :, 1], ALU.max)
                last = dve.tensor_tensor(lo[:, t], s5[:, t, :, :, 0], s5[:, t, :, :, 1], ALU.min)
            step(last)
            dve.tensor_tensor(four[0], hi[:, :, :, 0], hi[:, :, :, 1], ALU.max)
            dve.tensor_tensor(four[1], hi[:, :, :, 0], hi[:, :, :, 1], ALU.min)
            step(dve.tensor_tensor(four[2], lo[:, :, :, 0], lo[:, :, :, 1], ALU.max))
            step(dve.tensor_tensor(four[3], four[1], four[2], ALU.max))
            step(dve.tensor_tensor(four[4], four[0], four[3], ALU.add))
            first_max(four[4], C["first4"], NGRP, four[5], four[6], one[3], one[4])
            step(dve.tensor_scalar(four[7], four[5], 1.0, BIG, ALU.subtract, ALU.mult))
            for t in range(3):
                a = sel3[:, t, :].rearrange("p (g u) -> p g u", g=NGRP)
                b = tmp3[:, t, :].rearrange("p (g u) -> p g u", g=NGRP)
                step(dve.tensor_tensor(b, a, four[5][:, t, :].unsqueeze(2).to_broadcast([128, NGRP, EPG]), ALU.mult))
                step(dve.tensor_tensor(a, b, four[7][:, t, :].unsqueeze(2).to_broadcast([128, NGRP, EPG]), ALU.add))
            first_max(sel3, C["first16"], NE, pick3, tmp3, one[5], one[6])
            step(dve.scalar_tensor_tensor(out=sel3, in0=pick3, scalar=-2.0 * BIG, in1=sel3, op0=ALU.mult, op1=ALU.add))
            first_max(sel3, C["first16"], NE, chosen, tmp3, one[5], one[6])
            step(dve.tensor_tensor(chosen, chosen, pick3, ALU.add))
            step(dve.tensor_tensor(gatev, e3, chosen, ALU.mult))
            dve.tensor_tensor(chosen, chosen, over16(C["valid"]), ALU.mult).then_inc(chosen_ready, 1)
            step(dve.tensor_reduce(one[1], gatev, AX, ALU.add))
            step(dve.reciprocal(one[2], one[1]))
            step(dve.tensor_tensor(gatev, gatev, over16(one[2]), ALU.mult))
            ps = wait_full(dve, "counts", L)
            dve.wait_ge(chosen_ready, L + 1)
            step(dve.scalar_tensor_tensor(out=place, in0=ps[:, 0:3 * NE].rearrange("p (t e) -> p t e", t=3), scalar=1.0, in1=chosen,
                                          op0=ALU.add, op1=ALU.mult))
            step(dve.tensor_scalar(place, place, 1.0, None, ALU.subtract))
            dve.tensor_reduce(one[7][:, 0:1], ps[:, 3 * NE:4 * NE], AX, ALU.max).then_inc(freed(("counts", L)), 1)
            wait_emptied(dve, "counts", L)
            dve.tensor_copy(most[0:1, L:L + 1], one[7][0:1, 0:1]).then_inc(most_ready, 1)

            iota = C["iota"]

            def onehots(p):
                for t in range(3):
                    last = dve.tensor_tensor(OH[:, t], iota[:, 0:SLOTS].unsqueeze(1).to_broadcast([128, 2, SLOTS]),
                                             place[:, t, pair_of(p)].unsqueeze(2).to_broadcast([128, 2, SLOTS]), ALU.is_equal)
                last.then_inc(oh_ready, 1)

            def gates(p):
                for t in range(3):
                    last = dve.tensor_tensor(G[:, t], OH[:, t], gatev[:, t, pair_of(p)].unsqueeze(2).to_broadcast([128, 2, SLOTS]), ALU.mult)
                last.then_inc(g_ready, 1)

            def pair_of(p):
                return slice(2 * p, 2 * p + 2) if isinstance(p, int) else bass.ds(p * 2, 2)

            def columns_in(key, p):
                ps, free = nth_full(key, p)
                dve.tensor_copy(xs[:, 0:4, :], ps[:, :].rearrange("p (c s) -> p c s", c=4)).then_inc(free, 1)

            def add_rows(key_p, p):
                for j in range(6):
                    ps, free = nth_full(lambda x, j=j: ("scatter", L, key_p(x), j), p)
                    t, h = j // 2, j % 2
                    r = ROWS[t]
                    y = Y[0:r, t, h * 512:(h + 1) * 512]
                    dve.tensor_tensor(y, y, ps[0:r, :], ALU.add).then_inc(free, 1)

            def pair(p, first=False, final=False):
                if not final:
                    nth_full(lambda x: ("gather", L, x, 0), p)
                    nth_full(lambda x: ("gather", L, x, 1), p)
                    dve.wait_ge(g_ready, p + (NPAIR * L + 1))
                    onehots(p + 1)
                ps, free = nth_full(lambda x: ("up", L, x), p)
                b, n = nth(lambda x: ("gate", L, x), p)
                dve.wait_ge(bank_free[b], n + 1)
                dve.tensor_tensor(hid, sil, ps[:, :], ALU.mult).then_inc(free, 1)
                if not final:
                    columns_in(lambda x: ("gather", L, x + 1, 0), p)
                if not first:
                    add_rows(lambda x: x - 1, p)
                if not final:
                    nth_full(lambda x: ("gturn", L, x), p)
                    dve.wait_ge(oh_ready, p + (NPAIR * L + 2))
                    gates(p + 1)
                ps, free = nth_full(lambda x: ("down", L, x, 0), p)
                dve.tensor_copy(ys[:, 0:512], ps[:, :]).then_inc(free, 1)

            onehots(0)
            dve.wait_ge(oh_ready, NPAIR * L + 1)
            gates(0)
            columns_in(lambda x: ("gather", L, x, 0), 0)
            pair(0, first=True)
            with dve.Fori(1, NPAIR - 1) as p:
                pair(p)
            pair(NPAIR - 1, final=True)
            add_rows(lambda x: x - 1, NPAIR)
            for j in range(4, 6):
                wait_emptied(dve, "scatter", L, NPAIR - 1, j)

            S = over[L]

            def over_body(n, b, e):
                dve.wait_ge(S["pe"], n * OV["pe"])
                dve.wait_ge(S["dve"], n * OV["dve"])
                for t in range(3):
                    last = dve.tensor_tensor(OH[:, t, 0, :], iota[:, bass.ds(b * SLOTS, SLOTS)],
                                             place[:, t, bass.ds(e, 1)].to_broadcast([128, SLOTS]), ALU.is_equal)
                last.then_inc(S["dve"], 1)
                dve.wait_ge(S["dve"], n * OV["dve"] + 1)
                for t in range(3):
                    last = dve.tensor_tensor(G[:, t, 0, :], OH[:, t, 0, :], gatev[:, t, bass.ds(e, 1)].to_broadcast([128, SLOTS]), ALU.mult)
                last.then_inc(S["dve"], 1)
                dve.wait_ge(S["pe"], n * OV["pe"] + 3)
                dve.wait_ge(S["act"], n * OV["act"] + 2)
                dve.tensor_tensor(hid[0:64, :], sil[0:64, :], bank[3][0:64, :], ALU.mult).then_inc(S["dve"], 1)
                for j in range(6):
                    dve.wait_ge(S["pe"], n * OV["pe"] + 8 + j)
                    t, h = j // 2, j % 2
                    y = Y[0:ROWS[t], t, h * 512:(h + 1) * 512]
                    dve.tensor_tensor(y, y, bank[OVER_BANK[j]][0:ROWS[t], :], ALU.add).then_inc(S["dve"], 1)

            with dve.If(overflow_any(dve, L)):
                overflow_loop(dve, over_body)
                dve.wait_ge(S["dve"], (TOK // SLOTS - 1) * NE * OV["dve"])


        @block.vector
        def _(dve):
            step = Chain(dve, dve_step)

            def rope(x, y, a, table, nh, d, r, used, ready):
                cos = table[0:r, 0, :].unsqueeze(1).to_broadcast([r, 2 * nh, d // 2])
                sin = table[0:r, 1, :].unsqueeze(1).to_broadcast([r, nh, d // 2])
                ax, xx = (z[0:r].rearrange("p (g d) -> p g d", g=2 * nh) for z in (a, x))
                dve.tensor_tensor(ax, xx, cos, ALU.mult)
                x, y, a = (z[0:r].rearrange("p (h u d) -> p h u d", h=nh, u=2) for z in (x, y, a))
                dve.tensor_tensor(y[:, :, 0, :], x[:, :, 1, :], sin, ALU.mult)
                dve.tensor_tensor(y[:, :, 1, :], x[:, :, 0, :], sin, ALU.mult).then_inc(used[0], 1)
                dve.wait_ge(used[0], used[1])
                dve.tensor_tensor(y[:, :, 0, :], a[:, :, 0, :], y[:, :, 0, :], ALU.subtract)
                last = dve.tensor_tensor(y[:, :, 1, :], a[:, :, 1, :], y[:, :, 1, :], ALU.add)
                if ready is None:
                    step(last)
                else:
                    last.then_inc(ready, 1)

            table_a = AC["rope"].rearrange("p (t u d) -> p t u d", t=3, u=2)
            causal = AC["causal"].rearrange("p (t k) -> p t k", t=2)

            def rope_unit(n):
                for t in range(3):
                    k, r = 3 * n + t, ROWS[t]
                    wait_emptied(dve, "in", n, t)
                    if k == 0:
                        dve.wait_ge(attn_c_in, 16)
                    if n:
                        wait_full(dve, "inturn", n - 1, t)
                        if n in (2, 5):
                            dve.wait_ge(tile_stored[t], 16 * (1 if n == 2 else 2))
                    if k:
                        dve.wait_ge(r_ready, k)
                    if n == 1:
                        step(dve.tensor_scalar(wi[0:r, t, :], E[0:r, k % 2, ID:W_KW], IH ** -0.5, None, ALU.mult))
                        rope(E[:, k % 2, 0:ID], R[:, t, 0:ID], ropeA[:, 0:ID], table_a[:, t], 1, ID, r, (e_used, k + 1), None)
                        dve.tensor_copy(R[0:r, t, ID:2 * ID], R[0:r, t, 0:ID]).then_inc(r_ready, 1)
                    else:
                        rope(E[:, k % 2, :], R[:, t, :], ropeA, table_a[:, t], 8, HD, r, (e_used, k + 1), r_ready)

            def choose(scores, r, nk, topk, mask, out, key=None):
                w = work[0:r, 0:nk]
                first = dve.tensor_tensor(w, scores, mask, ALU.min)
                if key:
                    first.then_inc(freed(key), 1)
                    wait_emptied(dve, *key)
                else:
                    step(first)
                left = topk
                while left > 0:
                    step(dve.max(best[0:r, :], w))
                    if left < 8:
                        step(dve.memset(best[0:r, left:8], TAKEN))
                    step(dve.match_replace(w, best[0:r, :], w, TAKEN))
                    left -= 8
                step(dve.tensor_scalar(w, w, TAKEN, BIG, ALU.is_equal, ALU.mult))
                return dve.scalar_tensor_tensor(out=out, in0=w, scalar=-BIG, in1=mask, op0=ALU.add, op1=ALU.min)

            rope_unit(0)
            rope_unit(1)
            rope_unit(2)
            ps = wait_full(dve, "wspread")
            dve.tensor_tensor(WP[0:64], AC["wsel"][0:64].rearrange("p (s t) -> p s t", s=NSEQ),
                              ps[0:64, 0:64].unsqueeze(1).to_broadcast([64, NSEQ, 64]), ALU.mult).then_inc(freed(("wspread",)), 1)
            rope_unit(3)
            m = 0
            for qt in range(2):
                nk = 128 * (qt + 1)
                for cc in range(2):
                    for par in range(2):
                        wait_emptied(dve, "index", qt, cc, par)
                        for j in range(2):
                            head = 2 * (2 * cc + j) + par
                            src, acc = relu[:, m % 2, j * nk:(j + 1) * nk], bias_p[:, qt, 0:nk]
                            if cc == par == j == 0:
                                ins = dve.tensor_scalar(acc, src, wi[:, qt, head:head + 1], None, ALU.mult)
                            else:
                                ins = dve.scalar_tensor_tensor(out=acc, in0=src, scalar=wi[:, qt, head:head + 1], in1=acc,
                                                               op0=ALU.mult, op1=ALU.add)
                            if j == 0:
                                step(ins)
                            else:
                                ins.then_inc(relu_used, 1)
                                dve.wait_ge(relu_used, m + 1)
                        m += 1
            rope_unit(4)
            rope_unit(5)
            wait_emptied(dve, "inturn", 0, 2)
            dve.wait_ge(zeroed, 4)
            for s in range(NSEQ):
                if s >= 2:
                    wait_full(dve, "sindex", s - 2)
                q0 = PROMPT + s * DSEQ
                blocks = qib[:, s % 2].rearrange("p c r -> p (c r)")
                for par in range(2):
                    o = 64 * par
                    dst = bass_step(blocks[o:o + 64, :], 8 * par, 4, 64 + 16, DSEQ)
                    last = dve.tensor_copy(dst, qiT[o:o + 64, :, q0:q0 + DSEQ])
                last.then_inc(qib_ready, 1)
            for qt in range(2):
                nk = 128 * (qt + 1)
                step(choose(bias_p[:, qt, 0:nk], 128, nk, TOPK_P, causal[:, qt, 0:nk], bias_p[:, qt, 0:nk]))
            ps = wait_full(dve, "sscore")
            step(choose(ps[0:64, 0:KEYS], 64, KEYS, TOPK_S, AC["scausal"][0:64, :], bias_s[0:64, :], ("sscore",)))
            for i in (4, 5):
                wait_emptied(dve, "inturn", i, 2)
            for t in range(3):
                dve.wait_ge(tile_stored[t], 3 * 16)
            dve.tensor_copy(KT[:, :, PAST:KEYS], kT[:, :, PROMPT:TOK]).then_inc(new_kt, 1)
            for i in (2, 3):
                wait_emptied(dve, "inturn", i, 2)

            qbf = QB.rearrange("p c r -> p (c r)")
            for s in range(NSEQ + 1):
                if s < NSEQ:
                    if s:
                        wait_full(dve, "sattn", s - 1)
                    q0 = PROMPT + s * DSEQ
                    dve.tensor_scalar(rept[0:64, s % 2, :], AC["rep"][0:64, :], AC["ofseq"][0:64, s:s + 1], None, ALU.mult)
                    for par in range(2):
                        o = 64 * par
                        last = dve.tensor_copy(bass_step(qbf[o:o + 64, :], 8 * par, KC, 128 + 16, DSEQ), qT[o:o + 64, :, q0:q0 + DSEQ])
                    last.then_inc(qb_ready, 1)
                    for j in range(2, 4):
                        ps = wait_full(dve, "kturn", s, j)
                        dve.tensor_copy(KT[:, 2 * j:2 * j + 2, 0:PAST], ps[:, :].rearrange("p (c k) -> p c k", c=2)).then_inc(freed(("kturn", s, j)), 1)
                    ps = wait_full(dve, "sattn", s)
                    c = 4 * (s % 2)
                    step(dve.tensor_reduce(small[:, c:c + 1], ps[:, 0:KEYS], AX, ALU.max))
                    dve.tensor_scalar(small[:, c + 1:c + 2], small[:, c:c + 1], -HD ** -0.5, None, ALU.mult).then_inc(max_s, 1)
                if s:
                    b = s - 1
                    ps = wait_full(dve, "pv_s", b)
                    dve.tensor_tensor(osel.rearrange("p (h d) -> p h d", h=4), ps[:, 0:256].rearrange("p (h d) -> p h d", h=4),
                                      AC["hsel"].unsqueeze(2).to_broadcast([128, 4, HD]), ALU.mult).then_inc(freed(("pv_s", b)), 1)
                    wait_emptied(dve, "pv_s", b)
                    dve.tensor_reduce(O2, osel.rearrange("p (h d) -> p d h", h=4), AX, ALU.add).then_inc(o2_s, 1)
                    ps = wait_full(dve, "oturn_s", b)
                    view = ps[0:64, 0:128].rearrange("p (c u q) -> p c u q", c=KC, u=2)
                    q0 = PROMPT + b * DSEQ
                    for par in range(2):
                        last = dve.tensor_copy(oT[64 * par:64 * par + 64, :, q0:q0 + DSEQ], view[:, :, par, :])
                    last.then_inc(freed(("oturn_s", b)), 1)
                if s < NSEQ:
                    c = 4 * (s % 2)
                    wait_emptied(dve, "sattn", s)
                    step(dve.reciprocal(small[:, c + 3:c + 4], small[:, c + 2:c + 3]))
                    dve.tensor_scalar(P[:, s % 2, 0:KEYS], P[:, s % 2, 0:KEYS], small[:, c + 3:c + 4], None, ALU.mult).then_inc(p_s, 1)

            def scale(n):
                qt = n // 8
                nk = 128 * (qt + 1)
                c = 16 + 8 * (n % 2)
                dve.wait_ge(exp_ready, n + 1)
                step(dve.reciprocal(small[:, c + 6:c + 8], small[:, c + 4:c + 6]))
                view = P[:, n % 2, 0:2 * nk].rearrange("p (j k) -> p j k", j=2)
                dve.tensor_tensor(view, view, small[:, c + 6:c + 8].unsqueeze(2).to_broadcast([128, 2, nk]), ALU.mult).then_inc(p_ready, 1)

            for n in range(16):
                qt, cc, par = n // 8, n // 2 % 4, n % 2
                nk = 128 * (qt + 1)
                c = 16 + 8 * (n % 2)
                ps = wait_full(dve, "attn", qt, cc, par)
                if n >= 2:
                    wait_full(dve, "pturn", n - 2)
                view = P[:, n % 2, 0:2 * nk].rearrange("p (j k) -> p j k", j=2)
                dve.tensor_tensor(view, ps[:, 0:2 * nk].rearrange("p (j k) -> p j k", j=2),
                                  bias_p[:, qt, 0:nk].unsqueeze(1).to_broadcast([128, 2, nk]), ALU.add).then_inc(freed(("attn", qt, cc, par)), 1)
                wait_emptied(dve, "attn", qt, cc, par)
                step(dve.tensor_reduce(small[:, c:c + 2], view, AX, ALU.max))
                dve.tensor_scalar(small[:, c + 2:c + 4], small[:, c:c + 2], -HD ** -0.5, None, ALU.mult).then_inc(max_ready, 1)
                if n:
                    scale(n - 1)
            scale(15)

            def norm(L, k):
                j = 2 * L + k
                for t in range(3):
                    r = ROWS[t]
                    if k:
                        step(dve.scalar_tensor_tensor(out=X[0:r, t, :], in0=X[0:r, t, :], scalar=ALPHA, in1=Y[0:r, t, :],
                                                      op0=ALU.mult, op1=ALU.add))
                    else:
                        for u in range(2):
                            ps = wait_full(dve, "proj", L, t, u)
                            parts = [(u * 512, 512, 0)] if t < 2 else [(u * 512, 256, 0), (u * 512 + 256, 256, 64)]
                            for x0, w, o in parts:
                                last = dve.scalar_tensor_tensor(out=X[0:r, t, x0:x0 + w], in0=X[0:r, t, x0:x0 + w], scalar=ALPHA,
                                                                in1=ps[o:o + r, 0:w], op0=ALU.mult, op1=ALU.add)
                            last.then_inc(freed(("proj", L, t, u)), 1)
                        for u in range(2):
                            wait_emptied(dve, "proj", L, t, u)
                    for u in range(2):
                        last = dve.bn_stats(bnst[0:r, t, 6 * u:6 * u + 6], X[0:r, t, u * 512:(u + 1) * 512])
                    step(last)
                    dve.bn_aggr(mv[0:r, t, :], bnst[0:r, t, :].rearrange("p (u s) -> p u s", u=2)).then_inc(var_ready, 1)
                for t in range(3):
                    r = ROWS[t]
                    dve.wait_ge(std_ready, 3 * j + t + 1)
                    step(dve.reciprocal(sv[0:r, t, 1:2], sv[0:r, t, 0:1]))
                    dve.scalar_tensor_tensor(out=sv[0:r, t, 2:3], in0=mv[0:r, t, 0:1], scalar=-1.0, in1=sv[0:r, t, 1:2],
                                             op0=ALU.mult, op1=ALU.mult).then_inc(nmr_ready, 1)
                dve.wait_ge(ln_in[j], 32)
                for t in range(3):
                    r = ROWS[t]
                    dve.wait_ge(scaled, 3 * j + t + 1)
                    step(dve.tensor_tensor(X[0:r, t, :], X[0:r, t, :], lng[0:r, :], ALU.mult))
                    dve.tensor_tensor(X[0:r, t, :], X[0:r, t, :], lnb[0:r, :], ALU.add).then_inc(x_ready, 1)

            norm(0, 0)
            experts_dve(dve, 0, step)
            norm(0, 1)

            table_r = RC["rrope"].rearrange("p (t u d) -> p t u d", t=3, u=2)
            for n in range(4):
                for t in range(3):
                    k, r = 3 * n + t, ROWS[t]
                    wait_emptied(dve, "rin", n, t)
                    if k == 0:
                        dve.wait_ge(ret_c_in, 16)
                    if k >= 1:
                        dve.wait_ge(rk_ready, k)
                    if n < 2:
                        if k >= 2:
                            wait_full(dve, "rturn", (k - 2) // 3, (k - 2) % 3)
                        out = RR[:, k % 2, :]
                    else:
                        out = kt[:, t, 2 * (n - 2):2 * (n - 2) + 2].rearrange("p h d -> p (h d)")
                    rope(RE[:, k % 2, :], out, rropeA, table_r[:, t], 2, RQ, r, (re_used, k + 1), rk_ready)
            for t in range(2):
                for n in (2, 3):
                    wait_full(dve, "rturn", n, t)
            kp = kt[:, 0:2].rearrange("p t h d -> p (t h) d")
            dve.tensor_tensor(kp, kp, RC["kdecay"].unsqueeze(2).to_broadcast([128, 2 * RH, RQ]), ALU.mult).then_inc(kd_ready, 1)
            for n in range(2):
                wait_full(dve, "rturn", n, 2)
                wait_emptied(dve, "rturn", n, 2)
            dve.wait_ge(rk_ready, 12)
            step(dve.memset(QM, 0.0))
            decay = RC["qdecay"].rearrange("p (x q) -> p x q", x=2 * RH)
            for s in range(NSEQ):
                last = dve.tensor_tensor(QM[:, :, s, 8 * (s % 4):8 * (s % 4) + 8], rqT[:, :, PROMPT + 8 * s:PROMPT + 8 * s + 8],
                                         decay, ALU.mult)
            last.then_inc(qm_ready, 1)
            for h in range(RH):
                ps = wait_full(dve, "inner", h)
                dve.tensor_tensor(inn[:, 0:256], ps[:, 0:256], RC["decay"][:, h * 256:(h + 1) * 256], ALU.mult)
                dve.tensor_tensor(inn[:, 256:384], ps[:, 256:384], RC["decay"][:, h * 256:h * 256 + 128], ALU.mult)\
                   .then_inc(freed(("inner", h)), 1)
                for t in range(2):
                    ps = wait_full(dve, "ro", h, t)
                    step(dve.bn_stats(rst[:, t, 0:6], ps[:, :]))
                    last = dve.bn_aggr(rst[:, t, 12:14], rst[:, t, 0:6])
                    if t == 0:
                        step(last)
                last.then_inc(rvar, 1)
                dve.wait_ge(rstd, h + 1)
                step(dve.reciprocal(rst[:, 0:2, 15:16], rst[:, 0:2, 14:15]))
                dve.scalar_tensor_tensor(out=rst[:, 0:2, 16:17], in0=rst[:, 0:2, 12:13], scalar=-1.0, in1=rst[:, 0:2, 15:16],
                                         op0=ALU.mult, op1=ALU.mult).then_inc(rnmr, 1)
                for t in range(2):
                    wait_emptied(dve, "ro", h, t)
            ps = wait_full(dve, "sinner")
            dve.tensor_tensor(innS[0:64].rearrange("p h i -> p (h i)"), ps[0:64, 0:256], RC["sdecay"][0:64, :], ALU.mult)\
               .then_inc(freed(("sinner",)), 1)
            ksel = RC["ksel"].rearrange("p (s h) -> p s h", s=NSEQ)
            for s in range(NSEQ):
                if s:
                    wait_full(dve, "update", s - 1, 7)
                dve.tensor_tensor(kd[0:64], kt[0:64, 2], ksel[0:64, s, :].unsqueeze(2).to_broadcast([64, RH, RQ]), ALU.mult)\
                   .then_inc(kd_ready, 1)
                st = weights(UNIT["state", s])
                for j in range(8):
                    ps = wait_full(dve, "update", s, j)
                    dve.scalar_tensor_tensor(out=st[:, j, :], in0=st[:, j, :], scalar=GAMMA8[j // 2], in1=ps[:, :],
                                             op0=ALU.mult, op1=ALU.add).then_inc(freed(("update", s, j)), 1)
            for g in range(2):
                ps = wait_full(dve, "so", g)
                if g:
                    wait_emptied(dve, "so", 0)
                step(dve.bn_stats(rst[:, 2, 0:6], ps[:, :]))
                dve.bn_aggr(rst[:, 2, 12:14], rst[:, 2, 0:6]).then_inc(rvar, 1)
                dve.wait_ge(rstd, RH + g + 1)
                step(dve.reciprocal(rst[:, 2, 15:16], rst[:, 2, 14:15]))
                dve.scalar_tensor_tensor(out=rst[:, 2, 16:17], in0=rst[:, 2, 12:13], scalar=-1.0, in1=rst[:, 2, 15:16],
                                         op0=ALU.mult, op1=ALU.mult).then_inc(rnmr, 1)
            wait_emptied(dve, "so", 1)

            def gained(n, t):
                ps = wait_full(dve, "oturn", n, t)
                r = ROWS[t]
                dve.tensor_tensor(roT[:, 4 * n:4 * n + 4, t * 128:t * 128 + r], ps[:, :].rearrange("p (c t) -> p c t", c=4)[:, :, 0:r],
                                  gain[:, 4 * n:4 * n + 4].unsqueeze(2).to_broadcast([128, 4, r]), ALU.mult).then_inc(freed(("oturn", n, t)), 1)

            dve.wait_ge(gain_in, 16)
            for n in range(4):
                for t in range(3):
                    k, r = 3 * n + t, ROWS[t]
                    wait_emptied(dve, "rin", 8 + n, t)
                    dve.tensor_tensor(v[0:r, t, n, :], v[0:r, t, n, :], RE[0:r, k % 2, :], ALU.mult).then_inc(go_ready, 1)
                    if n:
                        gained(n - 1, t)
            for t in range(3):
                gained(3, t)
            norm(1, 0)
            experts_dve(dve, 1, step)
            norm(1, 1)

INS = {"x_p": lambda a: a["x_prompt"].reshape(PROMPT, D), "x_s": lambda a: a["x_sample"].reshape(SAMPLE, D),
       **{n: (lambda a, n=n: a[n]) for n in ("cache_k", "cache_v", "cache_idx_k", "state_ret", "page_table", "w_in_attn",
                                             "w_out_attn", "w_in_ret", "ret_norm_gain", "w_out_ret", "w_router", "b_router",
                                             "w_exp_gate", "w_exp_up", "w_exp_down", "ln_gain", "ln_bias")}}
OUTS = {"y_p": ((PROMPT, D), (1, PROMPT, D)), "y_s": ((SAMPLE, D), (NSEQ, DSEQ, D)),
        "k_p": ((PROMPT, D), (1, 1, PROMPT, HEADS, HD)), "v_p": ((PROMPT, D), (1, 1, PROMPT, HEADS, HD)),
        "ik_p": ((PROMPT, ID), (1, 1, PROMPT, ID)),
        "k_s": ((SAMPLE, D), (1, NSEQ, DSEQ, HEADS, HD)), "v_s": ((SAMPLE, D), (1, NSEQ, DSEQ, HEADS, HD)),
        "ik_s": ((SAMPLE, ID), (1, NSEQ, DSEQ, ID)),
        "state_p": ((RH, RQ, RV), (1, 1, RH, RQ, RV)), "state_s": ((NSEQ, RH, RQ, RV), (1, NSEQ, RH, RQ, RV))}


def kernel(**inputs):
    import concourse.bacc as bacc
    from concourse.bass_utils import run_bass_kernel_spmd

    nc = bacc.Bacc("TRN2", target_bir_lowering=False, num_devices=1)
    common, attn, ret = constants()
    arrays = {n: np.ascontiguousarray(f(inputs)) for n, f in INS.items()}
    arrays |= {"c_common": common, "c_attn": attn, "c_ret": ret}
    ins = {n: nc.dram_tensor(f"in_{n}", a.shape, mybir.dt.from_np(a.dtype), kind="ExternalInput").ap() for n, a in arrays.items()}
    outs = {n: nc.dram_tensor(f"out_{n}", shape, F32, kind="ExternalOutput").ap() for n, (shape, _) in OUTS.items()}
    build(nc, ins, outs)
    r = run_bass_kernel_spmd(nc, [{f"in_{n}": a for n, a in arrays.items()}], core_ids=[0])
    return tuple(np.asarray(r.results[0][f"out_{n}"]).reshape(shape) for n, (_, shape) in OUTS.items())
```

```python
from contextlib import ExitStack

import numpy as np
import concourse.bass as bass
from concourse import mybir

ALU = mybir.AluOpType
ACT = mybir.ActivationFunctionType
AX = mybir.AxisListType.X
F32 = mybir.dt.float32
F32R = mybir.dt.float32r
I32 = mybir.dt.int32

D = 1024
KC = D // 128
PROMPT, NSEQ, DSEQ = 256, 8, 8
SAMPLE = NSEQ * DSEQ
TOK = PROMPT + SAMPLE
ROWS = [128, 128, 64]
PAST, PAGE = 256, 128
HEADS, HD = 16, 64
IH, ID = 8, 64
TOPK_P, TOPK_S = PROMPT // 4, (PAST + DSEQ) // 4
KEYS = PAST + SAMPLE
RH, RQ, RV = 4, 256, 512
NE, NGRP, EPG, ED = 16, 4, 4, 512
SLOTS = 64
ALPHA = 4.0 ** 0.25
EPS = 1e-5
BIG = 2.0 ** 120
TAKEN = -(2.0 ** 125)
W_KW = ID + IH
NRING, SLOT = 6, 4096

IN_ORDER = (6, 7, 0, 1, 2, 3, 4, 5)
STREAM = ([("in", u) for u in IN_ORDER] + [("cache", s) for s in range(NSEQ)]
          + [("out", u) for u in range(2)] + [("moe0", n) for n in range(3 * NE)]
          + [("rin", u) for u in range(8)] + [("state", s) for s in range(NSEQ)]
          + [("rin", u) for u in range(8, 12)] + [("rout", u) for u in range(4)]
          + [("moe1", n) for n in range(3 * NE)])


def plan_slots():
    place, before, high, high_before, held = {}, {}, {}, {}, {}

    def load(key, s):
        place[key], before[key], held[s] = s, held.get(s), key

    def rounded(key, s):
        high[key], high_before[key], held[s] = s, held.get(s), key

    for n, u in enumerate(IN_ORDER):
        if n == 1:
            load(("in", u), 3)
            high["in", u], high_before["in", u] = 3, None
        else:
            m = n - (n > 1)
            load(("in", u), m % 3)
            rounded(("in", u), 4 + m % 2)
    held[3] = ("in", IN_ORDER[7])
    for s, where in enumerate((1, 2, 0, 5, 4, 3, 1, 2)):
        load(("cache", s), where)
    load(("out", 0), 0)
    load(("out", 1), 5)
    for j in range(6):
        load(("moe0", j), j)
        held[j] = ("moe0", 3 * NE - 6 * (1 + (j < 2)) + j)
    for n in range(8):
        load(("rin", n), n % 3)
        rounded(("rin", n), 4 + n % 2)
    for s, where in enumerate((2, 0, 1, 4, 5, 2, 0, 1)):
        load(("state", s), where)
    for n, where, copy_at in ((8, 4, 5), (9, 2, 0), (10, 1, 4), (11, 5, 2)):
        load(("rin", n), where)
        rounded(("rin", n), copy_at)
    held[3] = ("rin", 11)
    for n, where, copy_at in ((0, 0, 1), (1, 4, 5), (2, 2, 3), (3, 0, 1)):
        load(("rout", n), where)
        rounded(("rout", n), copy_at)
    for j in range(6):
        load(("moe1", j), j)
    return place, before, high, high_before


PLACE, BEFORE, HIGH, HIGH_BEFORE = plan_slots()
PARTED = [("in", u) for u in IN_ORDER] + [("rin", n) for n in range(12)] + [("rout", n) for n in range(4)]
WIDE = 256 + 2 * SAMPLE
LOW_X = KC * WIDE


def landed_counts():
    total, out = [0] * NRING, {}
    for kind, u in STREAM:
        s = u % 6 if kind in ("moe0", "moe1") else PLACE[kind, u]
        if kind in ("moe0", "moe1") and s < 2 and u // 6 % 2:
            continue
        total[s] += 64 if kind == "cache" else 16
        out[kind, u] = total[s]
    return out


LANDED = landed_counts()


def last_product(unit):
    kind, u = unit
    if kind in ("moe0", "moe1"):
        p, what = u // 6, u % 6 // 2
        return (("gate", "up", "down")[what], int(kind[3]), p) + ((1,) if what == 2 else ())
    return {"in": ("in", IN_ORDER.index(u) if kind == "in" else 0, 2), "cache": ("pv_s", u), "out": ("proj", 0, 2, u),
            "rin": ("rin", u, 2), "rout": ("proj", 1, 2, u // 2)}[kind]


def psum_uses():
    count, use = [0] * 8, {}

    def take(key, bank):
        use[key] = (bank, count[bank])
        count[bank] += 1

    def turn(name):
        for t in range(3):
            for h in range(2):
                take((name, t, h), 2 * t + h)

    def moe(L):
        take(("router", L), 6)
        take(("counts", L), 7)
        take(("totals", L), 4)

        def gather(p):
            take(("gather", L, p, 0), 0)
            take(("gather", L, p, 1), 1)

        gather(0)
        for p in range(NE // 2):
            take(("gate", L, p), 2)
            take(("up", L, p), 3)
            if p < NE // 2 - 1:
                gather(p + 1)
            take(("hturn", L, p), 4)
            if p:
                for j in range(6):
                    take(("scatter", L, p - 1, j), (6, 7, 5)[j % 3])
            take(("gturn", L, p), 4)
            take(("down", L, p, 0), 6)
            take(("down", L, p, 1), 7)
        for j in range(6):
            take(("scatter", L, NE // 2 - 1, j), (6, 7, 5)[j % 3])

    def index_step(k):
        if k < NSEQ:
            take(("ikturn", k), 6)
        if k == 0:
            take(("sscore",), 7)
        if 0 < k <= NSEQ:
            take(("sindex", k - 1), 4 + k % 2)

    turn("x0")
    for n in range(8):
        for t in range(3):
            take(("in", n, t), (3 * n + t) % 4)
            if 0 < n <= 6:
                take(("inturn", n - 1, t), 4 + (3 * n + t) % 2)
            if n >= 5:
                index_step(3 * (n - 5) + t)
        if n == 2:
            take(("wturn",), 6)
            take(("wspread",), 7)
        if n == 3:
            for qt in range(2):
                for cc in range(2):
                    for par in range(2):
                        take(("index", qt, cc, par), 6 + par)
    index_step(NSEQ + 1)
    for n in range(16):
        qt, cc, par = n // 8, n // 2 % 4, n % 2
        take(("attn", qt, cc, par), n % 4)
        if n >= 2:
            take(("pturn", n - 2), 4 + n % 2)
            take(("pv", n - 2), 6 + n % 2)
    for n in (16, 17):
        take(("pturn", n - 2), 4 + n % 2)
        take(("pv", n - 2), 6 + n % 2)
    for s in range(NSEQ + 2):
        if s < NSEQ:
            for j in range(4):
                take(("kturn", s, j), j)
        if s >= 2:
            take(("oturn_s", s - 2), 4 + (s - 1) % 2)
        if 0 < s <= NSEQ:
            take(("pturn_s", s - 1), 6)
        if s < NSEQ:
            take(("sattn", s), 4 + s % 2)
        if 0 < s <= NSEQ:
            take(("pv_s", s - 1), 7)
    for u in range(2):
        for t in range(3):
            take(("proj", 0, t, u), 2 * t + u)
    turn("x1")
    moe(0)
    turn("x2")
    for n in range(8):
        for t in range(3):
            take(("rin", n, t), (3 * n + t) % 4)
            if 0 < n <= 4:
                take(("rturn", n - 1, t), 4 + (3 * n + t) % 2)
    take(("sinner",), 1)
    take(("so", 0), 6)
    take(("so", 1), 7)
    for s in range(NSEQ):
        for j in range(8):
            take(("update", s, j), 2 + j % 4)
    for h in range(RH):
        take(("inner", h), 0)
        take(("rstate", h, 0), 4)
        take(("rstate", h, 1), 5)
        take(("ro", h, 0), 2 if h % 2 == 0 else 6)
        take(("ro", h, 1), 3 if h % 2 == 0 else 7)
    for n in range(4):
        for t in range(3):
            take(("rin", 8 + n, t), (3 * n + t) % 4)
            if n:
                take(("oturn", n - 1, t), 4 + (3 * n + t) % 2)
    for t in range(3):
        take(("oturn", 3, t), (5, 7, 5)[t])
    for u in range(2):
        for t in range(3):
            take(("proj", 1, t, u), 2 * t + u)
    turn("x3")
    moe(1)
    return use


USE = psum_uses()

COMMON = {"ident": 128, "tri": 128, "iota": TOK, "first16": NE, "first4": NGRP, "valid": 3}
ATTN_C = {"rope": 3 * 2 * 32, "causal": 512, "scausal": KEYS, "rep": 128, "ofseq": NSEQ,
          "wsel": NSEQ * 64, "hrep": 64, "hsel": 4}
RET_C = {"rrope": 3 * 2 * 128, "decay": RH * 256, "sdecay": RH * 64, "qdecay": 2 * RH * DSEQ,
         "kdecay": 2 * RH, "ksel": NSEQ * RH}


def constants():
    f = np.float32
    pos = np.concatenate([np.arange(PROMPT), PAST + np.arange(SAMPLE) % DSEQ, np.zeros(64, int)])
    pos = pos.reshape(3, 128)

    def rope(d):
        inv = f(10000.0) ** (-np.arange(0, d, 2, dtype=f) / f(d))
        ang = pos.astype(f)[:, :, None] * inv[None, None, :]
        t = np.stack([np.cos(ang), np.sin(ang)], 2)
        return t.transpose(1, 0, 2, 3).reshape(128, -1)

    i = np.arange(128)
    t64 = np.arange(64)
    c = {"ident": np.eye(128), "tri": (i[:, None] < i[None, :]), "iota": np.tile(np.arange(TOK), (128, 1)),
         "first16": np.tile(NE - np.arange(NE), (128, 1)), "first4": np.tile(NGRP - np.arange(NGRP), (128, 1)),
         "valid": np.stack([i >= 0, i >= 0, i < 64], 1), "rope": rope(HD)}
    q = i[:, None, None] + 128 * np.arange(2)[None, :, None]
    c["causal"] = np.where(np.arange(256)[None, None, :] <= q, BIG, -BIG).reshape(128, 512)
    sc = np.full((128, KEYS), BIG)
    same = (t64[:, None] // DSEQ == t64[None, :] // DSEQ) & (t64[None, :] % DSEQ <= t64[:, None] % DSEQ)
    sc[:64, PAST:] = np.where(same, BIG, -BIG)
    c["scausal"] = sc
    c["rep"] = np.zeros((128, 128))
    c["rep"][:64] = t64[:, None] % DSEQ == i[None, :] % DSEQ
    c["ofseq"] = i[:, None] // DSEQ == np.arange(NSEQ)[None, :]
    w = np.zeros((128, NSEQ, 64))
    w[:64] = (t64[:, None, None] % DSEQ == t64[None, None, :] % DSEQ) & (t64[None, None, :] // DSEQ == np.arange(NSEQ)[None, :, None])
    c["wsel"] = w.reshape(128, -1)
    c["hrep"] = np.zeros((128, 64))
    c["hrep"][:IH] = np.arange(IH)[:, None] == t64[None, :] // DSEQ
    c["hsel"] = (i[:, None] // DSEQ) % 4 == np.arange(4)[None, :]
    lg = np.log(1.0 - 2.0 ** (-5.0 - np.arange(RH)))
    ks = 1.0 / 16.0
    c["rrope"] = rope(RQ)
    diff = (np.arange(256)[None, :] - i[:, None])[:, None, :]
    c["decay"] = np.where(diff >= 0, np.exp(diff * lg[None, :, None]) * ks, 0).reshape(128, -1)
    sd = np.zeros((128, RH, 64))
    d8 = (t64[None, :] - t64[:, None])[:, None, :]
    inseq = (t64[None, :] // DSEQ == t64[:, None] // DSEQ)[:, None, :]
    sd[:64] = np.where((d8 >= 0) & inseq, np.exp(d8 * lg[None, :, None]) * ks, 0)
    c["sdecay"] = sd.reshape(128, -1)
    qd = np.exp((np.arange(DSEQ) + 1)[None, None, :] * lg[:, None, None]).repeat(2, 1)
    c["qdecay"] = np.tile(qd.reshape(1, -1), (128, 1))
    kd = 255 - i[:, None, None] - 128 * np.arange(2)[None, :, None]
    c["kdecay"] = (np.exp(kd * lg[None, None, :]) * ks).reshape(128, -1)
    k8 = np.exp((DSEQ - 1 - i % DSEQ)[:, None, None] * lg[None, None, :]) * ks
    c["ksel"] = np.where((i[:, None] // DSEQ == np.arange(NSEQ)[None, :])[:, :, None], k8, 0).reshape(128, -1)
    pack = lambda names: np.concatenate([np.asarray(c[n], f).reshape(128, names[n]) for n in names], 1)
    return pack(COMMON), pack(ATTN_C), pack(RET_C)


GAMMA8 = [float(np.exp(DSEQ * np.log(1.0 - 2.0 ** (-5.0 - h)))) for h in range(RH)]


def nth(key, p):
    if isinstance(p, int):
        return USE[key(p)]
    (b, n1), (_, n2) = USE[key(1)], USE[key(2)]
    assert all(USE[key(i)] == (b, n1 + (i - 1) * (n2 - n1)) for i in range(1, NE // 2 - 1))
    return b, p * (n2 - n1) + (2 * n1 - n2)


def columns(view, names):
    out, at = {}, 0
    for n, w in names.items():
        out[n] = view[:, at:at + w]
        at += w
    return out


class Chain:

    def __init__(self, eng, sem):
        self.eng, self.sem, self.n = eng, sem, 0

    def __call__(self, ins):
        self.n = self.n + 1
        ins.then_inc(self.sem, 1)
        self.eng.wait_ge(self.sem, self.n)


def build(nc, A, O):
    with ExitStack() as ctx:
        def sb(name, width, dt=F32, rows=128):
            return ctx.enter_context(nc.sbuf_tensor(name, [rows, width], dt))

        def sem(name):
            return ctx.enter_context(nc.semaphore(name))

        as_parts = {}

        def sb_with_parts(name, width):
            at = -(-nc.sbuf_base // 32) * 32
            a = sb(name, width)
            assert nc.sbuf_base == at + 4 * width
            as_parts[name] = nc.alloc_sbuf_tensor_at(name + "_parts", [128, width], F32R, offset=at)
            return a

        def single(a):
            return bass.AP(as_parts[a.tensor.name][:, :].tensor, a.offset, [list(d) for d in a.ap])

        ring = sb_with_parts("ring", NRING * SLOT)
        Xt = sb("Xt", 3 * D)
        XTt = sb_with_parts("XTt", KC * TOK)
        com = sb("com", sum(COMMON.values()))
        ones = sb("ones", 128)
        stats = sb("stats", 3 * 12 + 3 * 2 + 3 * 4)
        epst = sb("epst", 1)
        pages = sb("pages", NSEQ * 2, I32, 1)
        most = sb("most", 4, I32, 1)
        wrt = sb("wrt", KC * NE)
        bro = sb("bro", NE)
        ARENA = 22030
        narrow = nc.alloc_sbuf_tensor_at("narrow_parts", [128, KC * W_KW], F32R, offset=-(-nc.sbuf_base // 32) * 32)
        arena = sb_with_parts("arena", ARENA)
        bank = [ctx.enter_context(nc.psum_tensor(f"bank{b}", [128, 512], F32)) for b in range(8)]

        X = Xt[:, :].rearrange("p (t d) -> p t d", t=3)
        XT = XTt[:, :].rearrange("p (c t) -> p c t", c=KC)
        C = columns(com, COMMON)
        ident = C["ident"]
        bnst = stats[:, 0:36].rearrange("p (t j) -> p t j", t=3)
        mv = stats[:, 36:42].rearrange("p (t j) -> p t j", t=3)
        sv = stats[:, 42:54].rearrange("p (t j) -> p t j", t=3)

        def slot(s):
            return ring[:, s * SLOT:(s + 1) * SLOT]

        XLOW = slot(3)[:, 0:LOW_X].rearrange("p (c t) -> p c t", c=KC)

        at = [0]

        def part(width, start=None):
            if start is not None:
                at[0] = start
            a = arena[:, at[0]:at[0] + width]
            at[0] += width
            assert at[0] <= ARENA, at[0]
            return a

        lng, lnb = part(D, 0), part(D)
        AC = columns(part(sum(ATTN_C.values())), ATTN_C)
        qT = part(KC * TOK).rearrange("p (c t) -> p c t", c=KC)
        kT = part(KC * TOK).rearrange("p (c t) -> p c t", c=KC)
        qiT = part(4 * TOK).rearrange("p (c t) -> p c t", c=4)
        kiT = part(TOK)
        V = part(3 * D).rearrange("p (t d) -> p t d", t=3)
        wi = part(3 * IH).rearrange("p (t h) -> p t h", t=3)
        bias_p = part(512).rearrange("p (t k) -> p t k", t=2)
        bias_s = part(KEYS)
        small = part(64)
        best = part(8)
        QB = part(KC * 128).rearrange("p (c r) -> p c r", c=KC)
        here = at[0]
        E = part(1024).rearrange("p (b n) -> p b n", b=2)
        ropeA = part(512)
        R = part(1536).rearrange("p (b n) -> p b n", b=3)
        KT = part(KC * KEYS, here).rearrange("p (c t) -> p c t", c=KC)
        at[0] = here + 3072
        here = at[0]
        ikraw = arena[:, 1024:2048].rearrange("p (s g d) -> p s g d", s=NSEQ, g=2)
        kiS = part(2 * KEYS).rearrange("p (b k) -> p b k", b=2)
        qib = part(512).rearrange("p (b c r) -> p b c r", b=2, c=4)
        relu = arena[:, 0:1024].rearrange("p (b n) -> p b n", b=2)
        reluS = part(2 * KEYS).rearrange("p (b k) -> p b k", b=2)
        WP = part(512).rearrange("p (s t) -> p s t", s=NSEQ)
        wiT = part(64)
        work = part(512)
        end1 = at[0]
        P = part(3 * 512, here).rearrange("p (b n) -> p b n", b=3)
        PT = part(1024).rearrange("p (b n) -> p b n", b=2)
        osel = part(256)
        O2 = part(64)
        rept = part(256).rearrange("p (b n) -> p b n", b=2)
        oT = XT
        Y = part(3 * D, 2 * D).rearrange("p (t d) -> p t d", t=3)
        OH = part(3 * 128).rearrange("p (t j s) -> p t j s", t=3, j=2)
        G = part(3 * 128).rearrange("p (t j s) -> p t j s", t=3, j=2)
        GT = part(TOK)
        ys = part(D)
        rt = [ys[:, i * 3 * NE:(i + 1) * 3 * NE] for i in range(8)]
        gatev = part(3 * NE).rearrange("p (t e) -> p t e", t=3)
        place = part(3 * NE).rearrange("p (t e) -> p t e", t=3)
        chosen = part(3 * NE).rearrange("p (t e) -> p t e", t=3)
        yslow, OHT, gs = part(D), part(TOK), part(8)[:, 0:1]
        extra = [part(SLOT), part(SLOT)]
        wover = extra
        xs = XTt[:, 0:KC * 128].rearrange("p (c s) -> p c s", c=KC)
        sil, hid, hT = [XTt[:, KC * 128 + i * 512:KC * 128 + (i + 1) * 512] for i in range(3)]
        hT = hT.rearrange("p (m s) -> p m s", m=4)
        RC = columns(part(sum(RET_C.values()), 0), RET_C)
        at[0] = max(at[0], 2 * D)
        v = part(3 * RH * RV).rearrange("p (t h n) -> p t h n", t=3, h=RH)
        kt_flat = part(3 * D)
        kt = kt_flat.rearrange("p (t h d) -> p t h d", t=3, h=RH)
        rqT = part(KC * TOK).rearrange("p (c t) -> p c t", c=KC)
        rkT = part(KC * TOK).rearrange("p (c t) -> p c t", c=KC)
        roT = arena[:, at[0] - 2 * KC * TOK:at[0]].rearrange("p (c t) -> p c t", c=2 * KC)
        gain = part(RH * RV // 128)
        inn = part(384)
        rst = part(3 * 20).rearrange("p (t j) -> p t j", t=3)
        innS = part(RH * 64).rearrange("p (h i) -> p h i", h=RH)
        at_kd = at[0]
        kd = part(D).rearrange("p (h d) -> p h d", h=RH)
        st_out = part(1024).rearrange("p (b n) -> p b n", b=2)
        here = at[0]
        RE = part(1024).rearrange("p (b n) -> p b n", b=2)
        rropeA = part(512)
        RR = part(1024).rearrange("p (b n) -> p b n", b=2)
        rlow = [kt_flat[:, n * 4 * WIDE:(n + 1) * 4 * WIDE] for n in range(2)]
        rlow += [arena[:, at_kd:at_kd + 4 * WIDE], arena[:, here + 1024:here + 1024 + 4 * WIDE]]
        rlow = [a.rearrange("p (c t) -> p c t", c=4) for a in rlow]
        QM = part(RH * 2 * NSEQ * 32, here).rearrange("p (x s t) -> p x s t", x=RH * 2, s=NSEQ)

        bank_full = [sem(f"bank_full{b}") for b in range(8)]
        bank_free = [sem(f"bank_free{b}") for b in range(8)]
        landed = [sem(f"landed{i}") for i in range(NRING)]
        state_stored = [sem(f"state_stored{s}") for s in range(NSEQ)]
        dve_step, act_step = sem("dve_step"), sem("act_step")
        x_in, com_in, attn_c_in, ret_c_in = sem("x_in"), sem("com_in"), sem("attn_c_in"), sem("ret_c_in")
        router_in, gain_in, pages_in = sem("router_in"), sem("gain_in"), sem("pages_in")
        ln_in = [sem(f"ln_in{j}") for j in range(4)]
        ik_in = sem("ik_in")
        bro_in = sem("bro_in")
        zeroed = sem("zeroed")
        e_used, re_used = sem("e_used"), sem("re_used")
        r_ready, rk_ready = sem("r_ready"), sem("rk_ready")
        tile_stored = [sem(f"tile_stored{t}") for t in range(3)]
        v_stored, y_stored = sem("v_stored"), sem("y_stored")
        relu_used, qib_ready, bias_ready = sem("relu_used"), sem("qib_ready"), sem("bias_ready")
        qb_ready, new_kt = sem("qb_ready"), sem("new_kt")
        max_s, exp_s, p_s, o2_s = sem("max_s"), sem("exp_s"), sem("p_s"), sem("o2_s")
        max_ready, exp_ready, p_ready = sem("max_ready"), sem("exp_ready"), sem("p_ready")
        var_ready, std_ready, x_ready, y_begun = sem("var_ready"), sem("std_ready"), sem("x_ready"), sem("y_begun")
        logit_max, logit_exp, chosen_ready, most_ready = (sem("logit_max"), sem("logit_exp"), sem("chosen_ready"),
                                                          sem("most_ready"))
        oh_ready, g_ready = sem("oh_ready"), sem("g_ready")
        over = [{e: sem(f"over_{e}{L}") for e in ("gate", "up", "down", "pe", "act", "dve")} for L in range(2)]
        sto_stored = [sem("sto_stored0"), sem("sto_stored1")]
        rvar, rstd, rnmr, o_ready = sem("rvar"), sem("rstd"), sem("rnmr"), sem("o_ready")
        qm_ready, kd_ready, go_ready = sem("qm_ready"), sem("kd_ready"), sem("go_ready")

        high_ready, low_ready, first_low_ready, x_high = (sem("high_ready"), sem("low_ready"), sem("first_low_ready"),
                                                          sem("x_high"))
        ro_high, ro_ready, rout_used = sem("ro_high"), sem("ro_ready"), sem("rout_used")
        extra_landed = [sem("extra_landed0"), sem("extra_landed1")]
        ys_high, oht_ready = sem("ys_high"), sem("oht_ready")
        half_ready, silu_ready = sem("half_ready"), sem("silu_ready")
        NIN = len(IN_ORDER)

        block = ctx.enter_context(nc.Block())
        NPAIR = NE // 2

        def wait_full(eng, *key):
            b, n = USE[key]
            eng.wait_ge(bank_full[b], n + 1)
            return bank[b]

        def wait_emptied(eng, *key):
            b, n = USE[key]
            eng.wait_ge(bank_free[b], n + 1)

        def freed(key):
            return bank_free[USE[key][0]]

        def token_rows(prompt, sample, t):
            return prompt[t * 128:(t + 1) * 128, :] if t < 2 else sample[:, :]

        def expert_weights(L, what, e):
            w = (A["w_exp_gate"], A["w_exp_up"], A["w_exp_down"])[what]
            return w[L, e].rearrange("(k p) n -> p k n", p=128)

        def unit_source(kind, u):
            c512 = slice(u * 512, (u + 1) * 512)
            if kind == "in":
                return A["w_in_attn"][0, :, c512 if u < 7 else slice(3584, 3584 + W_KW)].rearrange("(k p) n -> p k n", p=128)
            if kind == "out":
                return A["w_out_attn"][0, :, c512].rearrange("(k p) n -> p k n", p=128)
            if kind == "rin":
                return A["w_in_ret"][0, :, c512].rearrange("(k p) n -> p k n", p=128)
            if kind == "rout":
                n, k = u // 2, u % 2
                return A["w_out_ret"][0, k * D:(k + 1) * D, n * 512:(n + 1) * 512].rearrange("(k p) n -> p k n", p=128)
            return A["state_ret"][0, u].rearrange("h (c p) n -> p (h c) n", p=128)

        def width_of(key):
            return W_KW if key == ("in", 7) else 512

        def weights(key):
            at = LOW_X if key == ("in", 7) else 0
            return slot(PLACE[key])[:, at:at + KC * width_of(key)].rearrange("p (k n) -> p k n", k=KC)

        def rounded(key):
            if key == ("in", 7):
                return narrow[:, :].rearrange("p (k n) -> p k n", k=KC)
            return single(slot(HIGH[key]).rearrange("p (k n) -> p k n", k=KC))

        def wait_landed(eng, key):
            eng.wait_ge(landed[PLACE[key]], LANDED[key])

        def wait_let_go(eng, key):
            if key and key[0] == "state":
                eng.wait_ge(state_stored[key[1]], 16)
            elif key and key[0] == "rout" and key[1] % 2 == 0:
                eng.wait_ge(rout_used, key[1] // 2 + 1)
            elif key:
                wait_full(eng, *last_product(key))

        def gated_places(n, t):
            if t < 2:
                cols = slice(t * 128, t * 128 + 128)
                return cols, roT[:, 4 * n:4 * n + 4, cols]
            return slice(320, 384), rlow[n][:, :, 256:320]

        def high_part(act, d):
            key = PARTED[d]
            wait_landed(act, key)
            wait_let_go(act, HIGH_BEFORE[key])
            for k in ([slice(0, 4), slice(4, 8)] if d == 0 else [slice(0, 8)]):
                act.activation(rounded(key)[:, k], weights(key)[:, k], ACT.Copy).then_inc(high_ready, 1)

        def low_part(pool, d):
            key = PARTED[d]
            pool.wait_ge(high_ready, d + 2)
            pool.tensor_tensor(single(weights(key)), weights(key), rounded(key), ALU.subtract).then_inc(low_ready, 1)

        def expert_slot(j):
            return slot(j).rearrange("p (k n) -> p k n", k=KC if j < 4 else 4)

        def overflow_any(eng, L):
            eng.wait_ge(most_ready, L + 1)
            return eng.value_load(most[0:1, L:L + 1], min_val=0, max_val=TOK) > SLOTS

        OV = {"gate": 16, "up": 16, "down": 16, "pe": 13, "act": 6, "dve": 9}

        OVER_BANK = (0, 1, 0, 1, 2, 3)

        def overflow_loop(eng, body):
            with eng.Fori(1, TOK // SLOTS) as b:
                with eng.Fori(0, NE) as e:
                    body((b - 1) * NE + e, b, e)

        def expert_load(sp, L, j, p, parity=0):
            what, back = j // 2, 2 if j < 2 else 1
            dst = extra[j].rearrange("p (k n) -> p k n", k=KC) if j < 2 and parity else expert_slot(j)
            arrived = extra_landed[j] if j < 2 and parity else landed[j]
            b, k = nth(lambda q: last_product((f"moe{L}", 6 * q + j)), p)
            dn = USE[last_product((f"moe{L}", 12 + j))][1] - USE[last_product((f"moe{L}", 6 + j))][1]
            w = (A["w_exp_gate"], A["w_exp_up"], A["w_exp_down"])[what]
            src = w[L, bass.ds(p * 2 + j % 2, 1)].rearrange("o (k p) n -> p (o k) n", p=128)
            if isinstance(p, int):
                src = expert_weights(L, what, 2 * p + j % 2)
                sp.wait_ge(bank_full[b], USE[last_product((f"moe{L}", 6 * (p - back) + j))][1] + 1)
            else:
                sp.wait_ge(bank_full[b], k - back * dn + 1)
            sp.dma_start(dst, src).then_inc(arrived, 16)

        def expert_loads(sp, L):
            if L == 0:
                wait_full(sp, "proj", 0, 2, 0)
                sp.wait_ge(v_stored, 3 * 16)
            else:
                wait_full(sp, "proj", 1, 2, 1)
                for c in range(2):
                    sp.wait_ge(sto_stored[c], RH * 16)
            for j in range(2):
                sp.dma_start(extra[j].rearrange("p (k n) -> p k n", k=KC), expert_weights(L, 0, 2 + j)).then_inc(extra_landed[j], 16)
            with sp.Fori(0, NPAIR // 2 - 1) as i:
                for p, parity in ((i * 2 + 1, 1), (i * 2 + 2, 0)):
                    for j in range(2):
                        expert_load(sp, L, j, p + 1, 1 - parity)
                    for j in range(2, 6):
                        expert_load(sp, L, j, p)
            for j in range(2, 6):
                expert_load(sp, L, j, NPAIR - 1)

        def overflow_loads(sp, L):
            S = over[L]

            def body(n, b, e):
                for name, buf in (("gate", 0), ("up", 1), ("down", 0)):
                    src = A["w_exp_" + name][L, bass.ds(e, 1)].rearrange("o (k p) n -> p (o k) n", p=128)
                    sp.wait_ge(S["pe"], n * OV["pe"] + (3 if name == "down" else 1))
                    sp.dma_start(wover[buf].rearrange("p (k n) -> p k n", k=4 if name == "down" else KC), src).then_inc(S[name], 16)

            wait_full(sp, "gate", L, NPAIR - 1)
            with sp.If(overflow_any(sp, L)):
                overflow_loop(sp, body)

        @block.sync
        def _(sp):
            sp.dma_start(pages[0:1, :], A["page_table"].rearrange("s g -> (s g)").rearrange("(o s) -> o s", o=1)).then_inc(pages_in, 16)
            for t in range(3):
                sp.dma_start(X[0:ROWS[t], t, :], token_rows(A["x_p"], A["x_s"], t)).then_inc(x_in, 16)
            for kind, u in STREAM:
                if kind in ("moe0", "moe1"):
                    if u == 0:
                        L = int(kind[3])
                        for j in ((4, 3, 1, 2, 0, 5), (4, 5, 2, 3, 0, 1))[L]:
                            wait_let_go(sp, BEFORE[kind, j])
                            sp.dma_start(expert_slot(j), expert_weights(L, j // 2, j % 2)).then_inc(landed[j], 16)
                        expert_loads(sp, L)
                        if L == 0:
                            overflow_loads(sp, L)
                    continue
                wait_let_go(sp, BEFORE[kind, u])
                where = PLACE[kind, u]
                if kind == "cache":
                    if u == 0:
                        sp.wait_ge(pages_in, 16)
                    for g in range(2):
                        page = sp.value_load(pages[0:1, 2 * u + g:2 * u + g + 1], min_val=0, max_val=A["cache_k"].shape[1] - 1)
                        for j, cache in enumerate((A["cache_k"], A["cache_v"])):
                            src = cache[0, bass.ds(page, 1)].rearrange("o p h d -> p (o h d)")
                            sp.dma_start(slot(where)[:, (2 * j + g) * D:(2 * j + g + 1) * D], src).then_inc(landed[where], 16)
                    continue
                sp.dma_start(weights((kind, u)), unit_source(kind, u)).then_inc(landed[where], 16)
            overflow_loads(sp, 1)

        @block.gpsimd
        def _(pool):
            def ln_load(j):
                for dst, src in ((lng, A["ln_gain"]), (lnb, A["ln_bias"])):
                    pool.dma_start(dst, src[j // 2, j % 2:j % 2 + 1, :].to_broadcast([128, D])).then_inc(ln_in[j], 16)

            pool.memset(ones[:, :], 1.0).then_inc(zeroed, 1)
            pool.memset(qib, 0.0).then_inc(zeroed, 1)
            pool.memset(QB, 0.0).then_inc(zeroed, 1)
            pool.memset(epst[:, :], EPS).then_inc(zeroed, 1)
            pool.dma_start(bro[:, :], A["b_router"].rearrange("(o e) -> o e", o=1).to_broadcast([128, NE])).then_inc(bro_in, 16)
            for L in range(2):
                pool.memset(most[0:1, 2 + L:3 + L], 0).then_inc(over[L]["pe"], 1)
            pool.wait_ge(pages_in, 16)
            for s in range(NSEQ):
                for g in range(2):
                    page = pool.value_load(pages[0:1, 2 * s + g:2 * s + g + 1], min_val=0, max_val=A["cache_k"].shape[1] - 1)
                    src = A["cache_idx_k"][0, bass.ds(page, 1)].rearrange("o p d -> p (o d)")
                    pool.dma_start(ikraw[:, s, g, :], src).then_inc(ik_in, 16)
            pool.dma_start(wrt[:, :].rearrange("p (k e) -> p k e", k=KC), A["w_router"].rearrange("(k p) e -> p k e", p=128)).then_inc(router_in, 16)
            low_part(pool, 1)
            low_part(pool, 2)
            for t in range(3):
                pool.wait_ge(r_ready, 3 + t + 1)
                pool.dma_start(token_rows(O["ik_p"], O["ik_s"], t), R[0:ROWS[t], t, 0:ID]).then_inc(tile_stored[t], 16)
            for d in (3, 4, 5):
                low_part(pool, d)
            for n in (4, 5):
                if n == 5:
                    low_part(pool, 6)
                    low_part(pool, 7)
                for t in range(3):
                    pool.wait_ge(r_ready, 3 * n + t + 1)
                    pool.dma_start(token_rows(O["k_p"], O["k_s"], t)[:, (n - 4) * 512:(n - 3) * 512],
                                   R[0:ROWS[t], t, :]).then_inc(tile_stored[t], 16)
            for t in range(3):
                wait_emptied(pool, "in", 7, t)
                pool.dma_start(token_rows(O["v_p"], O["v_s"], t), V[0:ROWS[t], t, :]).then_inc(v_stored, 16)
            pool.wait_ge(relu_used, IH)
            wait_full(pool, "ikturn", NSEQ - 1)
            ln_load(0)
            pool.wait_ge(v_stored, 3 * 16)
            pool.wait_ge(x_ready, 3)
            ln_load(1)
            low_part(pool, NIN)
            pool.wait_ge(x_ready, 6)
            pool.dma_start(arena[:, 0:sum(RET_C.values())], A["c_ret"]).then_inc(ret_c_in, 16)
            pool.dma_start(gain, A["ret_norm_gain"][0].rearrange("(c p) -> p c", p=128), allow_slow_non_contiguous=True).then_inc(gain_in, 16)
            for n in range(1, 8):
                low_part(pool, NIN + n)
            for s in range(NSEQ):
                wait_emptied(pool, "update", s, 7)
                pool.dma_start(O["state_s"][s].rearrange("h (c p) n -> p (h c) n", p=128),
                               weights(("state", s))).then_inc(state_stored[s], 16)
                if s == 5:
                    low_part(pool, NIN + 8)
            for n in range(2 * RH):
                wait_emptied(pool, "rstate", n // 2, n % 2)
                pool.dma_start(O["state_p"][n // 2, (n % 2) * 128:(n % 2 + 1) * 128, :], st_out[:, n % 2, :]).then_inc(sto_stored[n % 2], 16)
            wait_emptied(pool, "inner", RH - 1)
            pool.wait_ge(kd_ready, NSEQ + 1)
            ln_load(2)
            for n in range(9, 16):
                low_part(pool, NIN + n)
            pool.wait_ge(x_ready, 9)
            ln_load(3)
            for t in range(3):
                pool.wait_ge(x_ready, 9 + t + 1)
                pool.dma_start(token_rows(O["y_p"], O["y_s"], t), X[0:ROWS[t], t, :]).then_inc(y_stored, 16)
            for t in range(3):
                pool.wait_ge(tile_stored[t], 3 * 16)
            for b in range(2):
                pool.wait_ge(sto_stored[b], RH * 16)
            for s in range(NSEQ):
                pool.wait_ge(state_stored[s], 16)
            pool.wait_ge(y_stored, 3 * 16)

        def wait_expert_landed(eng, L, j, p, parity, half):
            if j >= 2:
                eng.wait_ge(landed[j], p * 16 + LANDED[f"moe{L}", j])
            elif parity:
                eng.wait_ge(extra_landed[j], half * 16 + (NPAIR // 2 * L + 1) * 16)
            else:
                eng.wait_ge(landed[j], half * 16 + LANDED[f"moe{L}", j])

        def before_overflow(key, L):
            keys = list(USE)
            return keys.index(key) <= keys.index(("scatter", L, NPAIR - 1, 5))

        def experts_pe(pe, L, fill, full):
            def nfill(key, p):
                b, n = nth(key, p)
                pe.wait_ge(bank_free[b], n)
                return bank[b]

            def nemptied(key, p):
                b, n = nth(key, p)
                pe.wait_ge(bank_free[b], n + 1)

            if L == 0:
                pe.wait_ge(zeroed, 4)
            pe.wait_ge(chosen_ready, L + 1)
            ps = fill(("counts", L))
            pe.matmul(ps[:, 0:3 * NE], C["tri"], chosen.rearrange("p t e -> p (t e)"), start=True, stop=False)
            pe.matmul(ps[:, NE:3 * NE], ones[:, :], chosen[:, 0:2, :].rearrange("p t e -> p (t e)"), start=False, stop=False)
            pe.matmul(ps[:, 2 * NE:3 * NE], ones[:, :], chosen[:, 0, :], start=False, stop=True).then_inc(full(("counts", L)), 1)
            ps = fill(("totals", L))
            for u in range(3):
                last = pe.matmul(ps[:, 0:NE], ones[:, :], chosen[:, u, :], start=(u == 0), stop=(u == 2))
            last.then_inc(full(("totals", L)), 1)

            def gather(p, q):
                key = (lambda i: lambda x: ("gather", L, x + (0 if q is None else 1), i))
                x = p if q is None else q
                pe.wait_ge(oh_ready, p + (NPAIR * L + 1))
                for h in range(2):
                    ps = nfill(key(h), x) if q is not None else fill(("gather", L, 0, h))
                    for c in range(4):
                        for t in range(3):
                            r, d = ROWS[t], slice((4 * h + c) * 128, (4 * h + c + 1) * 128)
                            last = pe.matmul(ps[:, c * 128:(c + 1) * 128], X[0:r, t, d], OH[0:r, t].rearrange("p j s -> p (j s)"),
                                             start=(t == 0), stop=(t == 2))
                    last.then_inc(full(("gather", L, 0, h)), 1)

            def scatter(q, key_p, tiles=range(6)):
                for j in tiles:
                    b, n = nth(lambda x, j=j: ("scatter", L, key_p(x), j), q)
                    pe.wait_ge(bank_free[b], n)
                    t, h = j // 2, j % 2
                    r = ROWS[t]
                    to, half = single(OHT[:, t * 128:t * 128 + r]), slice(h * 512, (h + 1) * 512)
                    pe.matmul(bank[b][0:r, :], to, single(ys[:, half]), start=True, stop=False)
                    pe.matmul(bank[b][0:r, :], to, single(yslow[:, half]), start=False, stop=True).then_inc(bank_full[b], 1)

            def pair(p, parity, half, first=False, final=False):
                for h in range(2):
                    nemptied(lambda x, h=h: ("gather", L, x, h), p)
                for what in range(2):
                    ps = nfill(lambda x: (("gate", "up")[what], L, x), p)
                    for j in range(2):
                        wait_expert_landed(pe, L, 2 * what + j, p, parity, half)
                    for k in range(KC):
                        for j in range(2):
                            w = extra[j].rearrange("p (k n) -> p k n", k=KC) if parity and what == 0 else expert_slot(2 * what + j)
                            last = pe.matmul(ps[64 * j:64 * j + 64, :], xs[:, k, 64 * j:64 * j + 64], w[:, k, :],
                                             start=(k == 0), stop=(k == KC - 1))
                    last.then_inc(full((("gate", "up")[what], L, 0)), 1)
                if not final:
                    gather(p + 1, p)
                nemptied(lambda x: ("up", L, x), p)
                ps = nfill(lambda x: ("hturn", L, x), p)
                for m in range(4):
                    last = pe.transpose(ps[:, m * 128:(m + 1) * 128], hid[:, m * 128:(m + 1) * 128], ident)
                last.then_inc(full(("hturn", L, 0)), 1)
                if not first:
                    nemptied(lambda x: ("down", L, x - 1, 0), p)
                    nemptied(lambda x: ("down", L, x - 1, 1), p)
                    scatter(p, lambda x: x - 1, range(3))
                pe.wait_ge(g_ready, p + (NPAIR * L + 1))
                ps = nfill(lambda x: ("gturn", L, x), p)
                for t in range(3):
                    r = ROWS[t]
                    last = pe.transpose(ps[:, t * 128:t * 128 + r], G[0:r, t].rearrange("p j s -> p (j s)"), ident[0:r, 0:r])
                last.then_inc(full(("gturn", L, 0)), 1)
                if not first:
                    scatter(p, lambda x: x - 1, range(3, 6))
                nemptied(lambda x: ("hturn", L, x), p)
                for j in range(2):
                    wait_expert_landed(pe, L, 4 + j, p, parity, half)
                for h in range(2):
                    ps = nfill(lambda x, h=h: ("down", L, x, h), p)
                    for k in range(4):
                        for j in range(2):
                            last = pe.matmul(ps[64 * j:64 * j + 64, :], hT[:, k, 64 * j:64 * j + 64],
                                             expert_slot(4 + j)[:, k, h * 512:(h + 1) * 512], start=(k == 0), stop=(k == 3))
                    last.then_inc(full(("down", L, 0, h)), 1)

            gather(0, None)
            pair(0, 0, 0, first=True)
            with pe.Fori(0, NPAIR // 2 - 1) as i:
                pair(i * 2 + 1, 1, i)
                pair(i * 2 + 2, 0, i + 1)
            pair(NPAIR - 1, 1, NPAIR // 2 - 1, final=True)
            nemptied(lambda x: ("gturn", L, x), NPAIR - 1)
            for h in range(2):
                nemptied(lambda x, h=h: ("down", L, x, h), NPAIR - 1)
            scatter(NPAIR, lambda x: x - 1)

            def over_body(n, b, e):
                S = over[L]

                def wait_step(eng, k):
                    pe.wait_ge(S[eng], n * OV[eng] + k)

                wait_step("dve", 2)
                for c in range(KC):
                    for t in range(3):
                        r = ROWS[t]
                        last = pe.matmul(bank[0][:, c * 64:(c + 1) * 64], X[0:r, t, c * 128:(c + 1) * 128], OH[0:r, t, 0, :],
                                         start=(t == 0), stop=(t == 2))
                last.then_inc(S["pe"], 1)
                wait_step("act", 1)
                for what in range(2):
                    wait_step(("gate", "up")[what], 16)
                    for k in range(KC):
                        last = pe.matmul(bank[2 + what][0:64, :], xs[:, k, 0:64], wover[what].rearrange("p (k n) -> p k n", k=KC)[:, k, :],
                                         start=(k == 0), stop=(k == KC - 1))
                    last.then_inc(S["pe"], 1)
                wait_step("dve", 3)
                for m in range(4):
                    last = pe.transpose(bank[4][:, m * 128:(m + 1) * 128], hid[:, m * 128:(m + 1) * 128], ident)
                last.then_inc(S["pe"], 1)
                for t in range(3):
                    r = ROWS[t]
                    last = pe.transpose(bank[5][0:64, t * 128:t * 128 + r], G[0:r, t, 0, :], ident[0:r, 0:r])
                last.then_inc(S["pe"], 1)
                wait_step("act", 3)
                wait_step("down", 16)
                for h in range(2):
                    for k in range(4):
                        last = pe.matmul(bank[6 + h][0:64, :], hT[:, k, 0:64], wover[0].rearrange("p (k n) -> p k n", k=4)[:, k, h * 512:(h + 1) * 512],
                                         start=(k == 0), stop=(k == 3))
                    last.then_inc(S["pe"], 1)
                wait_step("act", 6)
                for j in range(6):
                    t, h = j // 2, j % 2
                    r = ROWS[t]
                    if j in (2, 3):
                        wait_step("dve", 3 + j - 1)
                    pe.matmul(bank[OVER_BANK[j]][0:r, :], GT[0:64, t * 128:t * 128 + r], ys[0:64, h * 512:(h + 1) * 512],
                              start=True, stop=True).then_inc(S["pe"], 1)

            any_over = overflow_any(pe, L)
            with pe.If(any_over):
                for b in range(8):
                    last_use = max(n for key, (bb, n) in USE.items() if bb == b and before_overflow(key, L))
                    pe.wait_ge(bank_free[b], last_use + 1)
                overflow_loop(pe, over_body)
                pe.wait_ge(over[L]["dve"], (TOK // SLOTS - 1) * NE * OV["dve"])

        @block.tensor
        def _(pe):
            def fill(key):
                b, n = USE[key]
                if n:
                    pe.wait_ge(bank_free[b], n)
                return bank[b]

            def full(key):
                return bank_full[USE[key][0]]

            def turn(name, count, then=None):
                for t in range(3):
                    if count is not None:
                        pe.wait_ge(x_ready, count + t + 1)
                    r = ROWS[t]
                    for h in range(2):
                        ps = fill((name, t, h))
                        for c in range(4):
                            last = pe.transpose(ps[:, c * 128:c * 128 + r], X[0:r, t, (4 * h + c) * 128:(4 * h + c + 1) * 128],
                                                ident[0:r, 0:r])
                        last.then_inc(full((name, t, h)), 1)
                    if then and t:
                        then(t - 1)
                if then:
                    then(2)

            def route(L):
                def tile(t):
                    for h in range(2):
                        wait_emptied(pe, f"x{2 * L + 1}", t, h)
                    if L == t == 0:
                        pe.wait_ge(router_in, 16)
                    r = ROWS[t]
                    ps = fill(("router", L))
                    for k in range(KC):
                        last = pe.matmul(ps[0:r, t * NE:(t + 1) * NE], XT[:, k, t * 128:t * 128 + r], wrt[:, k * NE:(k + 1) * NE],
                                         start=(k == 0), stop=(k == KC - 1))
                    if t == 2:
                        last.then_inc(full(("router", L)), 1)
                return tile

            def project(ps, t, x, w, width=512, start=True, stop=True, halfway=None):
                r = ROWS[t]
                for k in range(KC):
                    if k == KC // 2 and halfway:
                        halfway()
                    if len(w) == 1:
                        pairs = [(0, 0)]
                    else:
                        pairs = [(0, 0), (0, 1), (1, 0)] if t < 2 else [(1, 0), (1, 1)]
                    for i, (a, c) in enumerate(pairs):
                        at = dict(start=(start and k == i == 0), stop=(stop and k == KC - 1 and i == len(pairs) - 1))
                        if t < 2 or len(w) == 2:
                            last = pe.matmul(ps[:, 0:width], x(t, a, k), w[c][:, k, 0:width], **at)
                        else:
                            for j in range(2):
                                last = pe.matmul(ps[64 * j:64 * j + 64, 0:256], x(t, a, k), w[c][:, k, 256 * j:256 * j + 256], **at)
                return last

            def parts(key):
                return [rounded(key), single(weights(key))]

            def x_parts(t, part, k):
                return single((XT, XLOW)[part][:, k, t * 128:t * 128 + 128])

            def index_step(k):
                if k < NSEQ:
                    ps = fill(("ikturn", k))
                    pe.wait_ge(ik_in, 2 * NSEQ * 16)
                    for g in range(2):
                        last = pe.transpose(ps[0:64, g * 128:(g + 1) * 128], ikraw[:, k, g, :], ident)
                    last.then_inc(full(("ikturn", k)), 1)
                if 0 < k <= NSEQ:
                    s = k - 1
                    ps = fill(("sindex", s))
                    wait_emptied(pe, "ikturn", s)
                    pe.wait_ge(qib_ready, s + 1)
                    for c in range(4):
                        last = pe.matmul(ps[0:64, 0:KEYS], qib[:, s % 2, c, :], kiS[:, s % 2, :], start=(c == 0), stop=(c == 3))
                    last.then_inc(full(("sindex", s)), 1)
                if k > 1:
                    s = k - 2
                    score = fill(("sscore",))
                    wait_emptied(pe, "wspread")
                    wait_emptied(pe, "sindex", s)
                    last = pe.matmul(score[0:64, 0:KEYS], WP[0:64, s, :], reluS[0:64, s % 2, :], start=(s == 0), stop=(s == NSEQ - 1))
                    if s == NSEQ - 1:
                        last.then_inc(full(("sscore",)), 1)

            pe.wait_ge(com_in, 16)
            pe.wait_ge(x_in, 48)
            turn("x0", None)
            for n in range(8):
                key = PARTED[n]
                if n:
                    pe.wait_ge(low_ready, n)
                for t in range(3):
                    halfway = None
                    if n == 0:
                        wait_emptied(pe, "x0", t, 1)
                        wait_emptied(pe, "x0", t, 0)
                        if t == 0:
                            pe.wait_ge(first_low_ready, 1)
                            halfway = lambda: pe.wait_ge(first_low_ready, 2)
                    project(fill(("in", n, t)), t, x_parts, parts(key), width_of(key), halfway=halfway).then_inc(full(("in", n, t)), 1)
                    if 0 < n <= 6:
                        pe.wait_ge(r_ready, 3 * (n - 1) + t + 1)
                        ps = fill(("inturn", n - 1, t))
                        r = ROWS[t]
                        for c in range(1 if n - 1 == 1 else 4):
                            last = pe.transpose(ps[:, c * 128:c * 128 + r], R[0:r, t, c * 128:(c + 1) * 128], ident[0:r, 0:r])
                        last.then_inc(full(("inturn", n - 1, t)), 1)
                    if n >= 5:
                        index_step(3 * (n - 5) + t)
                if n == 2:
                    ps = fill(("wturn",))
                    pe.transpose(ps[0:IH, 0:64], wi[0:64, 2, :], ident[0:64, 0:64]).then_inc(full(("wturn",)), 1)
                    wait_emptied(pe, "wturn")
                    pe.wait_ge(attn_c_in, 16)
                    ps = fill(("wspread",))
                    pe.matmul(ps[0:64, 0:64], AC["hrep"][0:IH, :], wiT[0:IH, :], start=True, stop=True).then_inc(full(("wspread",)), 1)
                if n == 3:
                    for t in range(2):
                        wait_emptied(pe, "inturn", 0, t)
                        wait_emptied(pe, "inturn", 1, t)
                    for qt in range(2):
                        nk = 128 * (qt + 1)
                        for cc in range(2):
                            for par in range(2):
                                key = ("index", qt, cc, par)
                                ps = fill(key)
                                o = 64 * par
                                for j in range(2):
                                    last = pe.matmul(ps[:, j * nk:(j + 1) * nk], qiT[o:o + 64, 2 * cc + j, qt * 128:(qt + 1) * 128],
                                                     kiT[o:o + 64, 0:nk], start=True, stop=True)
                                last.then_inc(full(key), 1)
            index_step(NSEQ + 1)

            def scores(n):
                qt, cc, par = n // 8, n // 2 % 4, n % 2
                nk, o = 128 * (qt + 1), 64 * (n % 2)
                ps = fill(("attn", qt, cc, par))
                for j in range(2):
                    last = pe.matmul(ps[:, j * nk:(j + 1) * nk], qT[o:o + 64, 2 * cc + j, qt * 128:(qt + 1) * 128],
                                     kT[o:o + 64, 2 * cc + j, 0:nk], start=True, stop=True)
                last.then_inc(full(("attn", qt, cc, par)), 1)

            for t in range(2):
                for i in (2, 3, 4, 5):
                    wait_emptied(pe, "inturn", i, t)
                for i in (6, 7):
                    wait_emptied(pe, "in", i, t)
            scores(0)
            scores(1)
            scores(2)
            for n in range(16):
                qt, cc, par = n // 8, n // 2 % 4, n % 2
                pe.wait_ge(p_ready, n + 1)
                ps = fill(("pturn", n))
                for i in range(2 * (qt + 1)):
                    last = pe.transpose(ps[:, i * 128:(i + 1) * 128], P[:, n % 3, i * 128:(i + 1) * 128], ident)
                last.then_inc(full(("pturn", n)), 1)
                if n + 3 < 16:
                    scores(n + 3)
                ps = fill(("pv", n))
                wait_emptied(pe, "pturn", n)
                for j in range(2):
                    head = 2 * (2 * cc + j) + par
                    for g in range(qt + 1):
                        i = j * (qt + 1) + g
                        last = pe.matmul(ps[64 * par:64 * par + 64, j * 128:(j + 1) * 128], V[:, g, head * 64:(head + 1) * 64],
                                         PT[:, n % 2, i * 128:(i + 1) * 128], start=(g == 0), stop=(g == qt))
                last.then_inc(full(("pv", n)), 1)

            def turn_back(s):
                pe.wait_ge(o2_s, s + 1)
                ps = fill(("oturn_s", s))
                pe.transpose(ps[0:64, 0:128], O2, ident).then_inc(full(("oturn_s", s)), 1)

            for s in range(NSEQ + 1):
                if s < NSEQ:
                    wait_landed(pe, ("cache", s))
                    raw = slot(PLACE["cache", s])
                    for j in range(4):
                        ps = fill(("kturn", s, j))
                        for i in range(4):
                            c, g = 2 * j + i // 2, i % 2
                            last = pe.transpose(ps[:, i * 128:(i + 1) * 128], raw[:, g * D + c * 128:g * D + (c + 1) * 128], ident)
                        last.then_inc(full(("kturn", s, j)), 1)
                if s >= 2:
                    turn_back(s - 2)
                b = s - 1
                if 0 <= b < NSEQ:
                    pe.wait_ge(p_s, b + 1)
                    ps = fill(("pturn_s", b))
                    for g in range(2):
                        pe.transpose(ps[:, g * 128:(g + 1) * 128], P[:, b % 2, g * 128:(g + 1) * 128], ident)
                    pe.transpose(ps[0:64, 256:384], P[:, b % 2, 256:KEYS], ident).then_inc(full(("pturn_s", b)), 1)
                if s < NSEQ:
                    ps = fill(("sattn", s))
                    if s == 0:
                        pe.wait_ge(new_kt, 1)
                    for j in range(4):
                        wait_emptied(pe, "kturn", s, j)
                    pe.wait_ge(qb_ready, s + 1)
                    for c in range(KC):
                        pe.matmul(ps[:, 0:KEYS], QB[:, c, :], KT[:, c, :], start=(c == 0), stop=False)
                    pe.matmul(ps[:, 0:KEYS], rept[0:64, s % 2, :], bias_s[0:64, :], start=False, stop=True).then_inc(full(("sattn", s)), 1)
                if 0 <= b < NSEQ:
                    raw = slot(PLACE["cache", b])
                    ps = fill(("pv_s", b))
                    wait_emptied(pe, "pturn_s", b)
                    if b == 0:
                        for i in (6, 7):
                            wait_emptied(pe, "in", i, 2)
                    for g in range(3):
                        for q in range(4):
                            r = 128 if g < 2 else 64
                            val = raw[:, (2 + g) * D + q * 256:(2 + g) * D + (q + 1) * 256] if g < 2 else V[0:64, 2, q * 256:(q + 1) * 256]
                            last = pe.matmul(ps[32 * q:32 * q + 32, 0:256], PT[0:r, b % 2, g * 128 + 32 * q:g * 128 + 32 * q + 32], val,
                                             start=(g == 0), stop=(g == 2))
                    last.then_inc(full(("pv_s", b)), 1)

            wait_emptied(pe, "pv", 14)
            wait_emptied(pe, "pv", 15)
            for u in range(2):
                wait_landed(pe, ("out", u))
                for t in range(3):
                    if u == 0 and t == 1:
                        turn_back(NSEQ - 1)
                    if u == 0 and t == 2:
                        wait_emptied(pe, "oturn_s", NSEQ - 1)
                    project(fill(("proj", 0, t, u)), t, lambda t, _, k: oT[:, k, t * 128:t * 128 + ROWS[t]], [weights(("out", u))]).then_inc(full(("proj", 0, t, u)), 1)
            turn("x1", 0, route(0))
            experts_pe(pe, 0, fill, full)
            turn("x2", 3)

            for n in range(8):
                pe.wait_ge(low_ready, NIN + n)
                for t in range(3):
                    if n == 0:
                        wait_emptied(pe, "x2", t, 0)
                        wait_emptied(pe, "x2", t, 1)
                    project(fill(("rin", n, t)), t, x_parts, parts(("rin", n))).then_inc(full(("rin", n, t)), 1)
                    if 0 < n <= 4:
                        i = n - 1
                        src = RR[:, (3 * i + t) % 2, :] if i < 2 else kt[:, t, 2 * (i - 2):2 * (i - 2) + 2].rearrange("p h d -> p (h d)")
                        pe.wait_ge(rk_ready, 3 * i + t + 1)
                        ps = fill(("rturn", i, t))
                        r = ROWS[t]
                        for c in range(4):
                            last = pe.transpose(ps[:, c * 128:c * 128 + r], src[0:r, c * 128:(c + 1) * 128], ident[0:r, 0:r])
                        last.then_inc(full(("rturn", i, t)), 1)

            for t in range(3):
                for n in range(4):
                    wait_emptied(pe, "rturn", n, t)
                for n in range(4, 8):
                    wait_emptied(pe, "rin", n, t)
            ps = fill(("sinner",))
            for h in range(RH):
                for c in range(2):
                    last = pe.matmul(ps[0:64, h * 64:(h + 1) * 64], rkT[:, 2 * h + c, PROMPT:TOK], rqT[:, 2 * h + c, PROMPT:TOK],
                                     start=(c == 0), stop=(c == 1))
            last.then_inc(full(("sinner",)), 1)
            wait_emptied(pe, "sinner")
            pe.wait_ge(qm_ready, 1)
            so = [fill(("so", g)) for g in range(2)]
            for s in range(NSEQ):
                g = s // 4
                if s % 4 == 0:
                    for h in range(RH):
                        pe.matmul(so[g][32 * h:32 * h + 32, :], innS[0:64, h, 32 * g:32 * g + 32], v[0:64, 2, h, :], start=True, stop=False)
                wait_landed(pe, ("state", s))
                st = weights(("state", s))
                for c in range(2):
                    for h in range(RH):
                        last = pe.matmul(so[g][32 * h:32 * h + 32, :], QM[:, 2 * h + c, s, :], st[:, 2 * h + c, :],
                                         start=False, stop=(s % 4 == 3 and c == 1))
                if s % 4 == 3:
                    last.then_inc(full(("so", g)), 1)
                pe.wait_ge(kd_ready, s + 2)
                for j in range(8):
                    h, c = j // 2, j % 2
                    ps = fill(("update", s, j))
                    pe.matmul(ps[:, :], kd[0:64, h, c * 128:(c + 1) * 128], v[0:64, 2, h, :],
                              start=True, stop=True).then_inc(full(("update", s, j)), 1)

            for h in range(RH):
                ps = fill(("inner", h))
                for c in range(2):
                    pe.matmul(ps[:, 0:256], rkT[:, 2 * h + c, 0:128], rqT[:, 2 * h + c, 0:256], start=(c == 0), stop=(c == 1))
                for c in range(2):
                    last = pe.matmul(ps[:, 256:384], rkT[:, 2 * h + c, 128:256], rqT[:, 2 * h + c, 128:256], start=(c == 0), stop=(c == 1))
                last.then_inc(full(("inner", h)), 1)
                if h == 0:
                    pe.wait_ge(kd_ready, 1)
                for c in range(2):
                    ps = fill(("rstate", h, c))
                    for t in range(2):
                        last = pe.matmul(ps[:, :], kt[:, t, h, c * 128:(c + 1) * 128], v[:, t, h, :], start=(t == 0), stop=(t == 1))
                    last.then_inc(full(("rstate", h, c)), 1)
                wait_emptied(pe, "inner", h)
                ps = fill(("ro", h, 0))
                pe.matmul(ps[:, :], inn[:, 0:128], v[:, 0, h, :], start=True, stop=True).then_inc(full(("ro", h, 0)), 1)
                ps = fill(("ro", h, 1))
                pe.matmul(ps[:, :], inn[:, 128:256], v[:, 0, h, :], start=True, stop=False)
                pe.matmul(ps[:, :], inn[:, 256:384], v[:, 1, h, :], start=False, stop=True).then_inc(full(("ro", h, 1)), 1)
            def turn_o(n, t):
                pe.wait_ge(go_ready, 3 * n + t + 1)
                ps = fill(("oturn", n, t))
                r = ROWS[t]
                for c in range(4):
                    last = pe.transpose(ps[:, c * 128:c * 128 + r], v[0:r, t, n, c * 128:(c + 1) * 128], ident[0:r, 0:r])
                last.then_inc(full(("oturn", n, t)), 1)

            for n in range(4):
                pe.wait_ge(low_ready, NIN + 8 + n)
                for t in range(3):
                    project(fill(("rin", 8 + n, t)), t, x_parts, parts(("rin", 8 + n))).then_inc(full(("rin", 8 + n, t)), 1)
                    if n:
                        turn_o(n - 1, t)
            for u in range(2):
                banks = [fill(("proj", 1, t, u)) for t in range(3)]
                for kh in range(2):
                    if u == 0 and kh == 1:
                        for t in range(3):
                            turn_o(3, t)
                    pe.wait_ge(low_ready, NIN + 12 + 2 * u + kh)
                    pe.wait_ge(ro_ready, 6 * (kh + 1))

                    def gated(t, part, k):
                        c = KC * kh + k
                        return single((rlow[c // 4][:, c % 4, :] if part else roT[:, c, :])[:, t * 128:t * 128 + 128])

                    for t in range(3):
                        last = project(banks[t], t, gated, parts(("rout", 2 * u + kh)), start=(kh == 0), stop=(kh == 1))
                        if kh:
                            last.then_inc(full(("proj", 1, t, u)), 1)
                        elif t == 2:
                            last.then_inc(rout_used, 1)
            turn("x3", 6, route(1))
            experts_pe(pe, 1, fill, full)

        def norm_act(act, j):
            for t in range(3):
                act.wait_ge(var_ready, 3 * j + t + 1)
                r = ROWS[t]
                act.activation(sv[0:r, t, 0:1], mv[0:r, t, 1:2], ACT.Sqrt, bias=epst[0:r, 0:1]).then_inc(std_ready, 1)

        def experts_act(act, L):
            def nth_full(key, p):
                b, n = nth(key, p)
                act.wait_ge(bank_full[b], n + 1)
                return bank[b], bank_free[b]

            act.wait_ge(logit_max, L + 1)
            act.activation(rt[0], rt[0], ACT.Exp).then_inc(logit_exp, 1)
            act.wait_ge(x_ready, 6 * L + 3)
            for t in range(3):
                act.activation(Y[0:ROWS[t], t, :], X[0:ROWS[t], t, :], ACT.Copy, scale=ALPHA).then_inc(y_begun, 1)

            def columns_in(key, p):
                ps, free = nth_full(key, p)
                act.activation(xs[:, 4:8, :], ps[:, :].rearrange("p (c s) -> p c s", c=4), ACT.Copy).then_inc(free, 1)

            def pair(p, final=False):
                ps, free = nth_full(lambda x: ("gate", L, x), p)
                if not (isinstance(p, int) and p == 0):
                    b, n = nth(lambda x: ("up", L, x), p)
                    act.wait_ge(bank_free[b], n)
                act.activation(sil, ps[:, :], ACT.Silu).then_inc(free, 1)
                if not final:
                    columns_in(lambda x: ("gather", L, x + 1, 1), p)
                ps, free = nth_full(lambda x: ("hturn", L, x), p)
                act.activation(hT, ps[:, :].rearrange("p (m s) -> p m s", m=4), ACT.Copy).then_inc(free, 1)
                ps, free = nth_full(lambda x: ("gturn", L, x), p)
                if not (isinstance(p, int) and p == 0 and L == 0):
                    act.wait_ge(oht_ready, p + NPAIR * L)
                act.activation(GT[:, :], ps[:, 0:TOK], ACT.Copy, accum_out=gs).then_inc(free, 1)
                b, n = nth(lambda x: ("gturn", L, x), p)
                act.wait_ge(bank_free[b], n + 1)
                for h in range(2):
                    ps, free = nth_full(lambda x, h=h: ("down", L, x, h), p)
                    act.activation(single(ys[:, h * 512:(h + 1) * 512]), ps[:, :], ACT.Identity, scale=gs).then_inc(ys_high, 1)

            columns_in(lambda x: ("gather", L, x, 1), 0)
            pair(0)
            with act.Fori(1, NPAIR - 1) as p:
                pair(p)
            pair(NPAIR - 1, final=True)

            S = over[L]

            def over_body(n, b, e):
                moves = [(1, lambda: act.activation(xs[:, :, 0:64], bank[0][:, :].rearrange("p (c s) -> p c s", c=KC), ACT.Copy)),
                         (2, lambda: act.activation(sil[0:64, :], bank[2][0:64, :], ACT.Silu)),
                         (4, lambda: act.activation(hT[:, :, 0:64], bank[4][:, :].rearrange("p (m s) -> p m s", m=4)[:, :, 0:64], ACT.Copy)),
                         (5, lambda: act.activation(GT[0:64, :], bank[5][0:64, 0:TOK], ACT.Copy)),
                         (6, lambda: act.activation(ys[0:64, 0:512], bank[6][0:64, :], ACT.Copy)),
                         (7, lambda: act.activation(ys[0:64, 512:1024], bank[7][0:64, :], ACT.Copy))]
                for k, move in moves:
                    act.wait_ge(S["pe"], n * OV["pe"] + k + 1)
                    move().then_inc(S["act"], 1)

            with act.If(overflow_any(act, L)):
                overflow_loop(act, over_body)

        @block.scalar
        def _(act):
            step = Chain(act, act_step)

            def copy(out, in_):
                return act.activation(out, in_, ACT.Copy)

            def turned(name):
                for t in range(3):
                    for h in range(2):
                        ps = wait_full(act, name, t, h)
                        r = ROWS[t]
                        parted = name in ("x0", "x2")
                        out = (XLOW if parted and t == 2 else XT)[:, 4 * h:4 * h + 4, t * 128:t * 128 + r]
                        copy(single(out) if parted else out, ps[:, :].rearrange("p (c t) -> p c t", c=4)[:, :, 0:r])\
                            .then_inc(x_high if parted else freed((name, t, h)), 1)

            def staged(key, t, out, func=ACT.Copy, width=512):
                ps = wait_full(act, *key)
                if t < 2:
                    act.activation(out[:, 0:width], ps[:, 0:width], func).then_inc(freed(key), 1)
                    return
                copy(out[0:64, 0:width], ps[0:64, 0:width]).then_inc(half_ready, 1)
                if func != ACT.Copy:
                    wait_emptied(act, *key)
                    act.activation(out[0:64, 0:width], out[0:64, 0:width], func).then_inc(silu_ready, 1)

            def index_step(k):
                if k == 0:
                    wait_emptied(act, "inturn", 1, 2)
                    for b in range(2):
                        step(copy(kiS[:, b, PAST:KEYS], kiT[:, PROMPT:TOK]))
                if k < NSEQ:
                    ps = wait_full(act, "ikturn", k)
                    copy(kiS[0:64, k % 2, 0:PAST], ps[0:64, 0:PAST])
                    copy(kiS[64:128, k % 2, 0:PAST], ps[0:64, 0:PAST]).then_inc(freed(("ikturn", k)), 1)
                if 0 < k <= NSEQ:
                    s = k - 1
                    ps = wait_full(act, "sindex", s)
                    act.activation(reluS[0:64, s % 2, :], ps[0:64, 0:KEYS], ACT.Relu, scale=ID ** -0.5).then_inc(freed(("sindex", s)), 1)

            act.dma_start(com[:, :], A["c_common"]).then_inc(com_in, 16)
            act.dma_start(arena[:, 2 * D:2 * D + sum(ATTN_C.values())], A["c_attn"]).then_inc(attn_c_in, 16)
            turned("x0")
            high_part(act, 0)
            high_part(act, 1)
            high_part(act, 2)
            for n in range(8):
                if n == 1:
                    high_part(act, 3)
                elif 3 <= n < 7:
                    high_part(act, n + 1)
                for t in range(3):
                    k = 3 * n + t
                    if n < 6:
                        if k >= 2:
                            act.wait_ge(e_used, k - 1)
                        staged(("in", n, t), t, E[:, k % 2, :], width=W_KW if n == 1 else 512)
                    else:
                        staged(("in", n, t), t, V[:, t, (n - 6) * 512:(n - 5) * 512])
                    if 0 < n <= 6:
                        i, r = n - 1, ROWS[t]
                        ps = wait_full(act, "inturn", i, t)
                        view = ps[:, :].rearrange("p (c t) -> p c t", c=4)[:, :, 0:r]
                        dst = {0: qiT[:, 0:4], 2: qT[:, 0:4], 3: qT[:, 4:8], 4: kT[:, 0:4], 5: kT[:, 4:8]}.get(i)
                        if i == 1:
                            copy(kiT[:, t * 128:t * 128 + r], ps[:, 0:r]).then_inc(freed(("inturn", i, t)), 1)
                        else:
                            copy(dst[:, :, t * 128:t * 128 + r], view).then_inc(freed(("inturn", i, t)), 1)
                    if n >= 5:
                        index_step(k - 15)
                if n == 2:
                    ps = wait_full(act, "wturn")
                    copy(wiT[0:IH, :], ps[0:IH, 0:64]).then_inc(freed(("wturn",)), 1)
                if n == 3:
                    m = 0
                    for qt in range(2):
                        nk = 128 * (qt + 1)
                        for cc in range(2):
                            for par in range(2):
                                ps = wait_full(act, "index", qt, cc, par)
                                if m >= 2:
                                    act.wait_ge(relu_used, m - 1)
                                act.activation(relu[:, m % 2, 0:2 * nk], ps[:, 0:2 * nk], ACT.Relu, scale=ID ** -0.5)\
                                   .then_inc(freed(("index", qt, cc, par)), 1)
                                m += 1
            index_step(NSEQ + 1)

            for n in range(16 + 2):
                m = n - 2
                if m >= 0:
                    w = 256 * (m // 8 + 1)
                    ps = wait_full(act, "pturn", m)
                    copy(PT[:, m % 2, 0:w], ps[:, 0:w]).then_inc(freed(("pturn", m)), 1)
                if n < 16:
                    nk = 128 * (n // 8 + 1)
                    act.wait_ge(max_ready, n + 1)
                    c = 16 + 8 * (n % 3)
                    for j in range(2):
                        last = act.activation(P[:, n % 3, j * nk:(j + 1) * nk], P[:, n % 3, j * nk:(j + 1) * nk], ACT.Exp,
                                              bias=small[:, c + 2 + j:c + 3 + j], scale=HD ** -0.5, accum_out=small[:, c + 4 + j:c + 5 + j])
                    last.then_inc(exp_ready, 1)
                if m >= 0:
                    qt, cc, par = m // 8, m // 2 % 4, m % 2
                    o = 64 * (m % 2)
                    ps = wait_full(act, "pv", m)
                    copy(oT[o:o + 64, 2 * cc:2 * cc + 2, qt * 128:(qt + 1) * 128],
                         ps[o:o + 64, 0:256].rearrange("p (c t) -> p c t", c=2)).then_inc(freed(("pv", m)), 1)
            for s in range(NSEQ + 1):
                if s < NSEQ:
                    if s == 0:
                        for t in range(3):
                            act.wait_ge(tile_stored[t], 3 * 16)
                    for j in range(2):
                        ps = wait_full(act, "kturn", s, j)
                        copy(KT[:, 2 * j:2 * j + 2, 0:PAST], ps[:, :].rearrange("p (c k) -> p c k", c=2)).then_inc(freed(("kturn", s, j)), 1)
                if s:
                    b = s - 1
                    ps = wait_full(act, "pturn_s", b)
                    copy(PT[:, b % 2, 0:256], ps[:, 0:256])
                    copy(PT[0:64, b % 2, 256:384], ps[0:64, 256:384]).then_inc(freed(("pturn_s", b)), 1)
                if s < NSEQ:
                    ps = wait_full(act, "sattn", s)
                    act.wait_ge(max_s, s + 1)
                    c = 4 * (s % 2)
                    act.activation(P[:, s % 2, 0:KEYS], ps[:, 0:KEYS], ACT.Exp, bias=small[:, c + 1:c + 2], scale=HD ** -0.5,
                                   accum_out=small[:, c + 2:c + 3]).then_inc(freed(("sattn", s)), 1)
            norm_act(act, 0)
            turned("x1")
            experts_act(act, 0)
            high_part(act, NIN)
            norm_act(act, 1)
            turned("x2")
            for n in range(8):
                if n < 7:
                    high_part(act, NIN + n + 1)
                for t in range(3):
                    k = 3 * n + t
                    if n < 4:
                        if k >= 2:
                            act.wait_ge(re_used, k - 1)
                        staged(("rin", n, t), t, RE[:, k % 2, :])
                    else:
                        staged(("rin", n, t), t, v[:, t, n - 4, :])
                    if 0 < n <= 4:
                        i, r = n - 1, ROWS[t]
                        ps = wait_full(act, "rturn", i, t)
                        dst = (rqT if i < 2 else rkT)[:, 4 * (i % 2):4 * (i % 2) + 4, t * 128:t * 128 + r]
                        copy(dst, ps[:, :].rearrange("p (c t) -> p c t", c=4)[:, :, 0:r]).then_inc(freed(("rturn", i, t)), 1)
            high_part(act, NIN + 8)
            for g in range(2):
                act.wait_ge(rvar, g + 1)
                act.activation(rst[:, 2, 14:15], rst[:, 2, 13:14], ACT.Sqrt, bias=epst[:, 0:1]).then_inc(rstd, 1)
                act.wait_ge(rnmr, g + 1)
                for h in range(RH):
                    ps = bank[USE["so", g][0]]
                    o = 32 * h
                    last = act.activation(v[32 * g:32 * g + 32, 2, h, :], ps[o:o + 32, :], ACT.Identity,
                                          bias=rst[o:o + 32, 2, 16:17], scale=rst[o:o + 32, 2, 15:16])
                last.then_inc(freed(("so", g)), 1)
            for h in range(RH):
                for c in range(2):
                    ps = wait_full(act, "rstate", h, c)
                    if h:
                        act.wait_ge(sto_stored[c], 16 * h)
                    copy(st_out[:, c, :], ps[:, :]).then_inc(freed(("rstate", h, c)), 1)
                act.wait_ge(rvar, 2 + h + 1)
                act.activation(rst[:, 0:2, 14:15], rst[:, 0:2, 13:14], ACT.Sqrt, bias=epst[:, 0:1]).then_inc(rstd, 1)
                act.wait_ge(rnmr, 2 + h + 1)
                for t in range(2):
                    ps = wait_full(act, "ro", h, t)
                    act.activation(v[:, t, h, :], ps[:, :], ACT.Identity, bias=rst[:, t, 16:17], scale=rst[:, t, 15:16])\
                       .then_inc(freed(("ro", h, t)), 1)
            def round_gated(n, t):
                wait_emptied(act, "oturn", n, t)
                cols, high = gated_places(n, t)
                copy(single(high), rlow[n][:, :, cols]).then_inc(ro_high, 1)

            for n in range(4):
                high_part(act, NIN + 9 + n)
                for t in range(3):
                    k = 3 * n + t
                    if k >= 2:
                        act.wait_ge(go_ready, k - 1)
                    staged(("rin", 8 + n, t), t, RE[:, k % 2, :], func=ACT.Silu)
                    if n:
                        round_gated(n - 1, t)
            high_part(act, NIN + 13)
            for t in range(3):
                round_gated(3, t)
            for n in (14, 15):
                high_part(act, NIN + n)
            norm_act(act, 2)
            turned("x3")
            experts_act(act, 1)
            norm_act(act, 3)

        def bass_step(a, start, count, stride, width):
            part, _ = a.ap[0], a.ap[1]
            return bass.AP(a.tensor, a.offset + start, [list(part), [stride, count], [1, width]])

        def experts_dve(dve, L, step):
            def nth_full(key, p):
                b, n = nth(key, p)
                dve.wait_ge(bank_full[b], n + 1)
                return bank[b], bank_free[b]

            def flat(a):
                return a.rearrange("p (t e) -> p t e", t=3)

            def over16(a, width=NE):
                return a.unsqueeze(2).to_broadcast([128, 3, width])

            def first_max(values, weights_, width, out, tmp, top, mark):
                step(dve.tensor_reduce(top, values, AX, ALU.max))
                step(dve.tensor_tensor(tmp, values, over16(top, width), ALU.is_equal))
                step(dve.tensor_tensor(tmp, tmp, weights_.unsqueeze(1).to_broadcast([128, 3, width]), ALU.mult))
                step(dve.tensor_reduce(mark, tmp, AX, ALU.max))
                step(dve.tensor_tensor(out, tmp, over16(mark, width), ALU.is_equal))

            e3, sel3, tmp3, pick3 = flat(rt[0]), flat(rt[1]), flat(rt[2]), flat(rt[3])
            four = [rt[4][:, 12 * i:12 * i + 12].rearrange("p (t g) -> p t g", t=3) for i in range(4)]
            four += [rt[5][:, 12 * i:12 * i + 12].rearrange("p (t g) -> p t g", t=3) for i in range(4)]
            hi = rt[6][:, 0:24].rearrange("p (t g u) -> p t g u", t=3, u=2)
            lo = rt[6][:, 24:48].rearrange("p (t g u) -> p t g u", t=3, u=2)
            one = [rt[7][:, 3 * i:3 * i + 3] for i in range(8)]
            step(dve.memset(rt[0], 0.0))
            ps = wait_full(dve, "router", L)
            dve.tensor_copy(e3[:, 0:2, :], ps[:, 0:2 * NE].rearrange("p (t e) -> p t e", t=2))
            dve.tensor_copy(e3[0:64, 2, :], ps[0:64, 2 * NE:3 * NE]).then_inc(freed(("router", L)), 1)
            wait_emptied(dve, "router", L)
            step(dve.tensor_reduce(one[0], e3, AX, ALU.max))
            dve.tensor_tensor(e3, e3, over16(one[0]), ALU.subtract).then_inc(logit_max, 1)
            dve.wait_ge(logit_exp, L + 1)
            step(dve.tensor_reduce(one[1], e3, AX, ALU.add))
            step(dve.reciprocal(one[2], one[1]))
            step(dve.tensor_tensor(e3, e3, over16(one[2]), ALU.mult))
            dve.wait_ge(bro_in, 16)
            step(dve.tensor_tensor(sel3, e3, bro[:, :].unsqueeze(1).to_broadcast([128, 3, NE]), ALU.add))
            s5 = rt[1].rearrange("p (t g u v) -> p t g u v", t=3, g=NGRP, u=2)
            for t in range(3):
                dve.tensor_tensor(hi[:, t], s5[:, t, :, :, 0], s5[:, t, :, :, 1], ALU.max)
                last = dve.tensor_tensor(lo[:, t], s5[:, t, :, :, 0], s5[:, t, :, :, 1], ALU.min)
            step(last)
            dve.tensor_tensor(four[0], hi[:, :, :, 0], hi[:, :, :, 1], ALU.max)
            dve.tensor_tensor(four[1], hi[:, :, :, 0], hi[:, :, :, 1], ALU.min)
            step(dve.tensor_tensor(four[2], lo[:, :, :, 0], lo[:, :, :, 1], ALU.max))
            step(dve.tensor_tensor(four[3], four[1], four[2], ALU.max))
            step(dve.tensor_tensor(four[4], four[0], four[3], ALU.add))
            first_max(four[4], C["first4"], NGRP, four[5], four[6], one[3], one[4])
            step(dve.tensor_scalar(four[7], four[5], 1.0, BIG, ALU.subtract, ALU.mult))
            a = rt[1].rearrange("p (x u) -> p x u", u=EPG)
            b = rt[2].rearrange("p (x u) -> p x u", u=EPG)
            groups = [rt[5][:, 12 * i:12 * i + 12].unsqueeze(2).to_broadcast([128, 3 * NGRP, EPG]) for i in (1, 3)]
            step(dve.tensor_tensor(b, a, groups[0], ALU.mult))
            step(dve.tensor_tensor(a, b, groups[1], ALU.add))
            top8 = rt[3][:, 0:24].rearrange("p (t j) -> p t j", t=3)
            for t in range(3):
                last = dve.max(top8[:, t, :], sel3[:, t, :])
            step(last)
            step(dve.memset(top8[:, :, 2:8], TAKEN))
            for t in range(3):
                last = dve.match_replace(sel3[:, t, :], top8[:, t, :], sel3[:, t, :], TAKEN)
            step(last)
            step(dve.tensor_scalar(chosen, sel3, TAKEN, None, ALU.is_equal))
            step(dve.tensor_tensor(gatev, e3, chosen, ALU.mult))
            dve.tensor_tensor(chosen, chosen, over16(C["valid"]), ALU.mult).then_inc(chosen_ready, 1)
            step(dve.tensor_reduce(one[1], gatev, AX, ALU.add))
            step(dve.reciprocal(one[2], one[1]))
            step(dve.tensor_tensor(gatev, gatev, over16(one[2]), ALU.mult))
            ps = wait_full(dve, "counts", L)
            dve.wait_ge(chosen_ready, L + 1)
            dve.scalar_tensor_tensor(out=place, in0=ps[:, 0:3 * NE].rearrange("p (t e) -> p t e", t=3), scalar=1.0, in1=chosen,
                                     op0=ALU.add, op1=ALU.mult).then_inc(freed(("counts", L)), 1)
            wait_emptied(dve, "counts", L)
            step(dve.tensor_scalar(place, place, 1.0, None, ALU.subtract))

            iota = C["iota"]

            def onehots(p):
                for t in range(3):
                    last = dve.tensor_tensor(OH[:, t], iota[:, 0:SLOTS].unsqueeze(1).to_broadcast([128, 2, SLOTS]),
                                             place[:, t, pair_of(p)].unsqueeze(2).to_broadcast([128, 2, SLOTS]), ALU.is_equal)
                last.then_inc(oh_ready, 1)

            def gates(p):
                for t in range(3):
                    last = dve.tensor_tensor(G[:, t], OH[:, t], gatev[:, t, pair_of(p)].unsqueeze(2).to_broadcast([128, 2, SLOTS]), ALU.mult)
                last.then_inc(g_ready, 1)

            def pair_of(p):
                return slice(2 * p, 2 * p + 2) if isinstance(p, int) else bass.ds(p * 2, 2)

            def columns_in(key, p):
                ps, free = nth_full(key, p)
                dve.tensor_copy(xs[:, 0:4, :], ps[:, :].rearrange("p (c s) -> p c s", c=4)).then_inc(free, 1)

            def add_rows(key_p, p):
                for j in range(6):
                    ps, free = nth_full(lambda x, j=j: ("scatter", L, key_p(x), j), p)
                    t, h = j // 2, j % 2
                    r = ROWS[t]
                    y = Y[0:r, t, h * 512:(h + 1) * 512]
                    dve.tensor_tensor(y, y, ps[0:r, :], ALU.add).then_inc(free, 1)

            def pair(p, first=False, final=False):
                if not final:
                    nth_full(lambda x: ("gather", L, x, 0), p)
                    nth_full(lambda x: ("gather", L, x, 1), p)
                    dve.wait_ge(g_ready, p + (NPAIR * L + 1))
                    onehots(p + 1)
                ps, free = nth_full(lambda x: ("up", L, x), p)
                b, n = nth(lambda x: ("gate", L, x), p)
                dve.wait_ge(bank_free[b], n + 1)
                dve.tensor_tensor(hid, sil, ps[:, :], ALU.mult).then_inc(free, 1)
                if not final:
                    columns_in(lambda x: ("gather", L, x + 1, 0), p)
                if not first:
                    add_rows(lambda x: x - 1, p)
                if not final:
                    nth_full(lambda x: ("gturn", L, x), p)
                    dve.wait_ge(oh_ready, p + (NPAIR * L + 2))
                    gates(p + 1)
                b, n = nth(lambda x: ("gturn", L, x), p)
                dve.wait_ge(bank_free[b], n + 1)
                dve.tensor_scalar(single(OHT[:, :]), GT[:, :], 0.0, None, ALU.is_gt).then_inc(oht_ready, 1)
                for h in range(2):
                    ps, free = nth_full(lambda x, h=h: ("down", L, x, h), p)
                    dve.wait_ge(ys_high, p * 2 + (2 * NPAIR * L + h + 1))
                    half = slice(h * 512, (h + 1) * 512)
                    dve.scalar_tensor_tensor(out=single(yslow[:, half]), in0=ps[:, :], scalar=gs, in1=single(ys[:, half]),
                                             op0=ALU.mult, op1=ALU.subtract).then_inc(free, 1)

            onehots(0)
            dve.wait_ge(oh_ready, NPAIR * L + 1)
            gates(0)
            ps = wait_full(dve, "totals", L)
            dve.tensor_reduce(one[7][:, 0:1], ps[:, 0:NE], AX, ALU.max).then_inc(freed(("totals", L)), 1)
            wait_emptied(dve, "totals", L)
            dve.tensor_copy(most[0:1, L:L + 1], one[7][0:1, 0:1]).then_inc(most_ready, 1)
            columns_in(lambda x: ("gather", L, x, 0), 0)
            pair(0, first=True)
            dve.wait_ge(y_begun, 3 * (L + 1))
            with dve.Fori(1, NPAIR - 1) as p:
                pair(p)
            pair(NPAIR - 1, final=True)
            add_rows(lambda x: x - 1, NPAIR)
            for j in range(3, 6):
                wait_emptied(dve, "scatter", L, NPAIR - 1, j)

            S = over[L]

            def over_body(n, b, e):
                dve.wait_ge(S["pe"], n * OV["pe"] + 1)
                for t in range(3):
                    last = dve.tensor_tensor(OH[:, t, 0, :], iota[:, bass.ds(b * SLOTS, SLOTS)],
                                             place[:, t, bass.ds(e, 1)].to_broadcast([128, SLOTS]), ALU.is_equal)
                last.then_inc(S["dve"], 1)
                dve.wait_ge(S["dve"], n * OV["dve"] + 1)
                for t in range(3):
                    last = dve.tensor_tensor(G[:, t, 0, :], OH[:, t, 0, :], gatev[:, t, bass.ds(e, 1)].to_broadcast([128, SLOTS]), ALU.mult)
                last.then_inc(S["dve"], 1)
                dve.wait_ge(S["pe"], n * OV["pe"] + 4)
                dve.wait_ge(S["act"], n * OV["act"] + 2)
                dve.tensor_tensor(hid[0:64, :], sil[0:64, :], bank[3][0:64, :], ALU.mult).then_inc(S["dve"], 1)
                for j in range(6):
                    dve.wait_ge(S["pe"], n * OV["pe"] + 9 + j)
                    t, h = j // 2, j % 2
                    y = Y[0:ROWS[t], t, h * 512:(h + 1) * 512]
                    dve.tensor_tensor(y, y, bank[OVER_BANK[j]][0:ROWS[t], :], ALU.add).then_inc(S["dve"], 1)

            with dve.If(overflow_any(dve, L)):
                overflow_loop(dve, over_body)
                dve.wait_ge(S["dve"], (TOK // SLOTS - 1) * NE * OV["dve"])


        @block.vector
        def _(dve):
            step = Chain(dve, dve_step)

            def rope(x, y, a, table, nh, d, r, used, ready):
                cos = table[0:r, 0, :].unsqueeze(1).to_broadcast([r, 2 * nh, d // 2])
                sin = table[0:r, 1, :].unsqueeze(1).to_broadcast([r, nh, d // 2])
                ax, xx = (z[0:r].rearrange("p (g d) -> p g d", g=2 * nh) for z in (a, x))
                dve.tensor_tensor(ax, xx, cos, ALU.mult)
                x, y, a = (z[0:r].rearrange("p (h u d) -> p h u d", h=nh, u=2) for z in (x, y, a))
                dve.tensor_tensor(y[:, :, 0, :], x[:, :, 1, :], sin, ALU.mult)
                dve.tensor_tensor(y[:, :, 1, :], x[:, :, 0, :], sin, ALU.mult).then_inc(used[0], 1)
                dve.wait_ge(used[0], used[1])
                dve.tensor_tensor(y[:, :, 0, :], a[:, :, 0, :], y[:, :, 0, :], ALU.subtract)
                last = dve.tensor_tensor(y[:, :, 1, :], a[:, :, 1, :], y[:, :, 1, :], ALU.add)
                if ready is None:
                    step(last)
                else:
                    last.then_inc(ready, 1)

            table_a = AC["rope"].rearrange("p (t u d) -> p t u d", t=3, u=2)
            causal = AC["causal"].rearrange("p (t k) -> p t k", t=2)

            def fold(count, key, out, width=512):
                dve.wait_ge(half_ready, count)
                ps, out = bank[USE[key][0]], out[0:64, 0:width]
                dve.tensor_tensor(out, out, ps[64:128, 0:width], ALU.add).then_inc(freed(key), 1)

            def rope_unit(n):
                for t in range(3):
                    k, r = 3 * n + t, ROWS[t]
                    if t == 2:
                        fold(n + 1, ("in", n, t), E[:, k % 2, :], W_KW if n == 1 else 512)
                    wait_emptied(dve, "in", n, t)
                    if k == 0:
                        dve.wait_ge(attn_c_in, 16)
                    if n:
                        wait_full(dve, "inturn", n - 1, t)
                        if n in (2, 5):
                            dve.wait_ge(tile_stored[t], 16 * (1 if n == 2 else 2))
                    if k:
                        dve.wait_ge(r_ready, k)
                    if n == 1:
                        step(dve.tensor_scalar(wi[0:r, t, :], E[0:r, k % 2, ID:W_KW], IH ** -0.5, None, ALU.mult))
                        rope(E[:, k % 2, 0:ID], R[:, t, 0:ID], ropeA[:, 0:ID], table_a[:, t], 1, ID, r, (e_used, k + 1), None)
                        dve.tensor_copy(R[0:r, t, ID:2 * ID], R[0:r, t, 0:ID]).then_inc(r_ready, 1)
                    else:
                        rope(E[:, k % 2, :], R[:, t, :], ropeA, table_a[:, t], 8, HD, r, (e_used, k + 1), r_ready)

            def choose(w, r, topk, mask, out):
                left = topk
                while left > 0:
                    step(dve.max(best[0:r, :], w))
                    if left < 8:
                        step(dve.memset(best[0:r, left:8], TAKEN))
                    step(dve.match_replace(w, best[0:r, :], w, TAKEN))
                    left -= 8
                    yield
                step(dve.tensor_scalar(w, w, TAKEN, BIG, ALU.is_equal, ALU.mult))
                step(dve.scalar_tensor_tensor(out=out, in0=w, scalar=-BIG, in1=mask, op0=ALU.add, op1=ALU.min))

            def low_x(name, count):
                for t in range(3):
                    for h in range(2):
                        dve.wait_ge(x_high, count + 2 * t + h + 1)
                        ps, r = bank[USE[name, t, h][0]], ROWS[t]
                        c4, cols = slice(4 * h, 4 * h + 4), slice(t * 128, t * 128 + r)
                        high = (XT if t < 2 else XLOW)[:, c4, cols]
                        low = XLOW[:, c4, cols if t < 2 else slice(320, 384)]
                        dve.tensor_tensor(single(low), ps[:, :].rearrange("p (c t) -> p c t", c=4)[:, :, 0:r], single(high),
                                          ALU.subtract).then_inc(freed((name, t, h)), 1)

            low_x("x0", 0)
            for i, k in enumerate((slice(0, 4), slice(4, 8))):
                dve.wait_ge(high_ready, i + 1)
                w = weights(PARTED[0])[:, k]
                dve.tensor_tensor(single(w), w, rounded(PARTED[0])[:, k], ALU.subtract).then_inc(first_low_ready, 1)
            rope_unit(0)
            rope_unit(1)
            rope_unit(2)
            ps = wait_full(dve, "wspread")
            dve.tensor_tensor(WP[0:64], AC["wsel"][0:64].rearrange("p (s t) -> p s t", s=NSEQ),
                              ps[0:64, 0:64].unsqueeze(1).to_broadcast([64, NSEQ, 64]), ALU.mult).then_inc(freed(("wspread",)), 1)
            rope_unit(3)
            m = 0
            for qt in range(2):
                nk = 128 * (qt + 1)
                for cc in range(2):
                    for par in range(2):
                        wait_emptied(dve, "index", qt, cc, par)
                        for j in range(2):
                            head = 2 * (2 * cc + j) + par
                            src, acc = relu[:, m % 2, j * nk:(j + 1) * nk], bias_p[:, qt, 0:nk]
                            if cc == par == j == 0:
                                ins = dve.tensor_scalar(acc, src, wi[:, qt, head:head + 1], None, ALU.mult)
                            else:
                                ins = dve.scalar_tensor_tensor(out=acc, in0=src, scalar=wi[:, qt, head:head + 1], in1=acc,
                                                               op0=ALU.mult, op1=ALU.add)
                            if j == 0:
                                step(ins)
                            else:
                                ins.then_inc(relu_used, 1)
                                dve.wait_ge(relu_used, m + 1)
                        m += 1
            rope_unit(4)
            wait_emptied(dve, "inturn", 0, 2)
            dve.wait_ge(zeroed, 4)

            def query_blocks(s):
                if s >= 2:
                    wait_full(dve, "sindex", s - 2)
                q0 = PROMPT + s * DSEQ
                blocks = qib[:, s % 2].rearrange("p c r -> p (c r)")
                for par in range(2):
                    o = 64 * par
                    dst = bass_step(blocks[o:o + 64, :], 8 * par, 4, 64 + 16, DSEQ)
                    last = dve.tensor_copy(dst, qiT[o:o + 64, :, q0:q0 + DSEQ])
                last.then_inc(qib_ready, 1)

            query_blocks(0)
            query_blocks(1)
            rope_unit(5)
            for qt in range(2):
                nk = 128 * (qt + 1)
                query_blocks(2 + 2 * qt)
                query_blocks(3 + 2 * qt)
                w, mask = work[:, 0:nk], causal[:, qt, 0:nk]
                step(dve.tensor_tensor(w, bias_p[:, qt, 0:nk], mask, ALU.min))
                for _ in choose(w, 128, TOPK_P, mask, bias_p[:, qt, 0:nk]):
                    pass
            query_blocks(6)
            query_blocks(7)
            for n in (6, 7):
                fold(n + 1, ("in", n, 2), V[:, 2, (n - 6) * 512:(n - 5) * 512])
            ps = wait_full(dve, "sscore")
            masked = bias_s[0:64, :]
            dve.tensor_tensor(masked, ps[0:64, 0:KEYS], AC["scausal"][0:64, :], ALU.min).then_inc(freed(("sscore",)), 1)
            wait_emptied(dve, "sscore")
            sample_choice = choose(masked, 64, TOPK_S, AC["scausal"][0:64, :], masked)

            def scale(n):
                nk = 128 * (n // 8 + 1)
                c = 16 + 8 * (n % 3)
                dve.wait_ge(exp_ready, n + 1)
                step(dve.reciprocal(small[:, c + 6:c + 8], small[:, c + 4:c + 6]))
                view = P[:, n % 3, 0:2 * nk].rearrange("p (j k) -> p j k", j=2)
                dve.tensor_tensor(view, view, small[:, c + 6:c + 8].unsqueeze(2).to_broadcast([128, 2, nk]), ALU.mult).then_inc(p_ready, 1)

            for n in range(16):
                qt, cc, par = n // 8, n // 2 % 4, n % 2
                nk = 128 * (qt + 1)
                c = 16 + 8 * (n % 3)
                ps = wait_full(dve, "attn", qt, cc, par)
                if n >= 3:
                    wait_full(dve, "pturn", n - 3)
                view = P[:, n % 3, 0:2 * nk].rearrange("p (j k) -> p j k", j=2)
                dve.tensor_tensor(view, ps[:, 0:2 * nk].rearrange("p (j k) -> p j k", j=2),
                                  bias_p[:, qt, 0:nk].unsqueeze(1).to_broadcast([128, 2, nk]), ALU.add).then_inc(freed(("attn", qt, cc, par)), 1)
                wait_emptied(dve, "attn", qt, cc, par)
                step(dve.tensor_reduce(small[:, c:c + 2], view, AX, ALU.max))
                dve.tensor_scalar(small[:, c + 2:c + 4], small[:, c:c + 2], -HD ** -0.5, None, ALU.mult).then_inc(max_ready, 1)
                if n:
                    scale(n - 1)
                next(sample_choice, None)
            scale(15)

            for i in (4, 5):
                wait_emptied(dve, "inturn", i, 2)
            for t in range(3):
                dve.wait_ge(tile_stored[t], 3 * 16)
            dve.tensor_copy(KT[:, :, PAST:KEYS], kT[:, :, PROMPT:TOK]).then_inc(new_kt, 1)
            for i in (2, 3):
                wait_emptied(dve, "inturn", i, 2)

            qbf = QB.rearrange("p c r -> p (c r)")
            for s in range(NSEQ + 2):
                if s < NSEQ:
                    if s:
                        wait_full(dve, "sattn", s - 1)
                    q0 = PROMPT + s * DSEQ
                    dve.tensor_scalar(rept[0:64, s % 2, :], AC["rep"][0:64, :], AC["ofseq"][0:64, s:s + 1], None, ALU.mult)
                    for par in range(2):
                        o = 64 * par
                        last = dve.tensor_copy(bass_step(qbf[o:o + 64, :], 8 * par, KC, 128 + 16, DSEQ), qT[o:o + 64, :, q0:q0 + DSEQ])
                    last.then_inc(qb_ready, 1)
                    for j in range(2, 4):
                        ps = wait_full(dve, "kturn", s, j)
                        dve.tensor_copy(KT[:, 2 * j:2 * j + 2, 0:PAST], ps[:, :].rearrange("p (c k) -> p c k", c=2)).then_inc(freed(("kturn", s, j)), 1)
                if s >= 2:
                    b = s - 2
                    ps = wait_full(dve, "oturn_s", b)
                    view = ps[0:64, 0:128].rearrange("p (c u q) -> p c u q", c=KC, u=2)
                    q0 = PROMPT + b * DSEQ
                    for par in range(2):
                        last = dve.tensor_copy(oT[64 * par:64 * par + 64, :, q0:q0 + DSEQ], view[:, :, par, :])
                    last.then_inc(freed(("oturn_s", b)), 1)
                if s < NSEQ:
                    ps = wait_full(dve, "sattn", s)
                    c = 4 * (s % 2)
                    step(dve.tensor_reduce(small[:, c:c + 1], ps[:, 0:KEYS], AX, ALU.max))
                    dve.tensor_scalar(small[:, c + 1:c + 2], small[:, c:c + 1], -HD ** -0.5, None, ALU.mult).then_inc(max_s, 1)
                    wait_emptied(dve, "sattn", s)
                    step(dve.reciprocal(small[:, c + 3:c + 4], small[:, c + 2:c + 3]))
                    dve.tensor_scalar(P[:, s % 2, 0:KEYS], P[:, s % 2, 0:KEYS], small[:, c + 3:c + 4], None, ALU.mult).then_inc(p_s, 1)
                if 0 < s <= NSEQ:
                    b = s - 1
                    ps = wait_full(dve, "pv_s", b)
                    dve.tensor_tensor(osel.rearrange("p (h d) -> p h d", h=4), ps[:, 0:256].rearrange("p (h d) -> p h d", h=4),
                                      AC["hsel"].unsqueeze(2).to_broadcast([128, 4, HD]), ALU.mult).then_inc(freed(("pv_s", b)), 1)
                    wait_emptied(dve, "pv_s", b)
                    dve.tensor_reduce(O2, osel.rearrange("p (h d) -> p d h", h=4), AX, ALU.add).then_inc(o2_s, 1)

            def norm(L, k):
                j = 2 * L + k
                S = Y if k else X

                def summed(t, u):
                    r = ROWS[t]
                    ps = wait_full(dve, "proj", L, t, u)
                    parts = [(u * 512, 512, 0)] if t < 2 or L else [(u * 512, 256, 0), (u * 512 + 256, 256, 64)]
                    for x0, w, o in parts:
                        last = dve.scalar_tensor_tensor(out=X[0:r, t, x0:x0 + w], in0=X[0:r, t, x0:x0 + w], scalar=ALPHA,
                                                        in1=ps[o:o + r, 0:w], op0=ALU.mult, op1=ALU.add)
                    if t == 2 and L:
                        step(last)
                        x = X[0:64, t, u * 512:(u + 1) * 512]
                        last = dve.tensor_tensor(x, x, ps[64:128, 0:512], ALU.add)
                    last.then_inc(freed(("proj", L, t, u)), 1)
                    wait_emptied(dve, "proj", L, t, u)
                    step(dve.bn_stats(bnst[0:r, t, 6 * u:6 * u + 6], X[0:r, t, u * 512:(u + 1) * 512]))

                def moments(t):
                    r = ROWS[t]
                    if k:
                        dve.bn_stats(bnst[0:r, t, 0:6], S[0:r, t, 0:512])
                        step(dve.bn_stats(bnst[0:r, t, 6:12], S[0:r, t, 512:1024]))
                    else:
                        summed(t, 1)
                    dve.bn_aggr(mv[0:r, t, :], bnst[0:r, t, :].rearrange("p (u s) -> p u s", u=2)).then_inc(var_ready, 1)

                def apply(t):
                    r = ROWS[t]
                    if t == 0:
                        dve.wait_ge(ln_in[j], 32)
                    dve.wait_ge(var_ready, 3 * j + t + 1)
                    step(dve.scalar_tensor_tensor(out=X[0:r, t, :], in0=S[0:r, t, :], scalar=mv[0:r, t, 0:1], in1=lng[0:r, :],
                                                  op0=ALU.subtract, op1=ALU.mult))
                    dve.wait_ge(std_ready, 3 * j + t + 1)
                    step(dve.reciprocal(sv[0:r, t, 1:2], sv[0:r, t, 0:1]))
                    dve.scalar_tensor_tensor(out=X[0:r, t, :], in0=X[0:r, t, :], scalar=sv[0:r, t, 1:2], in1=lnb[0:r, :],
                                             op0=ALU.mult, op1=ALU.add).then_inc(x_ready, 1)

                if not k:
                    for t in range(3):
                        summed(t, 0)
                moments(0)
                moments(1)
                apply(0)
                moments(2)
                apply(1)
                apply(2)

            norm(0, 0)
            experts_dve(dve, 0, step)
            norm(0, 1)

            low_x("x2", 6)

            table_r = RC["rrope"].rearrange("p (t u d) -> p t u d", t=3, u=2)
            for n in range(4):
                for t in range(3):
                    k, r = 3 * n + t, ROWS[t]
                    if t == 2:
                        fold(NIN + n + 1, ("rin", n, t), RE[:, k % 2, :])
                    wait_emptied(dve, "rin", n, t)
                    if k == 0:
                        dve.wait_ge(ret_c_in, 16)
                    if k >= 1:
                        dve.wait_ge(rk_ready, k)
                    if n < 2:
                        if k >= 2:
                            wait_full(dve, "rturn", (k - 2) // 3, (k - 2) % 3)
                        out = RR[:, k % 2, :]
                    else:
                        out = kt[:, t, 2 * (n - 2):2 * (n - 2) + 2].rearrange("p h d -> p (h d)")
                    rope(RE[:, k % 2, :], out, rropeA, table_r[:, t], 2, RQ, r, (re_used, k + 1), rk_ready)
            fold(NIN + 5, ("rin", 4, 2), v[:, 2, 0, :])
            for t in range(2):
                for n in (2, 3):
                    wait_full(dve, "rturn", n, t)
            kp = kt[:, 0:2].rearrange("p t h d -> p (t h) d")
            dve.tensor_tensor(kp, kp, RC["kdecay"].unsqueeze(2).to_broadcast([128, 2 * RH, RQ]), ALU.mult).then_inc(kd_ready, 1)
            for n in range(2):
                wait_full(dve, "rturn", n, 2)
                wait_emptied(dve, "rturn", n, 2)
            dve.wait_ge(rk_ready, 12)
            step(dve.memset(QM, 0.0))
            decay = RC["qdecay"].rearrange("p (x q) -> p x q", x=2 * RH)
            for s in range(NSEQ):
                last = dve.tensor_tensor(QM[:, :, s, 8 * (s % 4):8 * (s % 4) + 8], rqT[:, :, PROMPT + 8 * s:PROMPT + 8 * s + 8],
                                         decay, ALU.mult)
            last.then_inc(qm_ready, 1)
            for n in (5, 6, 7):
                fold(NIN + n + 1, ("rin", n, 2), v[:, 2, n - 4, :])
            ps = wait_full(dve, "sinner")
            dve.tensor_tensor(innS[0:64].rearrange("p h i -> p (h i)"), ps[0:64, 0:256], RC["sdecay"][0:64, :], ALU.mult)\
               .then_inc(freed(("sinner",)), 1)
            ksel = RC["ksel"].rearrange("p (s h) -> p s h", s=NSEQ)
            for s in range(NSEQ):
                if s:
                    wait_full(dve, "update", s - 1, 7)
                dve.tensor_tensor(kd[0:64], kt[0:64, 2], ksel[0:64, s, :].unsqueeze(2).to_broadcast([64, RH, RQ]), ALU.mult)\
                   .then_inc(kd_ready, 1)
                st = weights(("state", s))
                for j in range(8):
                    ps = wait_full(dve, "update", s, j)
                    dve.scalar_tensor_tensor(out=st[:, j, :], in0=st[:, j, :], scalar=GAMMA8[j // 2], in1=ps[:, :],
                                             op0=ALU.mult, op1=ALU.add).then_inc(freed(("update", s, j)), 1)
            for g in range(2):
                ps = wait_full(dve, "so", g)
                if g:
                    wait_emptied(dve, "so", 0)
                step(dve.bn_stats(rst[:, 2, 0:6], ps[:, :]))
                dve.bn_aggr(rst[:, 2, 12:14], rst[:, 2, 0:6]).then_inc(rvar, 1)
                dve.wait_ge(rstd, g + 1)
                step(dve.reciprocal(rst[:, 2, 15:16], rst[:, 2, 14:15]))
                dve.scalar_tensor_tensor(out=rst[:, 2, 16:17], in0=rst[:, 2, 12:13], scalar=-1.0, in1=rst[:, 2, 15:16],
                                         op0=ALU.mult, op1=ALU.mult).then_inc(rnmr, 1)
            wait_emptied(dve, "so", 1)

            for h in range(RH):
                ps = wait_full(dve, "inner", h)
                dve.tensor_tensor(inn[:, 0:256], ps[:, 0:256], RC["decay"][:, h * 256:(h + 1) * 256], ALU.mult)
                dve.tensor_tensor(inn[:, 256:384], ps[:, 256:384], RC["decay"][:, h * 256:h * 256 + 128], ALU.mult)\
                   .then_inc(freed(("inner", h)), 1)
                for t in range(2):
                    ps = wait_full(dve, "ro", h, t)
                    step(dve.bn_stats(rst[:, t, 0:6], ps[:, :]))
                    last = dve.bn_aggr(rst[:, t, 12:14], rst[:, t, 0:6])
                    if t == 0:
                        step(last)
                last.then_inc(rvar, 1)
                dve.wait_ge(rstd, 2 + h + 1)
                step(dve.reciprocal(rst[:, 0:2, 15:16], rst[:, 0:2, 14:15]))
                dve.scalar_tensor_tensor(out=rst[:, 0:2, 16:17], in0=rst[:, 0:2, 12:13], scalar=-1.0, in1=rst[:, 0:2, 15:16],
                                         op0=ALU.mult, op1=ALU.mult).then_inc(rnmr, 1)
                for t in range(2):
                    wait_emptied(dve, "ro", h, t)
            def gained(n, t):
                ps = wait_full(dve, "oturn", n, t)
                r = ROWS[t]
                cols = gated_places(n, t)[0]
                if n == 2 and t == 0:
                    for c in range(2):
                        dve.wait_ge(sto_stored[c], 16 * RH)
                dve.tensor_tensor(rlow[n][:, :, cols], ps[:, :].rearrange("p (c t) -> p c t", c=4)[:, :, 0:r],
                                  gain[:, 4 * n:4 * n + 4].unsqueeze(2).to_broadcast([128, 4, r]), ALU.mult).then_inc(freed(("oturn", n, t)), 1)

            def gated_low(n, t):
                dve.wait_ge(ro_high, 3 * n + t + 1)
                cols, high = gated_places(n, t)
                dve.tensor_tensor(single(rlow[n][:, :, cols]), rlow[n][:, :, cols], single(high),
                                  ALU.subtract).then_inc(ro_ready, 1)

            dve.wait_ge(gain_in, 16)
            for n in range(4):
                for t in range(3):
                    k, r = 3 * n + t, ROWS[t]
                    if t == 2:
                        fold(NIN + 8 + n + 1, ("rin", 8 + n, t), RE[:, k % 2, :])
                        dve.wait_ge(silu_ready, n + 1)
                    wait_emptied(dve, "rin", 8 + n, t)
                    dve.tensor_tensor(v[0:r, t, n, :], v[0:r, t, n, :], RE[0:r, k % 2, :], ALU.mult).then_inc(go_ready, 1)
                    if n:
                        gained(n - 1, t)
                        if k > 3:
                            gated_low((k - 4) // 3, (k - 4) % 3)
            for t in range(3):
                gained(3, t)
                gated_low((8 + t) // 3, (8 + t) % 3)
            gated_low(3, 2)
            norm(1, 0)
            experts_dve(dve, 1, step)
            norm(1, 1)

INS = {"x_p": lambda a: a["x_prompt"].reshape(PROMPT, D), "x_s": lambda a: a["x_sample"].reshape(SAMPLE, D),
       **{n: (lambda a, n=n: a[n]) for n in ("cache_k", "cache_v", "cache_idx_k", "state_ret", "page_table", "w_in_attn",
                                             "w_out_attn", "w_in_ret", "ret_norm_gain", "w_out_ret", "w_router", "b_router",
                                             "w_exp_gate", "w_exp_up", "w_exp_down", "ln_gain", "ln_bias")}}
OUTS = {"y_p": ((PROMPT, D), (1, PROMPT, D)), "y_s": ((SAMPLE, D), (NSEQ, DSEQ, D)),
        "k_p": ((PROMPT, D), (1, 1, PROMPT, HEADS, HD)), "v_p": ((PROMPT, D), (1, 1, PROMPT, HEADS, HD)),
        "ik_p": ((PROMPT, ID), (1, 1, PROMPT, ID)),
        "k_s": ((SAMPLE, D), (1, NSEQ, DSEQ, HEADS, HD)), "v_s": ((SAMPLE, D), (1, NSEQ, DSEQ, HEADS, HD)),
        "ik_s": ((SAMPLE, ID), (1, NSEQ, DSEQ, ID)),
        "state_p": ((RH, RQ, RV), (1, 1, RH, RQ, RV)), "state_s": ((NSEQ, RH, RQ, RV), (1, NSEQ, RH, RQ, RV))}


def kernel(**inputs):
    import concourse.bacc as bacc
    from concourse.bass_utils import run_bass_kernel_spmd

    nc = bacc.Bacc("TRN2", target_bir_lowering=False, num_devices=1)
    common, attn, ret = constants()
    arrays = {n: np.ascontiguousarray(f(inputs)) for n, f in INS.items()}
    arrays |= {"c_common": common, "c_attn": attn, "c_ret": ret}
    ins = {n: nc.dram_tensor(f"in_{n}", a.shape, mybir.dt.from_np(a.dtype), kind="ExternalInput").ap() for n, a in arrays.items()}
    outs = {n: nc.dram_tensor(f"out_{n}", shape, F32, kind="ExternalOutput").ap() for n, (shape, _) in OUTS.items()}
    build(nc, ins, outs)
    r = run_bass_kernel_spmd(nc, [{f"in_{n}": a for n, a in arrays.items()}], core_ids=[0])
    return tuple(np.asarray(r.results[0][f"out_{n}"]).reshape(shape) for n, (_, shape) in OUTS.items())
```
